# Optimizing a Trainium2 kernel written in Bass

```python
import jax, jax.numpy as jnp
from jax import lax
import numpy as np

D_MODEL = 1024
BATCH = 1
SEQ = 256
DEPTH = 1

HG_HEADS = 4
HG_KEY_DIM = 128
HG_VAL_DIM = 128
HG_CHUNK = 64
HG_QK_W = HG_HEADS * HG_KEY_DIM
HG_V_W = HG_HEADS * HG_VAL_DIM
ATT_Q_HEADS = 8
ATT_KV_HEADS = 2
ATT_HEAD_DIM = 64
ATT_GROUP = ATT_Q_HEADS // ATT_KV_HEADS
ATT_Q_W = ATT_Q_HEADS * ATT_HEAD_DIM
ATT_KV_W = ATT_KV_HEADS * ATT_HEAD_DIM
WINDOW = 128
ATT_BLOCK = 128
ROPE_THETA = 500000.0
ROPE_DIM = ATT_HEAD_DIM // 4
N_EXPERTS = 32
TOP_K = 4
D_EXPERT = D_MODEL
SWIGLU_ALPHA = 1.702
SWIGLU_LIMIT = 7.0
MOE_BLOCK = 128
EPS = 1e-6
IN_WIDTHS = (HG_QK_W, HG_QK_W, HG_V_W, HG_V_W, ATT_Q_W, ATT_KV_W, ATT_KV_W, D_MODEL, D_MODEL)
IN_WIDTH = HG_QK_W * 2 + HG_V_W * 2 + ATT_Q_W + ATT_KV_W * 2 + D_MODEL * 2


def _split_points():
    pts, acc = [], 0
    for w in IN_WIDTHS[:-1]:
        acc += w
        pts.append(acc)
    return pts

def rms_norm(x, gain):
    xf = x.astype(jnp.float32)
    y = xf * lax.rsqrt(jnp.mean(xf * xf, axis=-1, keepdims=True) + EPS)
    return (y * gain.astype(jnp.float32)).astype(x.dtype)

def partial_rotary(x, positions):
    half = ROPE_DIM // 2
    inv_freq = ROPE_THETA ** (-jnp.arange(half, dtype=jnp.float32) / half)
    ang = positions.astype(jnp.float32)[:, None, :, None] * inv_freq
    cos, sin = jnp.cos(ang), jnp.sin(ang)
    xr = x[..., :ROPE_DIM].astype(jnp.float32)
    x1, x2 = xr[..., :half], xr[..., half:]
    rot = jnp.concatenate([x1 * cos - x2 * sin, x2 * cos + x1 * sin], axis=-1).astype(x.dtype)
    return jnp.concatenate([rot, x[..., ROPE_DIM:]], axis=-1)

def hgrn2_branch(q_pre, f_pre, i_pre, g_pre, lower_bound, out_norm_gain):
    B, S, _ = q_pre.shape
    f32 = jnp.float32

    def heads(t, d):
        return t.reshape(B, S, HG_HEADS, d).transpose(0, 2, 1, 3)

    forget = lower_bound + (1.0 - lower_bound) * jax.nn.sigmoid(f_pre.astype(f32))
    q = heads(jax.nn.silu(q_pre.astype(f32)), HG_KEY_DIM)
    k = heads(1.0 - forget, HG_KEY_DIM)
    log_f = heads(jnp.log(forget), HG_KEY_DIM)
    v = heads(i_pre.astype(f32), HG_VAL_DIM)
    n_chunks = S // HG_CHUNK

    def chunks(t):
        return t.reshape(B, HG_HEADS, n_chunks, HG_CHUNK, t.shape[-1]).transpose(2, 0, 1, 3, 4)

    causal = jnp.tril(jnp.ones((HG_CHUNK, HG_CHUNK), dtype=bool))[:, :, None]

    def step(state, inp):
        qc, kc, vc, lfc = inp
        b = jnp.cumsum(lfc, axis=-2)
        o_inter = jnp.einsum('bhck,bhkv->bhcv', qc * jnp.exp(b), state)
        rel = b[:, :, :, None, :] - b[:, :, None, :, :]
        decay = jnp.exp(jnp.where(causal, rel, -jnp.inf))
        scores = jnp.einsum('bhik,bhjk,bhijk->bhij', qc, kc, decay)
        o = o_inter + jnp.einsum('bhij,bhjv->bhiv', scores, vc)
        b_last = b[:, :, -1:, :]
        new_state = jnp.exp(b_last[:, :, 0, :])[..., None] * state + jnp.einsum(
            'bhjk,bhjv->bhkv', kc * jnp.exp(b_last - b), vc)
        return new_state, o

    state0 = jnp.zeros((B, HG_HEADS, HG_KEY_DIM, HG_VAL_DIM), f32)
    _, o = lax.scan(step, state0, (chunks(q), chunks(k), chunks(v), chunks(log_f)))
    o = o.transpose(1, 2, 0, 3, 4).reshape(B, HG_HEADS, S, HG_VAL_DIM).transpose(0, 2, 1, 3)
    o = rms_norm(o, out_norm_gain).reshape(B, S, HG_V_W) * jax.nn.silu(g_pre.astype(f32))
    return o.astype(q_pre.dtype)

def swa_branch(q_pre, k_pre, v_pre, positions, q_gain, k_gain, sinks):
    B, S, _ = q_pre.shape
    nb = S // ATT_BLOCK
    f32 = jnp.float32
    q = q_pre.reshape(B, S, ATT_Q_HEADS, ATT_HEAD_DIM).transpose(0, 2, 1, 3)
    k = k_pre.reshape(B, S, ATT_KV_HEADS, ATT_HEAD_DIM).transpose(0, 2, 1, 3)
    v = v_pre.reshape(B, S, ATT_KV_HEADS, ATT_HEAD_DIM).transpose(0, 2, 1, 3)
    q = partial_rotary(rms_norm(q, q_gain), positions)
    k = partial_rotary(rms_norm(k, k_gain), positions)
    q = q.reshape(B, ATT_KV_HEADS, ATT_GROUP, nb, ATT_BLOCK, ATT_HEAD_DIM)

    def banded(t):
        tb = t.reshape(B, ATT_KV_HEADS, nb, ATT_BLOCK, ATT_HEAD_DIM)
        prev = jnp.pad(tb, ((0, 0), (0, 0), (1, 0), (0, 0), (0, 0)))[:, :, :-1]
        return jnp.concatenate([prev, tb], axis=3)

    kb, vb = banded(k), banded(v)
    scores = jnp.einsum('bhgnqd,bhnkd->bhgnqk', q, kb).astype(f32) * (ATT_HEAD_DIM ** -0.5)
    blk = jnp.arange(nb)[:, None] * ATT_BLOCK
    q_pos = blk + jnp.arange(ATT_BLOCK)[None, :]
    k_pos = blk - ATT_BLOCK + jnp.arange(2 * ATT_BLOCK)[None, :]
    dist = q_pos[:, :, None] - k_pos[:, None, :]
    mask = (dist >= 0) & (dist < WINDOW) & (k_pos[:, None, :] >= 0)
    scores = jnp.where(mask, scores, -jnp.inf)
    sink = sinks.astype(f32).reshape(1, ATT_KV_HEADS, ATT_GROUP, 1, 1, 1)
    logits = jnp.concatenate([scores, jnp.broadcast_to(sink, scores.shape[:-1] + (1,))], axis=-1)
    probs = jax.nn.softmax(logits, axis=-1)[..., :-1]
    out = jnp.einsum('bhgnqk,bhnkd->bhgnqd', probs.astype(vb.dtype), vb)
    out = out.reshape(B, ATT_Q_HEADS, S, ATT_HEAD_DIM).transpose(0, 2, 1, 3)
    return out.reshape(B, S, ATT_Q_W)

def moe_ffn(h, w_router, b_router, w_up, b_up, w_down, b_down):
    B, S, D = h.shape
    T = B * S
    A = T * TOP_K
    xf = h.reshape(T, D)
    logits = (xf @ w_router + b_router).astype(jnp.float32)
    top_vals, top_idx = lax.top_k(logits, TOP_K)
    gates = jax.nn.softmax(top_vals, axis=-1)
    flat_e = top_idx.reshape(A)
    flat_tok = (jnp.arange(A, dtype=jnp.int32) // TOP_K).astype(jnp.int32)
    flat_w = gates.reshape(A)
    order = jnp.argsort(flat_e)
    sorted_e = flat_e[order]
    counts = jnp.bincount(flat_e, length=N_EXPERTS)
    padded = (counts + MOE_BLOCK - 1) // MOE_BLOCK * MOE_BLOCK
    start = jnp.cumsum(counts) - counts
    pad_end = jnp.cumsum(padded)
    pad_start = pad_end - padded
    dest = pad_start[sorted_e] + jnp.arange(A) - start[sorted_e]
    P = A + N_EXPERTS * MOE_BLOCK
    n_blocks = P // MOE_BLOCK
    tok_buf = jnp.full((P,), T, jnp.int32).at[dest].set(flat_tok[order])
    w_buf = jnp.zeros((P,), jnp.float32).at[dest].set(flat_w[order])
    block_expert = jnp.minimum(
        jnp.searchsorted(pad_end, jnp.arange(n_blocks) * MOE_BLOCK, side='right'), N_EXPERTS - 1)
    x_pad = jnp.concatenate([xf, jnp.zeros((1, D), xf.dtype)], axis=0)
    x_buf = x_pad[tok_buf].reshape(n_blocks, MOE_BLOCK, D)

    def expert_block(args):
        xb, e = args
        hu = xb @ w_up[e] + b_up[e]
        x_glu = jnp.minimum(hu[:, ::2], SWIGLU_LIMIT)
        x_lin = jnp.clip(hu[:, 1::2], -SWIGLU_LIMIT, SWIGLU_LIMIT)
        act = x_glu * jax.nn.sigmoid(SWIGLU_ALPHA * x_glu) * (x_lin + 1.0)
        return act @ w_down[e] + b_down[e]

    y_buf = lax.map(expert_block, (x_buf, block_expert)).reshape(P, D)
    y = jax.ops.segment_sum(y_buf * w_buf[:, None].astype(y_buf.dtype), tok_buf, num_segments=T + 1)[:T]
    return y.reshape(B, S, D)

def first_inputs(seed: int = 0) -> dict:
    key = jax.random.key(seed)
    ks = jax.random.split(key, 24)
    D = D_MODEL
    f32 = jnp.float32

    def dense(k, shape, fan_in, scale=1.0):
        return jax.random.normal(k, shape, f32) * (scale * fan_in ** -0.5)

    def gain(k, shape):
        return 1.0 + 0.02 * jax.random.normal(k, shape, f32)

    x = jax.random.normal(ks[0], (BATCH, SEQ, D), f32)
    c = jax.random.normal(ks[1], (BATCH, D), f32)
    positions = (jax.random.randint(ks[2], (BATCH, 1), 0, 4096, dtype=jnp.int32)
                 + jnp.arange(SEQ, dtype=jnp.int32)[None, :]).astype(jnp.int32)
    return {
        'x': x,
        'c': c,
        'positions': positions,
        'w_ada': dense(ks[3], (DEPTH, D, 6 * D), D, 0.5),
        'b_ada': 0.02 * jax.random.normal(ks[4], (DEPTH, 6 * D), f32),
        'norm1_gain': gain(ks[5], (DEPTH, D)),
        'w_in': dense(ks[6], (DEPTH, D, IN_WIDTH), D),
        'lower_bound_logits': 0.1 * jax.random.normal(ks[7], (DEPTH + 1, HG_QK_W), f32),
        'hg_norm_gain': gain(ks[8], (DEPTH, HG_VAL_DIM)),
        'w_hg_branch': dense(ks[9], (DEPTH, HG_V_W, D), HG_V_W),
        'q_norm_gain': gain(ks[10], (DEPTH, ATT_HEAD_DIM)),
        'k_norm_gain': gain(ks[11], (DEPTH, ATT_HEAD_DIM)),
        'attn_sinks': jax.random.normal(ks[12], (DEPTH, ATT_Q_HEADS), f32),
        'w_attn_branch': dense(ks[13], (DEPTH, ATT_Q_W, D), ATT_Q_W),
        'w_out': dense(ks[14], (DEPTH, D, D), D),
        'norm2_gain': gain(ks[15], (DEPTH, D)),
        'w_router': dense(ks[16], (DEPTH, D, N_EXPERTS), D),
        'b_router': 0.01 * jax.random.normal(ks[17], (DEPTH, N_EXPERTS), f32),
        'w_up': dense(ks[18], (DEPTH, N_EXPERTS, D, 2 * D_EXPERT), D),
        'b_up': 0.01 * jax.random.normal(ks[19], (DEPTH, N_EXPERTS, 2 * D_EXPERT), f32),
        'w_down': dense(ks[20], (DEPTH, N_EXPERTS, D_EXPERT, D), D_EXPERT),
        'b_down': 0.01 * jax.random.normal(ks[21], (DEPTH, N_EXPERTS, D), f32),
    }

def first_block(x, c, positions, w_ada, b_ada, norm1_gain, w_in, lower_bound_logits, hg_norm_gain,
              w_hg_branch, q_norm_gain, k_norm_gain, attn_sinks, w_attn_branch, w_out, norm2_gain,
              w_router, b_router, w_up, b_up, w_down, b_down):
    lower_bounds = jnp.cumsum(jax.nn.softmax(lower_bound_logits.astype(jnp.float32), axis=0), axis=0)
    cond = jax.nn.silu(c)
    split_pts = _split_points()
    for l in range(DEPTH):
        mod = cond @ w_ada[l] + b_ada[l]
        sh1, sc1, g1, sh2, sc2, g2 = jnp.split(mod[:, None, :], 6, axis=-1)
        h = rms_norm(x, norm1_gain[l]) * (1.0 + sc1) + sh1
        proj = h @ w_in[l]
        hq, hf, hi, hg, aq, ak, av, gate_h, gate_a = jnp.split(proj, split_pts, axis=-1)
        y_h = hgrn2_branch(hq, hf, hi, hg, lower_bounds[l], hg_norm_gain[l]) @ w_hg_branch[l]
        y_a = swa_branch(aq, ak, av, positions, q_norm_gain[l], k_norm_gain[l], attn_sinks[l]) @ w_attn_branch[l]
        merged = jax.nn.sigmoid(gate_h) * y_h + jax.nn.sigmoid(gate_a) * y_a
        x = x + g1 * (merged @ w_out[l])
        h2 = rms_norm(x, norm2_gain[l]) * (1.0 + sc2) + sh2
        x = x + g2 * moe_ffn(h2, w_router[l], b_router[l], w_up[l], b_up[l], w_down[l], b_down[l])
    return x


SB_HEADS = 8
SB_HEAD_DIM = 64
SB_WIDTH = SB_HEADS * SB_HEAD_DIM
Q_BLOCK = 128
CONV_GROUPS = 8
CONV_GROUP_DIM = 64
CONV_WIDTH = CONV_GROUPS * CONV_GROUP_DIM
CONV_KSIZE = 3
N_BRANCHES = 2
N_GROUPS = 4
EXPERTS_PER_GROUP = 8
N_EXPERTS_2 = N_GROUPS * EXPERTS_PER_GROUP
TOP_K_IN_GROUP = 2
D_EXPERT_2 = 256
NORM_EPS = 1e-6
IN_SIZES = (SB_WIDTH, SB_WIDTH, SB_WIDTH, CONV_WIDTH, CONV_WIDTH, CONV_WIDTH, D_MODEL, D_MODEL)
IN_PROJ_WIDTH = sum(IN_SIZES)
IN_SPLITS = tuple(int(s) for s in np.cumsum(IN_SIZES)[:-1])


def rms_norm_2(x, g):
    xf = x.astype(jnp.float32)
    y = xf * lax.rsqrt(jnp.mean(xf * xf, axis=-1, keepdims=True) + NORM_EPS)
    return (y * g.astype(jnp.float32)).astype(x.dtype)

def stick_breaking_attention(q, k, v):
    B, H, S, dh = q.shape
    n_blocks = S // Q_BLOCK
    scale = SB_HEAD_DIM ** -0.5
    kf = k.astype(jnp.float32)
    vf = v.astype(jnp.float32)
    key_pos = jnp.arange(S)

    def one_block(i):
        start = i * Q_BLOCK
        qb = lax.dynamic_slice_in_dim(q, start, Q_BLOCK, axis=2).astype(jnp.float32)
        z = jnp.einsum('bhqd,bhkd->bhqk', qb, kf) * scale
        q_pos = start + jnp.arange(Q_BLOCK)
        mask = key_pos[None, :] < q_pos[:, None]
        neg_log_1m_beta = jnp.where(mask, jax.nn.softplus(z), 0.0)
        tail = lax.cumsum(neg_log_1m_beta, axis=3, reverse=True) - neg_log_1m_beta
        a = jnp.where(mask, jnp.exp(jax.nn.log_sigmoid(z) - tail), 0.0)
        return jnp.einsum('bhqk,bhkd->bhqd', a, vf)

    out = lax.map(one_block, jnp.arange(n_blocks))
    out = jnp.transpose(out, (1, 0, 3, 2, 4)).reshape(B, S, H * dh)
    return out.astype(q.dtype)

def short_conv_mixer(b_gate, c_gate, u, conv_w):
    S = u.shape[1]
    cu = c_gate * u
    cu_pad = jnp.pad(cu, ((0, 0), (CONV_KSIZE - 1, 0), (0, 0)))
    y = conv_w[0] * cu_pad[:, 0:S]
    for j in range(1, CONV_KSIZE):
        y = y + conv_w[j] * cu_pad[:, j:j + S]
    return b_gate * y

def hierarchical_moe(h, w_rg, b_rg, w_re, b_re, w_gate, w_up, w_down):
    N = h.shape[0]
    hf = h.astype(jnp.float32)
    g_logits = hf @ w_rg.astype(jnp.float32) + b_rg.astype(jnp.float32)
    g_prob = jax.nn.softmax(g_logits, axis=-1)
    _, g_idx = lax.top_k(g_logits, 1)
    g_w = jnp.take_along_axis(g_prob, g_idx, axis=-1)
    e_logits = (hf @ w_re.astype(jnp.float32) + b_re.astype(jnp.float32)).reshape(N, N_GROUPS, EXPERTS_PER_GROUP)
    e_in_group = jnp.take_along_axis(e_logits, g_idx[:, :, None], axis=1)[:, 0]
    top_v, top_i = lax.top_k(e_in_group, TOP_K_IN_GROUP)
    top_w = jax.nn.softmax(top_v, axis=-1)
    within = jnp.sum(jax.nn.one_hot(top_i, EXPERTS_PER_GROUP, dtype=jnp.float32) * top_w[..., None], axis=1)
    combine = (jax.nn.one_hot(g_idx[:, 0], N_GROUPS, dtype=jnp.float32)[:, :, None]
               * within[:, None, :] * g_w[:, :, None]).astype(h.dtype)
    y = jnp.zeros_like(h)
    for g in range(N_GROUPS):
        sl = slice(g * EXPERTS_PER_GROUP, (g + 1) * EXPERTS_PER_GROUP)
        act = jax.nn.silu(jnp.einsum('nd,edf->nef', h, w_gate[sl])) * jnp.einsum('nd,edf->nef', h, w_up[sl])
        act = act * combine[:, g, :, None]
        y = y + jnp.einsum('nef,efd->nd', act, w_down[sl])
    return y

def second_inputs(seed: int = 0) -> dict:
    key = jax.random.key(seed)
    ks = jax.random.split(key, 20)
    f32 = jnp.float32
    nrm = lambda k, shape, fan_in: jax.random.normal(k, shape, f32) * (fan_in ** -0.5)
    gain = lambda k, shape: 1.0 + 0.05 * jax.random.normal(k, shape, f32)
    return {
        "x": jax.random.normal(ks[0], (BATCH, SEQ, D_MODEL), f32),
        "norm_mix_g": gain(ks[1], (DEPTH, D_MODEL)),
        "w_in": nrm(ks[2], (DEPTH, D_MODEL, IN_PROJ_WIDTH), D_MODEL),
        "q_norm_g": gain(ks[3], (DEPTH, SB_HEAD_DIM)),
        "k_norm_g": gain(ks[4], (DEPTH, SB_HEAD_DIM)),
        "conv_w": nrm(ks[5], (DEPTH, CONV_KSIZE, CONV_WIDTH), CONV_KSIZE),
        "w_sb_branch": nrm(ks[6], (DEPTH, SB_WIDTH, D_MODEL), SB_WIDTH),
        "w_conv_branch": nrm(ks[7], (DEPTH, CONV_WIDTH, D_MODEL), CONV_WIDTH),
        "w_out": nrm(ks[8], (DEPTH, D_MODEL, D_MODEL), D_MODEL),
        "norm_ffn_g": gain(ks[9], (DEPTH, D_MODEL)),
        "w_router_group": nrm(ks[10], (DEPTH, D_MODEL, N_GROUPS), D_MODEL),
        "b_router_group": 0.01 * jax.random.normal(ks[11], (DEPTH, N_GROUPS), f32),
        "w_router_expert": nrm(ks[12], (DEPTH, D_MODEL, N_EXPERTS_2), D_MODEL),
        "b_router_expert": 0.01 * jax.random.normal(ks[13], (DEPTH, N_EXPERTS_2), f32),
        "w_gate_e": nrm(ks[14], (DEPTH, N_EXPERTS_2, D_MODEL, D_EXPERT_2), D_MODEL),
        "w_up_e": nrm(ks[15], (DEPTH, N_EXPERTS_2, D_MODEL, D_EXPERT_2), D_MODEL),
        "w_down_e": nrm(ks[16], (DEPTH, N_EXPERTS_2, D_EXPERT_2, D_MODEL), D_EXPERT_2),
    }

def second_block(x, norm_mix_g, w_in, q_norm_g, k_norm_g, conv_w, w_sb_branch, w_conv_branch,
              w_out, norm_ffn_g, w_router_group, b_router_group, w_router_expert,
              b_router_expert, w_gate_e, w_up_e, w_down_e):
    B, S, D = x.shape
    for l in range(DEPTH):
        h = rms_norm_2(x, norm_mix_g[l])
        proj = h @ w_in[l]
        q, k, v, c_b, c_c, c_u, g_a, g_b = jnp.split(proj, IN_SPLITS, axis=-1)
        q = rms_norm_2(q.reshape(B, S, SB_HEADS, SB_HEAD_DIM), q_norm_g[l]).transpose(0, 2, 1, 3)
        k = rms_norm_2(k.reshape(B, S, SB_HEADS, SB_HEAD_DIM), k_norm_g[l]).transpose(0, 2, 1, 3)
        v = v.reshape(B, S, SB_HEADS, SB_HEAD_DIM).transpose(0, 2, 1, 3)
        branch_a = stick_breaking_attention(q, k, v) @ w_sb_branch[l]
        branch_b = short_conv_mixer(c_b, c_c, c_u, conv_w[l]) @ w_conv_branch[l]
        merged = jax.nn.sigmoid(g_a) * branch_a + jax.nn.sigmoid(g_b) * branch_b
        x = x + merged @ w_out[l]
        h2 = rms_norm_2(x, norm_ffn_g[l]).reshape(B * S, D)
        y = hierarchical_moe(h2, w_router_group[l], b_router_group[l], w_router_expert[l],
                             b_router_expert[l], w_gate_e[l], w_up_e[l], w_down_e[l])
        x = x + y.reshape(B, S, D)
    return x


def setup_inputs(seed=0):
    out = dict(first_inputs(seed))
    for name, value in second_inputs(seed + 1).items():
        if name != "x":
            out[name + "_2"] = value
    return out


def reference(
    x, c, positions, w_ada, b_ada, norm1_gain, w_in, lower_bound_logits, hg_norm_gain,
    w_hg_branch, q_norm_gain, k_norm_gain, attn_sinks, w_attn_branch, w_out, norm2_gain,
    w_router, b_router, w_up, b_up, w_down, b_down, norm_mix_g_2, w_in_2, q_norm_g_2,
    k_norm_g_2, conv_w_2, w_sb_branch_2, w_conv_branch_2, w_out_2, norm_ffn_g_2,
    w_router_group_2, b_router_group_2, w_router_expert_2, b_router_expert_2, w_gate_e_2,
    w_up_e_2, w_down_e_2,
):
    x = first_block(
        x, c, positions, w_ada, b_ada, norm1_gain, w_in, lower_bound_logits, hg_norm_gain,
        w_hg_branch, q_norm_gain, k_norm_gain, attn_sinks, w_attn_branch, w_out, norm2_gain,
        w_router, b_router, w_up, b_up, w_down, b_down,
    )
    return second_block(
        x, norm_mix_g_2, w_in_2, q_norm_g_2, k_norm_g_2, conv_w_2, w_sb_branch_2,
        w_conv_branch_2, w_out_2, norm_ffn_g_2, w_router_group_2, b_router_group_2,
        w_router_expert_2, b_router_expert_2, w_gate_e_2, w_up_e_2, w_down_e_2,
    )


_drawn_inputs = setup_inputs


def setup_inputs(seed=0):
    import zlib

    import numpy as np

    out = dict(_drawn_inputs(seed))
    spreads = {}
    factors = {'norm1_gain': 3.552,
     'lower_bound_logits': 4.565,
     'hg_norm_gain': 3.014,
     'q_norm_gain': 8.0,
     'k_norm_gain': 8.0,
     'attn_sinks': 30.616,
     'b_router': 17.082,
     'b_up': 31.144,
     'b_down': 37.063,
     'q_norm_g_2': 4.111,
     'k_norm_g_2': 3.646,
     'b_router_group_2': 16.838,
     'b_router_expert_2': 17.361,
     'norm2_gain': 4.813,
     'norm_ffn_g_2': 2.684}
    for name, (base, spread) in spreads.items():
        noise = np.random.default_rng([zlib.crc32(name.encode()), seed]).standard_normal(out[name].shape)
        drawn = base * np.exp(spread * noise) if base else spread * noise
        out[name] = __import__('jax').numpy.asarray(drawn.astype(out[name].dtype))
    for name, factor in factors.items():
        out[name] = (out[name] * factor).astype(out[name].dtype)
    return out
```

```python
import numpy as np
import concourse.bass as bass
from concourse import mybir
from contextlib import ExitStack

F32 = mybir.dt.float32
I32 = mybir.dt.int32
U32 = mybir.dt.uint32
ALU = mybir.AluOpType
ACT = mybir.ActivationFunctionType
AX = mybir.AxisListType.X

P = 128
SEQ, D = 256, 1024
TT, KD = SEQ // P, D // P
EPS = 1e-6
NSLOT, SLOTW = 6, 4096
CH, SUB = 64, 16
EXP_CAP = 80.0
HH, AH, KVH, HD = 4, 8, 2, 64
NE, CAP = 32, 64
EXTRA = SEQ // CAP - 1
NEG = -1.0e30
C_IN, C_IN2 = 4864, 5120

CONST = {}
_cols = []


def _const(name, a):
    a = np.asarray(a, np.float32).reshape(P, -1)
    CONST[name] = (sum(c.shape[1] for c in _cols), a.shape[1])
    _cols.append(a)


_p = np.arange(P)[:, None]
_f = np.arange(P)[None, :]
_const("ident", _p == _f)
_const("before", _p < _f)
_const("from_here", _p >= _f)
_const("ones", np.ones((P, P)))
_const("win_bias", np.concatenate([np.where(_f > _p, 0.0, NEG), np.where(_f <= _p, 0.0, NEG)], 1))
_const("chunk_causal", (_p % CH) <= np.arange(CH)[None, :])
_const("iota", np.broadcast_to(np.arange(SEQ)[None, :], (P, SEQ)))
_const("inv_freq", np.broadcast_to((np.float32(500000.0) ** (-np.arange(8, dtype=np.float32) / 8))[None, :], (P, 8)))
CONSTS = np.concatenate(_cols, axis=1)
NCONST = CONSTS.shape[1]

SMALL = {}
_at = 0
for _n, _w in [("w_r1", KD * NE), ("w_r2", KD * 36), ("hg_gain", 128), ("q_gain", 64), ("k_gain", 64), ("sink", 8),
               ("b_r1", NE), ("b_r2", 36), ("q_gain2", 64), ("k_gain2", 64), ("cols", 28), ("cond", 8), ("lb", 4),
               ("one_lb", 4), ("lbd", 4), ("posf", 2), ("ss", 2), ("rs", 2), ("ang", 16), ("rn", 16), ("rr", 16), ("cos", 16),
               ("sin", 16), ("decay", 16), ("ssh", 8), ("rsh", 8), ("ssa", 32), ("rsa", 32), ("m", 16), ("nm", 16),
               ("es", 16), ("den", 16), ("cond32", KD * 32)]:
    SMALL[_n] = (_at, _w)
    _at += _w
NSMALL = _at

KB = 256
ARENA = 78.125
A1MAP = dict(h=(0, 8), acc=(8, 8), g1=(16, 4), a2=(20, 4), sh2=(24, 4), g2=(28, 4), gain=(32, 4),
             q=(0, 4), k=(4, 4), b=(8, 4), v=(12, 4), state=(16, 6), tmp=(20, 4), qt=(24, 4), oT=(24, 4), gs=(28, 4),
             kt=(32, 10), kdT=(32, 4), o=(36, 4), gates=(42, 16), qk=(58, 6), qkT=(64, 6), vv=(70, 1), st=(71, 2),
             rt=(73, 4), attT=(58, 4), s=(0, 12), pT0=(32, 8), pT1=(20, 4), reset=(73, 4),
             )
MMAP = dict(h=(0, 8), acc=(8, 8), gain=(32, 4), xg=(42, 4), glu=(46, 2), lin=(48, 2), sg=(50, 2), act=(52, 2), aT=(54, 2),
            ye=(56, 4), swT=(60, 1), selS=(61, 1), selW=(62, 1), brow=(63, 8), bdown=(71, 4), rt=(75, 3))
A2MAP = dict(h=(0, 8), qkT=(0, 8), v=(8, 4), attT=(12, 4), qk=(16, 8), z=(16, 12), sp=(28, 12), gates=(42, 16),
             tmp=(58, 4), cu=(62, 4.125), cb=(66.125, 4), cv=(70.125, 4), gain=(74.125, 4))

PRE = ([("ada", 0, i) for i in range(4)] + [("in", 0), ("in", 1), ("ada", 1, 0), ("in", 2), ("ada", 1, 1), ("in", 3),
       ("ada", 1, 2), ("in", 4), ("ada", 1, 3), ("in", 5), ("ada", 2, 0), ("in", 6), ("ada", 2, 1), ("in", 7),
       ("ada", 2, 2), ("in", 8), ("ada", 2, 3), ("in", 9), ("hg",), ("at",), ("out", 0), ("out", 1)])
MOE1 = len(PRE)
MID0 = MOE1 + 6 * NE
MID = [("in", i) for i in range(10)] + [("sb",), ("cv",), ("out", 0), ("out", 1)]
MOE2 = MID0 + len(MID)
IN_COLS = [(0, 512), (512, 512), (1024, 512), (1536, 512), (2048, 512), (2560, 256), (2816, 512), (3328, 512),
           (3840, 512), (4352, 512)]


def program(nc, t, out):
    ctx = ExitStack()
    with ctx:
        def sb(name, shape, dt=F32):
            return ctx.enter_context(nc.sbuf_tensor(name, shape, dt))

        sems = {}

        def S(name):
            if name not in sems:
                sems[name] = ctx.enter_context(nc.semaphore(name))
            return sems[name]

        ring = sb("ring", [P, NSLOT, SLOTW])
        x = sb("x", [P, TT, D])
        hT = sb("hT", [P, KD, SEQ])
        modrow = sb("modrow", [P, 3, 512])
        consts = sb("consts", [P, NCONST])
        small = sb("small", [P, NSMALL])
        rows = sb("rows", [34, P])
        pos = sb("pos", [34, P], I32)
        idx = sb("idx", [P, TT, 8], U32)
        idx2 = sb("idx2", [P, TT, 8], U32)
        flag = sb("flag", [P, 2], I32)
        arena = sb("arena", [P, int(ARENA * KB)])
        PS = ctx.enter_context(nc.psum_tensor("PS", [P, 8, 512], F32))

        def C(name):
            a, n = CONST[name]
            return consts[:, a:a + n]

        def sm(name, n=None):
            a, w = SMALL[name]
            return small[:, a:a + (n or w)]

        def at(m, name, lo=0, n=None):
            a, w = m[name]
            a = int(a * KB) + lo
            return arena[:, a:a + (n if n else int(w * KB) - lo)]

        ident = C("ident")
        slots = [ring[:, i, :] for i in range(NSLOT)]

        h = at(A1MAP, "h").rearrange("p (t d) -> p t d", t=TT)
        acc = at(A1MAP, "acc")
        acc4 = acc.rearrange("p (t c n) -> p (t c) n", t=TT, c=2)
        gain = at(A1MAP, "gain")
        xres = x[:, :, :]
        A1 = at(A1MAP, "a2")
        SH1 = at(A1MAP, "sh2")
        G1 = at(A1MAP, "g1")
        A2 = at(A1MAP, "a2")
        SH2 = at(A1MAP, "sh2")
        G2 = at(A1MAP, "g2")

        def unit_load(eng, u, desc):
            s = u % NSLOT
            kind = desc[0]
            blk2 = u >= MID0
            if kind == "ada":
                _, b, kp = desc
                dst = slots[s].rearrange("p (k n) -> p k n", k=2)
                src = t["w_ada"][0, kp * 256:(kp + 1) * 256, b * 2048:(b + 1) * 2048].rearrange("(k p) n -> p k n", p=P)
            elif kind == "in":
                w = t["w_in_2"] if blk2 else t["w_in"]
                c0, cn = (512 * desc[1], 512) if blk2 else IN_COLS[desc[1]]
                dst = slots[s][:, 0:KD * cn].rearrange("p (k n) -> p k n", k=KD)
                src = w[0, :, c0:c0 + cn].rearrange("(k p) n -> p k n", p=P)
            elif kind in ("hg", "at", "sb", "cv"):
                w = t[{"hg": "w_hg_branch", "at": "w_attn_branch", "sb": "w_sb_branch_2", "cv": "w_conv_branch_2"}[kind]]
                dst = slots[s].rearrange("p (k n) -> p k n", k=4)
                src = w[0].rearrange("(k p) n -> p k n", p=P)
            else:
                w = t["w_out_2"] if blk2 else t["w_out"]
                dst = slots[s].rearrange("p (k n) -> p k n", k=KD)
                src = w[0, :, desc[1] * 512:(desc[1] + 1) * 512].rearrange("(k p) n -> p k n", p=P)
            eng.dma_start(dst, src).then_inc(S(f"loaded{s}"), 16)

        def loaded(u):
            return S(f"loaded{u % NSLOT}"), 16 * (u // NSLOT + 1)

        def big_rounds():
            out_ = []
            for base, units in ((0, PRE), (MID0, MID)):
                for n, d in enumerate(units):
                    if d[0] in ("in", "out"):
                        out_.append((base + n, d, 0, True))
                    elif d[0] != "ada":
                        out_ += [(base + n, d, 0, False), (base + n, d, 1, True)]
            return out_

        ROUNDS = big_rounds()
        R2 = sum(1 for r in ROUNDS if r[0] < MID0)
        ADA = [n for n, d in enumerate(PRE) if d[0] == "ada"]

        def unit_free(u):
            if u < MOE1 and PRE[u][0] == "ada":
                return S("ada_done"), ADA.index(u) + 1
            if MOE1 <= u < MID0:
                i = (u - MOE1) % 6
                e = (u - MOE1) // 6
                return (S("m1_up_done"), 4 * e + i + 1) if i < 4 else (S("m1_down_done"), 2 * e + i - 3)
            return S("big_done"), [n for n, r in enumerate(ROUNDS) if r[0] == u and r[3]][0] + 1

        EVAC = "VAAVVV" + "AAAA" + "VVVV" + "VV" + "VVA" + "VVV" + "AAAA" + "VVVV" + "VV"
        assert len(EVAC) == len(ROUNDS)

        def round_free(r):
            e = EVAC[r]
            return S(f"big_free_{e}"), EVAC[:r + 1].count(e)

        def wait(eng, sv):
            eng.wait_ge(sv[0], sv[1])

        block = ctx.enter_context(nc.Block())

        w_up_u = t["w_up"][0].rearrange("e (i k p) n -> e i p k n", p=P, k=2)
        w_dn_u = t["w_down"][0].rearrange("e (i k p) n -> e i p k n", p=P, k=4)

        def moe1_src(e, i):
            w = w_up_u if i < 4 else w_dn_u
            j = i if i < 4 else i - 4
            return w[bass.ds(e, 1), j, :, :, :].rearrange("o p k n -> p (o k) n")

        def moe1_dst(i):
            return slots[(MOE1 + i) % NSLOT].rearrange("p (k n) -> p k n", k=2 if i < 4 else 4)

        def moe2_src(pair, i):
            w = t[("w_gate_e_2", "w_up_e_2", "w_down_e_2")[i]][0]
            return w[bass.ds(2 * pair, 2), :, :].rearrange("o (k p) n -> p (o k) n", p=P)

        def moe2_dst(j, i):
            return slots[(MOE2 + 3 * j + i) % NSLOT].rearrange("p (k n) -> p k n", k=16 if i < 2 else 4)

        brow = at(MMAP, "brow")[0:1, 0:2048]


        def banks(r):
            return slice(2 * (r % 2), 2 * (r % 2) + 2)

        def kt_view(i):
            lo = 8 * SUB * i * (i + 1)
            return at(A1MAP, "kt", lo, 256 * (i + 1)).rearrange("p (g j) -> p g j", g=16)

        HG_EXPS = [at(A1MAP, "qt")] + [at(A1MAP, "kt", 8 * SUB * i * (i + 1), 256 * (i + 1)) for i in range(4)] \
            + [at(A1MAP, "b"), sm("decay")]

        rt = at(MMAP, "rt")
        G = rt[:, 0:68].rearrange("p (t e) -> p t e", t=TT)
        SL = rt[:, 68:136].rearrange("p (t e) -> p t e", t=TT)
        M = rt[:, 136:200].rearrange("p (t e) -> p t e", t=TT)
        LG = rt[:, 200:272].rearrange("p (t e) -> p t e", t=TT)
        V8 = rt[:, 272:288].rearrange("p (t e) -> p t e", t=TT)
        IDF = rt[:, 288:304].rearrange("p (t e) -> p t e", t=TT)
        EX = rt[:, 304:320].rearrange("p (t e) -> p t e", t=TT)
        ESUM = rt[:, 320:322]
        CMAX = rt[:, 322:323]
        TMPE = rt[:, 324:388].rearrange("p (t e) -> p t e", t=TT)
        GV8 = rt[:, 388:404].rearrange("p (t e) -> p t e", t=TT)
        GID = rt[:, 404:420].rearrange("p (t e) -> p t e", t=TT)
        GEX = rt[:, 420:436].rearrange("p (t e) -> p t e", t=TT)
        GSUM = rt[:, 436:438]
        GL = rt[:, 440:456].rearrange("p (t e) -> p t e", t=TT)
        EIG = rt[:, 456:472].rearrange("p (t e) -> p t e", t=TT)
        OH = rt[:, 472:480].rearrange("p (t e) -> p t e", t=TT)
        W8 = rt[:, 480:496].rearrange("p (t e) -> p t e", t=TT)
        M8 = rt[:, 496:512].rearrange("p (t e) -> p t e", t=TT)
        GT = rt[0:NE, 512:768]

        xg1 = at(MMAP, "xg", 0, 512)
        xg2 = at(MMAP, "xg", 0, 1024)
        glu, lin, sg, actb, aT = (at(MMAP, n) for n in ("glu", "lin", "sg", "act", "aT"))
        ye = at(MMAP, "ye")
        swT = at(MMAP, "swT")
        selS = at(MMAP, "selS")
        selW = at(MMAP, "selW")

        def gate_sig(act, r, n, m):
            act.wait_ge(S("big_done"), r + 1)
            nc.scalar.activation(at(m, "gates", 1024 * n, 1024), PS[:, banks(r), :], ACT.Sigmoid)\
                .then_inc(S("big_free_A"), 1)

        def rms_sums(act, n):
            act.wait_ge(S("x_ready"), int(n[1]) - 1)
            for i in range(TT):
                nc.scalar.activation(hT[:, 4 * i:4 * i + 4, :], x[:, i, :].rearrange("p (k n) -> p k n", k=4), ACT.Square,
                                     accum_out=sm("ss")[:, i:i + 1]).then_inc(S("squares"), 1)
            act.wait_ge(S("mean_square"), int(n[1]))
            nc.scalar.sqrt(sm("rs"), sm("ss")).then_inc(S("rms"), 1)

        def hT_copy_act(act, n):
            act.wait_ge(S("h_transposed"), 2 * int(n[1]))
            nc.scalar.activation(hT[:, 4:8, :], PS[:, 2:4, :], ACT.Copy).then_inc(S("hT_A"), 1)

        def moe1_act_gather(act, X, g):
            act.wait_ge(S(f"{X}_gath_done"), g + 1)
            nc.scalar.activation(xg1, PS[:, 0, :], ACT.Copy).then_inc(S(f"{X}_xg"), 1)

        def moe1_act(act, X, it, g):
            act.wait_ge(S(f"{X}_glu"), it + 1)
            nc.scalar.activation(sg, glu, ACT.Sigmoid, scale=1.702).then_inc(S(f"{X}_sg"), 1)
            moe1_act_gather(act, X, g + 1)
            act.wait_ge(S(f"{X}_down_done"), 2 * it + 2)
            nc.scalar.activation(ye[:, 0:512], PS[:, 1, :], ACT.Copy).then_inc(S(f"{X}_ye"), 1)

        def moe2_act_gather(act, X, g):
            act.wait_ge(S(f"{X}_gath_done"), g + 1)
            nc.scalar.activation(xg2, PS[:, 0:2, :], ACT.Copy).then_inc(S(f"{X}_xg"), 1)

        def moe2_act(act, X, it, g):
            act.wait_ge(S(f"{X}_gu_done"), 2 * it + 1)
            nc.scalar.activation(sg[:, 0:256], PS[:, 2, 0:256], ACT.Sigmoid).then_inc(S(f"{X}_sg"), 1)
            moe2_act_gather(act, X, g + 1)
            act.wait_ge(S(f"{X}_down_done"), it + 1)
            nc.scalar.activation(ye, PS[:, 0:2, :], ACT.Copy).then_inc(S(f"{X}_ye"), 1)

        def mm(o, w, m, first, last):
            return nc.tensor.matmul(o, w, m, start=first, stop=last)

        def transpose_h(pe, n):
            pe.wait_ge(S("h"), 2 * int(n[1]))
            for k in range(KD):
                for i in range(TT):
                    c = (k % 2) * 256 + i * P
                    last = nc.tensor.transpose(PS[:, k // 2, c:c + P], h[:, i, k * P:(k + 1) * P], ident)
                if k % 4 == 3:
                    last.then_inc(S("h_transposed"), 1)

        def router_mm(pe, n, w, ne):
            pe.wait_ge(S("hT_V"), int(n[1]))
            pe.wait_ge(S("hT_A"), int(n[1]))
            for i in range(TT):
                for k in range(KD):
                    last = mm(PS[:, 4, 64 * i:64 * i + ne], hT[:, k, i * P:(i + 1) * P], w[:, k, :], k == 0, k == KD - 1)
            last.then_inc(S("logits"), 1)

        def positions_mm(pe, n):
            pe.wait_ge(S("mask"), int(n[1]) // 2)
            mm(PS[:, 5, 0:32], C("before"), M[:, 0, :], True, True)
            mm(PS[:, 5, 64:96], C("ones"), M[:, 0, :], True, False)
            mm(PS[:, 5, 64:96], C("before"), M[:, 1, :], False, True)
            mm(PS[:, 5, 128:160], C("ones"), M[:, 0, :], True, False)
            mm(PS[:, 5, 128:160], C("ones"), M[:, 1, :], False, True).then_inc(S("positions"), 1)

        def moe1_gather(pe, X, g):
            pe.wait_ge(S(f"{X}_sel"), g + 1)
            for k in range(KD):
                for i in range(TT):
                    last = mm(PS[:, 0, k * CAP:(k + 1) * CAP], h[:, i, k * P:(k + 1) * P],
                              selS[:, i * CAP:(i + 1) * CAP], i == 0, i == TT - 1)
            last.then_inc(S(f"{X}_gath_done"), 1)

        def moe1_pe(pe, X, it, g, arrived):
            pe.wait_ge(S(f"{X}_sel"), g + 1)
            pe.wait_ge(S(f"{X}_xg"), g + 1)
            for i in range(TT):
                last = nc.tensor.transpose(PS[:, 0, i * P:(i + 1) * P], selW[:, i * P:(i + 1) * P], ident)
            last.then_inc(S(f"{X}_swt_done"), 1)
            arrived(pe, "bias")
            for b in range(2):
                for half in range(2):
                    c = half * 1024 + b * 512
                    mm(PS[64 * half:64 * half + 64, 2 + b, :], C("ones")[0:1, 0:CAP], brow[:, c:c + 512], True, False)
            for i in range(4):
                arrived(pe, i)
                w = moe1_dst(i)
                for kk in range(2):
                    k = 2 * i + kk
                    for b in range(2):
                        for half in range(2):
                            c = half * 1024 + b * 512
                            last = mm(PS[64 * half:64 * half + 64, 2 + b, :], xg1[:, k * CAP:(k + 1) * CAP],
                                      w[:, kk, c:c + 512], False, k == KD - 1)
                last.then_inc(S(f"{X}_up_done"), 1)
            pe.wait_ge(S(f"{X}_swt"), it + 1)
            moe1_gather(pe, X, g + 1)
            pe.wait_ge(S(f"{X}_act"), it + 1)
            for i in range(4):
                last = nc.tensor.transpose(PS[:, 1, i * P:(i + 1) * P], actb[:, i * P:(i + 1) * P], ident)
            last.then_inc(S(f"{X}_at_done"), 1)
            pe.wait_ge(S(f"{X}_aT"), it + 1)
            for i in range(2):
                arrived(pe, 4 + i)
                w = moe1_dst(4 + i)
                for kk in range(4):
                    for dh in range(2):
                        c = kk * P + i * CAP
                        last = mm(PS[64 * dh:64 * dh + 64, 1, :], aT[:, c:c + CAP], w[:, kk, dh * 512:(dh + 1) * 512],
                                  i == 0 and kk == 0, i == 1 and kk == 3)
                last.then_inc(S(f"{X}_down_done"), 1)
            pe.wait_ge(S(f"{X}_ye"), it + 1)
            pe.wait_ge(S(f"{X}_acc"), it + 1)
            for i in range(TT):
                for dh in range(2):
                    q = slice(64 * dh, 64 * dh + 64)
                    last = mm(PS[:, 4 + 2 * i + dh, :], swT[q, i * P:(i + 1) * P], ye[q, 0:512], True, True)
            last.then_inc(S(f"{X}_scat_done"), 1)

        def moe2_gather(pe, X, g):
            pe.wait_ge(S(f"{X}_sel"), g + 1)
            for k in range(KD):
                for i in range(TT):
                    last = mm(PS[:, k // 4, (k % 4) * P:(k % 4 + 1) * P], h[:, i, k * P:(k + 1) * P],
                              selS[:, i * P:(i + 1) * P], i == 0, i == TT - 1)
            last.then_inc(S(f"{X}_gath_done"), 1)

        def moe2_pe(pe, X, it, g, j, arrived):
            pe.wait_ge(S(f"{X}_sel"), g + 1)
            pe.wait_ge(S(f"{X}_xg"), g + 1)
            for i in range(TT):
                last = nc.tensor.transpose(PS[:, 0, i * P:(i + 1) * P], selW[:, i * P:(i + 1) * P], ident)
            last.then_inc(S(f"{X}_swt_done"), 1)
            for i in range(2):
                arrived(pe, i)
                w = moe2_dst(j, i)
                for k in range(KD):
                    for half in range(2):
                        last = mm(PS[64 * half:64 * half + 64, 2 + i, 0:256],
                                  xg2[:, k * P + 64 * half:k * P + 64 * half + 64], w[:, 8 * half + k, :],
                                  k == 0, k == KD - 1)
                last.then_inc(S(f"{X}_gu_done"), 1)
            pe.wait_ge(S(f"{X}_swt"), it + 1)
            moe2_gather(pe, X, g + 1)
            pe.wait_ge(S(f"{X}_act"), it + 1)
            for i in range(2):
                last = nc.tensor.transpose(PS[:, 2, i * P:(i + 1) * P], actb[:, i * P:(i + 1) * P], ident)
            last.then_inc(S(f"{X}_at_done"), 1)
            pe.wait_ge(S(f"{X}_aT"), it + 1)
            pe.wait_ge(S(f"{X}_xg"), g + 2)
            arrived(pe, 2)
            w = moe2_dst(j, 2)
            for kk in range(2):
                for b in range(2):
                    for half in range(2):
                        c = kk * P + 64 * half
                        last = mm(PS[64 * half:64 * half + 64, b, :], aT[:, c:c + 64],
                                  w[:, 2 * half + kk, b * 512:(b + 1) * 512], kk == 0, kk == 1)
            last.then_inc(S(f"{X}_down_done"), 1)
            pe.wait_ge(S(f"{X}_ye"), it + 1)
            pe.wait_ge(S(f"{X}_acc"), it + 1)
            for i in range(TT):
                for b in range(2):
                    last = mm(PS[:, 4 + 2 * i + b, :], swT[:, i * P:(i + 1) * P], ye[:, b * 512:(b + 1) * 512], True, True)
            last.then_inc(S(f"{X}_scat_done"), 1)

        V = nc.vector

        def bc_mid(a, n):
            return a.rearrange("p (o w) -> p o w", o=1).broadcast_to([a.shape[0], n, a.shape[1]])

        def bc_last(a, n):
            return a.rearrange("p (g o) -> p g o", o=1).broadcast_to([a.shape[0], a.shape[1], n])

        def moe1_select(X, e, iota):
            for i in range(TT):
                V.tensor_scalar(selS[:, i * CAP:(i + 1) * CAP], iota, SL[:, i, bass.ds(e, 1)], None, ALU.is_equal)
                last = V.tensor_scalar(selW[:, i * P:(i + 1) * P].rearrange("p (a w) -> p a w", a=2), bc_mid(iota, 2),
                                       SL[:, i, bass.ds(e, 1)], G[:, i, bass.ds(e, 1)], ALU.is_equal, ALU.mult)
            last.then_inc(S(f"{X}_sel"), 1)

        def moe1_dve(v, X, it, e, g, iota):
            v.wait_ge(S(f"{X}_swt_done"), it + 1)
            V.tensor_copy(swT, PS[:, 0, 0:256]).then_inc(S(f"{X}_swt"), 1)
            v.wait_ge(S(f"{X}_gath_done"), g + 1)
            moe1_select(X, e + 1, iota)
            v.wait_ge(S(f"{X}_up_done"), 4 * it + 4)
            hu = PS[:, 2:4, :].rearrange("p b (n two) -> p b n two", two=2)
            V.tensor_scalar(glu.rearrange("p (b n) -> p b n", b=2), hu[:, :, :, 0], 7.0, None, ALU.min)\
                .then_inc(S(f"{X}_glu"), 1)
            V.tensor_scalar(lin.rearrange("p (b n) -> p b n", b=2), hu[:, :, :, 1], 7.0, -7.0, ALU.min, ALU.max)\
                .then_inc(S(f"{X}_lin"), 1)
            v.wait_ge(S(f"{X}_glu"), it + 1)
            v.wait_ge(S(f"{X}_lin"), 2 * it + 1)
            V.scalar_tensor_tensor(out=lin, in0=lin, scalar=1.0, in1=glu, op0=ALU.add, op1=ALU.mult)\
                .then_inc(S(f"{X}_lin"), 1)
            v.wait_ge(S(f"{X}_lin"), 2 * it + 2)
            v.wait_ge(S(f"{X}_sg"), it + 1)
            V.tensor_tensor(actb, lin, sg, ALU.mult).then_inc(S(f"{X}_act"), 1)
            v.wait_ge(S(f"{X}_at_done"), it + 1)
            V.tensor_copy(aT, PS[:, 1, :]).then_inc(S(f"{X}_aT"), 1)
            v.wait_ge(S(f"{X}_scat_done"), it + 1)
            v.wait_ge(S(f"{X}_acc"), it + 1)
            V.tensor_tensor(acc, acc, PS[:, 4:8, :].rearrange("p b n -> p (b n)"), ALU.add).then_inc(S(f"{X}_acc"), 1)

        def moe2_select(X, e0, iota):
            for i in range(TT):
                for j in range(2):
                    c = i * P + j * CAP
                    col = bass.ds(e0 + j, 1)
                    V.tensor_scalar(selS[:, c:c + CAP], iota, SL[:, i, col], None, ALU.is_equal)
                    last = V.tensor_scalar(selW[:, c:c + CAP], iota, SL[:, i, col], G[:, i, col], ALU.is_equal, ALU.mult)
            last.then_inc(S(f"{X}_sel"), 1)

        def moe2_dve(v, X, it, pair, g, iota):
            v.wait_ge(S(f"{X}_swt_done"), it + 1)
            V.tensor_copy(swT, PS[:, 0, 0:256]).then_inc(S(f"{X}_swt"), 1)
            v.wait_ge(S(f"{X}_gath_done"), g + 1)
            moe2_select(X, 2 * pair + 2, iota)
            v.wait_ge(S(f"{X}_sg"), it + 1)
            V.tensor_tensor(glu[:, 0:256], PS[:, 2, 0:256], sg[:, 0:256], ALU.mult).then_inc(S(f"{X}_glu"), 1)
            v.wait_ge(S(f"{X}_glu"), it + 1)
            v.wait_ge(S(f"{X}_gu_done"), 2 * it + 2)
            V.tensor_tensor(actb[:, 0:256], glu[:, 0:256], PS[:, 3, 0:256], ALU.mult).then_inc(S(f"{X}_act"), 1)
            v.wait_ge(S(f"{X}_at_done"), it + 1)
            V.tensor_copy(aT[:, 0:256], PS[:, 2, 0:256]).then_inc(S(f"{X}_aT"), 1)
            v.wait_ge(S(f"{X}_scat_done"), it + 1)
            v.wait_ge(S(f"{X}_acc"), it + 1)
            V.tensor_tensor(acc, acc, PS[:, 4:8, :].rearrange("p b n -> p (b n)"), ALU.add).then_inc(S(f"{X}_acc"), 1)

        @block.sync
        def _(sp):
            for u, d in enumerate(PRE):
                if u >= NSLOT:
                    wait(sp, unit_free(u - NSLOT))
                unit_load(sp, u, d)
            for i in range(6):
                wait(sp, unit_free(MOE1 + i - NSLOT))
                if i == 0:
                    sp.wait_ge(S("m1_brow_free"), 1)
                    sp.dma_start(brow, t["b_up"][0, 0:1, :]).then_inc(S("m1_brow"), 16)
                sp.dma_start(moe1_dst(i), moe1_src(0, i)).then_inc(S(f"loaded{(MOE1 + i) % NSLOT}"), 16)
            with sp.Fori(1, NE) as e:
                for i in range(6):
                    if i < 4:
                        sp.wait_ge(S("m1_up_done"), 4 * e + (i - 3))
                    else:
                        sp.wait_ge(S("m1_down_done"), 2 * e + (i - 5))
                    if i == 0:
                        sp.dma_start(brow, t["b_up"][0, bass.ds(e, 1), :]).then_inc(S("m1_brow"), 16)
                    sp.dma_start(moe1_dst(i), moe1_src(e, i)).then_inc(S(f"loaded{(MOE1 + i) % NSLOT}"), 16)
            sp.wait_ge(S("m1_flag"), 1)
            more = sp.value_load(flag[0:1, 0:1], min_val=0, max_val=SEQ)
            sp.wait_ge(S("m1_down_done"), 2 * NE)
            with sp.If(more > CAP):
                with sp.Fori(0, EXTRA) as p:
                    with sp.Fori(0, NE) as e:
                        sp.wait_ge(S("m1_scat_done"), NE * (p + 1) + e)
                        sp.dma_start(brow, t["b_up"][0, bass.ds(e, 1), :]).then_inc(S("x1_loaded"), 16)
                        for i in range(6):
                            sp.dma_start(moe1_dst(i), moe1_src(e, i)).then_inc(S("x1_loaded"), 16)
                sp.wait_ge(S("m1_scat_done"), NE * (EXTRA + 1))
            for n, d in enumerate(MID):
                wait(sp, unit_free(MID0 + n - NSLOT))
                unit_load(sp, MID0 + n, d)
            for j in range(2):
                for i in range(3):
                    wait(sp, unit_free(MOE2 + 3 * j + i - NSLOT))
                    sp.dma_start(moe2_dst(j, i), moe2_src(j, i)).then_inc(S(f"loaded{(MOE2 + 3 * j + i) % NSLOT}"), 16)
            with sp.Fori(1, NE // 4) as q:
                for j in range(2):
                    for i in range(3):
                        if i < 2:
                            sp.wait_ge(S("m2_gu_done"), 4 * q + (2 * j + i - 3))
                        else:
                            sp.wait_ge(S("m2_down_done"), 2 * q + (j - 1))
                        sp.dma_start(moe2_dst(j, i), moe2_src(2 * q + j, i))\
                          .then_inc(S(f"loaded{(MOE2 + 3 * j + i) % NSLOT}"), 16)
            sp.wait_ge(S("m2_flag"), 1)
            more = sp.value_load(flag[0:1, 1:2], min_val=0, max_val=SEQ)
            sp.wait_ge(S("m2_down_done"), NE // 2)
            with sp.If(more > CAP):
                with sp.Fori(0, EXTRA) as p:
                    with sp.Fori(0, NE // 2) as q:
                        sp.wait_ge(S("m2_scat_done"), (NE // 2) * (p + 1) + q)
                        for i in range(3):
                            sp.dma_start(moe2_dst(0, i), moe2_src(q, i)).then_inc(S("x2_loaded"), 16)
                sp.wait_ge(S("m2_scat_done"), (NE // 2) * (EXTRA + 1))
            sp.wait_ge(S("result"), 1)
            sp.dma_start(out[0].rearrange("(t p) d -> p t d", p=P), x[:, :, :]).then_inc(S("stored"), 16)
            sp.wait_ge(S("stored"), 16)

        @block.gpsimd
        def _(pool):
            def bc(src):
                return src.partition_broadcast(P)

            def small_load(dst, src, name):
                pool.dma_start(dst, src).then_inc(S(name), 16)

            small_load(gain, bc(t["norm1_gain"][0]), "gain")
            small_load(sm("hg_gain"), bc(t["hg_norm_gain"][0]), "smalls")
            small_load(sm("q_gain"), bc(t["q_norm_gain"][0]), "smalls")
            small_load(sm("k_gain"), bc(t["k_norm_gain"][0]), "smalls")
            small_load(sm("q_gain2"), bc(t["q_norm_g_2"][0]), "smalls")
            small_load(sm("k_gain2"), bc(t["k_norm_g_2"][0]), "smalls")
            small_load(sm("sink"), bc(t["attn_sinks"][0]), "smalls")
            small_load(sm("b_r1"), bc(t["b_router"][0]), "smalls")
            small_load(sm("b_r2", 4), bc(t["b_router_group_2"][0]), "smalls")
            small_load(sm("b_r2")[:, 4:36], bc(t["b_router_expert_2"][0]), "smalls")
            small_load(sm("w_r1").rearrange("p (k n) -> p k n", k=KD),
                       t["w_router"][0].rearrange("(k p) n -> p k n", p=P), "smalls")
            wr2 = sm("w_r2").rearrange("p (k n) -> p k n", k=KD)
            small_load(wr2[:, :, 0:4], t["w_router_group_2"][0].rearrange("(k p) n -> p k n", p=P), "smalls")
            small_load(wr2[:, :, 4:36], t["w_router_expert_2"][0].rearrange("(k p) n -> p k n", p=P), "smalls")
            pool.wait_ge(S("gain_free"), 1)
            small_load(gain, bc(t["norm2_gain"][0]), "gain")
            pool.wait_ge(S("m1_brow_free"), 1)
            small_load(at(MMAP, "bdown")[0:NE, 0:D], t["b_down"][0], "bdown")
            pool.wait_ge(S("gain_free"), 2)
            small_load(gain, bc(t["norm_mix_g_2"][0]), "gain")
            pool.wait_ge(S("gain_free"), 3)
            small_load(at(A2MAP, "gain"), bc(t["norm_ffn_g_2"][0]), "ffn_gain")

        NSMALLS = 12 * 16
        lb_rows = t["lower_bound_logits"].rearrange("l (h k) -> (l h) k", k=P)
        conv_rows = t["conv_w_2"][0].rearrange("j (m k) -> (j m) k", k=P)

        @block.scalar
        def _(act):
            A = nc.scalar.activation
            act.dma_start(consts[:, :], t["consts"]).then_inc(S("consts"), 16)
            act.dma_start(rows[0:8, :], t["c"][0].rearrange("(k p) -> k p", p=P)).then_inc(S("rows"), 16)
            act.dma_start(rows[8:16, :], lb_rows).then_inc(S("rows"), 16)
            act.dma_start(rows[16:28, :], conv_rows).then_inc(S("rows"), 16)
            act.dma_start(x[:, :, :], t["x"][0].rearrange("(t p) d -> p t d", p=P)).then_inc(S("x"), 16)
            act.dma_start(pos[32:34, :], t["positions"][0].rearrange("(t p) -> t p", p=P)).then_inc(S("pos"), 16)
            act.wait_ge(S("modrow_zero"), 1)
            for j in range(4):
                act.dma_start(modrow[32 * j:32 * j + 1, :, :],
                              t["b_ada"].rearrange("o (b j n) -> o b j n", b=3, j=4)[:, :, j, :]).then_inc(S("b_ada"), 16)

            act.wait_ge(S("x"), 16)
            for i in range(TT):
                A(hT[:, 4 * i:4 * i + 4, :], x[:, i, :].rearrange("p (k n) -> p k n", k=4), ACT.Square,
                  accum_out=sm("ss")[:, i:i + 1]).then_inc(S("squares"), 1)
            act.wait_ge(S("cols"), 1)
            A(sm("cond"), sm("cols", 8), ACT.Sigmoid).then_inc(S("sig_c"), 1)
            act.wait_ge(S("lbd"), 1)
            A(sm("lb"), sm("lbd"), ACT.Sigmoid).then_inc(S("lb"), 1)
            act.wait_ge(S("mean_square"), 1)
            nc.scalar.sqrt(sm("rs"), sm("ss")).then_inc(S("rms"), 1)
            act.wait_ge(S("angles"), 2)
            A(sm("sin"), sm("rr"), ACT.Sin).then_inc(S("sincos"), 1)
            A(sm("cos"), sm("rn"), ACT.Sin).then_inc(S("sincos"), 1)
            hT_copy_act(act, "n1")
            act.wait_ge(S("big_done"), 1)
            A(at(A1MAP, "tmp"), PS[:, 0:2, :], ACT.Sigmoid).then_inc(S("sig_q"), 1)
            act.wait_ge(S("big_done"), 2)
            A(at(A1MAP, "b"), PS[:, 2:4, :], ACT.Sigmoid).then_inc(S("big_free_A"), 1)
            act.wait_ge(S("forget"), 4)
            A(at(A1MAP, "b"), at(A1MAP, "k"), ACT.Ln).then_inc(S("log_f"), 1)
            act.wait_ge(S("big_done"), 3)
            A(at(A1MAP, "v"), PS[:, 0:2, :], ACT.Copy).then_inc(S("big_free_A"), 1)
            act.wait_ge(S("big_done"), 4)
            A(at(A1MAP, "gs"), PS[:, 2:4, :], ACT.Sigmoid).then_inc(S("sig_g"), 1)
            act.wait_ge(S("b_ready"), 1)
            A(at(A1MAP, "tmp"), at(A1MAP, "b"), ACT.Exp).then_inc(S("hg_expb"), 1)
            for n, buf in enumerate(HG_EXPS):
                act.wait_ge(S("hg_arg"), min(n + 1, 6))
                A(buf, buf, ACT.Exp).then_inc(S("hg_exp"), 1)
            act.wait_ge(S("att_ms"), 1)
            nc.scalar.sqrt(sm("rsa", 24), sm("ssa", 24)).then_inc(S("att_std"), 1)
            for n in range(2):
                gate_sig(act, 6 + n, n, A1MAP)
            act.wait_ge(S("hgo_ms"), 1)
            nc.scalar.sqrt(sm("rsh"), sm("ssh")).then_inc(S("hgo_std"), 1)
            for n in range(2, 4):
                gate_sig(act, 6 + n, n, A1MAP)
            act.wait_ge(S("att_nm"), 1)
            s = at(A1MAP, "s").rearrange("p (h n) -> p h n", h=AH)
            for hh in range(AH):
                A(s[:, hh, 0:P], s[:, hh, 0:P], ACT.Exp, bias=sm("nm")[:, hh:hh + 1],
                  accum_out=sm("den")[:, hh:hh + 1]).then_inc(S("att_exp"), 1)
                A(s[:, hh, P:3 * P], s[:, hh, P:3 * P], ACT.Exp, bias=sm("nm")[:, 8 + hh:9 + hh],
                  accum_out=sm("den")[:, 8 + hh:9 + hh]).then_inc(S("att_exp"), 1)
            A(sm("es"), sm("es"), ACT.Exp).then_inc(S("att_exp"), 1)
            rms_sums(act, "n2")
            hT_copy_act(act, "n2")
            act.wait_ge(S("r1_arg"), TT)
            for i in range(TT):
                A(EX[:, i, 0:4], EX[:, i, 0:4], ACT.Exp, accum_out=ESUM[:, i:i + 1])\
                    .then_inc(S("r1_exp"), 1)
            moe1_act_gather(act, "m1", 0)
            with act.Fori(0, NE) as e:
                moe1_act(act, "m1", e, e)
            act.wait_ge(S("m1_flag"), 1)
            more = act.value_load(flag[0:1, 0:1], min_val=0, max_val=SEQ)
            with act.If(more > CAP):
                with act.Fori(0, EXTRA) as p:
                    moe1_act_gather(act, "m1", (NE + 1) * (p + 1))
                    with act.Fori(0, NE) as e:
                        moe1_act(act, "m1", NE * (p + 1) + e, (NE + 1) * (p + 1) + e)
            rms_sums(act, "n3")
            hT_copy_act(act, "n3")
            act.wait_ge(S("big_done"), R2 + 3)
            A(at(A2MAP, "v"), PS[:, banks(R2 + 2), :], ACT.Copy).then_inc(S("big_free_A"), 1)
            act.wait_ge(S("sb_ms"), 1)
            nc.scalar.sqrt(sm("rsa"), sm("ssa")).then_inc(S("sb_std"), 1)
            for n in range(2):
                gate_sig(act, R2 + 6 + n, n, A2MAP)
            z = at(A2MAP, "z")
            sp_ = at(A2MAP, "sp")
            for g in range(2):
                act.wait_ge(S("sb_z"), g + 1)
                c = slice(1536 * g, 1536 * (g + 1))
                A(sp_[:, c], z[:, c], ACT.Abs).then_inc(S("sb_e"), 1)
                act.wait_ge(S("sb_e"), 2 * g + 1)
                A(sp_[:, c], sp_[:, c], ACT.Exp, scale=-1.0).then_inc(S("sb_e"), 1)
                act.wait_ge(S("sb_e"), 2 * g + 2)
                A(sp_[:, c], sp_[:, c], ACT.Ln, bias=C("ones")[:, 0:1]).then_inc(S("sb_ln"), 1)
            for n in range(2, 4):
                gate_sig(act, R2 + 6 + n, n, A2MAP)
            for g in range(2):
                act.wait_ge(S("sb_d"), g + 1)
                c = slice(1536 * g, 1536 * (g + 1))
                A(z[:, c], z[:, c], ACT.Exp).then_inc(S("sb_a"), 1)
            rms_sums(act, "n4")
            hT_copy_act(act, "n4")
            act.wait_ge(S("r2_arg"), TT)
            for i in range(TT):
                A(GEX[:, i, 0:4], GEX[:, i, 0:4], ACT.Exp, accum_out=GSUM[:, i:i + 1])\
                    .then_inc(S("r2_exp"), 1)
                A(EX[:, i, 0:2], EX[:, i, 0:2], ACT.Exp, accum_out=ESUM[:, i:i + 1])\
                    .then_inc(S("r2_exp"), 1)
            moe2_act_gather(act, "m2", 0)
            with act.Fori(0, NE // 4) as q:
                for j in range(2):
                    moe2_act(act, "m2", 2 * q + j, 2 * q + j)
            act.wait_ge(S("m2_flag"), 1)
            more = act.value_load(flag[0:1, 1:2], min_val=0, max_val=SEQ)
            with act.If(more > CAP):
                with act.Fori(0, EXTRA) as p:
                    moe2_act_gather(act, "m2", (NE // 2 + 1) * (p + 1))
                    with act.Fori(0, NE // 2) as q:
                        moe2_act(act, "m2", (NE // 2) * (p + 1) + q, (NE // 2 + 1) * (p + 1) + q)

        @block.tensor
        def _(pe):
            aux = [0]

            def aux_bank():
                r = aux[0]
                aux[0] += 1
                if r >= 2:
                    pe.wait_ge(S("aux_free"), r - 1)
                return PS[:, 4 + r % 2, :]

            def begin(r):
                wait(pe, loaded(ROUNDS[r][0]))
                if r >= 2:
                    wait(pe, round_free(r - 2))
                return PS[:, banks(r), :], slots[ROUNDS[r][0] % NSLOT]

            def dense_tokens(r, n=512, src=hT):
                o, w = begin(r)
                w = w[:, 0:KD * n].rearrange("p (k n) -> p k n", k=KD)
                for i in range(TT):
                    for k in range(KD):
                        last = mm(o[:, i, 0:n], src[:, k, i * P:(i + 1) * P], w[:, k, :], k == 0, k == KD - 1)
                last.then_inc(S("big_done"), 1)

            def dense_cols(r, src, nk, n, c0=0):
                o, w = begin(r)
                o = o.rearrange("p b (c t) -> p (b c) t", c=2)
                w = w.rearrange("p (k n) -> p k n", k=nk)
                for c in range(4):
                    for k in range(nk):
                        last = mm(o[:, c, :], w[:, k, c0 + c * P:c0 + (c + 1) * P], src[:, k, :], k == 0, k == nk - 1)
                last.then_inc(S("big_done"), 1)

            def ada(n):
                u = ADA[n]
                b, kp = PRE[u][1:]
                wait(pe, loaded(u))
                w = slots[u % NSLOT].rearrange("p (k n) -> p k n", k=2)
                for kk in range(2):
                    k = 2 * kp + kk
                    for j in range(4):
                        last = nc.tensor.matmul(PS[32 * j:32 * j + 32, 7 if b != 1 else 6, :],
                                                sm("cond32")[:, 32 * k:32 * k + 32], w[:, kk, 512 * j:512 * (j + 1)],
                                                start=k == 0, stop=k == KD - 1, tile_position=(0, 32 * j))
                last.then_inc(S("ada_done"), 1)

            def spread_row(j):
                return ident[:, 32 * j:32 * j + 1].broadcast_to([P, P])

            pe.wait_ge(S("consts"), 16)
            pe.wait_ge(S("rows"), 48)
            nc.tensor.transpose(PS[:, 0, 0:28], rows[0:28, :], ident[0:28, 0:28])
            pe.wait_ge(S("posf"), 1)
            nc.tensor.transpose(PS[:, 1, 0:2], rows[32:34, :], ident[32:34, 32:34]).then_inc(S("rowsT"), 1)
            pe.wait_ge(S("cond32"), 1)
            for n in range(4):
                ada(n)
            pe.wait_ge(S("modrow"), 1)
            for j in range(4):
                mm(PS[:, j, :], spread_row(j), modrow[:, 0, :], True, True).then_inc(S("mod1"), 1)
            transpose_h(pe, "n1")
            pe.wait_ge(S("hT_V"), 1)
            pe.wait_ge(S("hT_A"), 1)
            dense_cols(0, hT, KD, 512)
            dense_cols(1, hT, KD, 512)
            ada(4)
            dense_tokens(2)
            ada(5)
            dense_tokens(3)
            ada(6)
            dense_tokens(4)
            ada(7)
            dense_tokens(5, 256)
            ada(8)
            pe.wait_ge(S("hg_scores_in"), 1)
            o = aux_bank().rearrange("p (g i) -> p g i", g=8)
            qt = at(A1MAP, "qt").rearrange("p (g i) -> p g i", g=16)
            for hc in range(16):
                q0 = 64 * (hc % 2)
                for i in range(4):
                    n = SUB * (i + 1)
                    last = mm(o[q0:q0 + n, hc // 2, SUB * i:SUB * i + SUB], kt_view(i)[:, hc, :],
                              qt[:, hc, SUB * i:SUB * i + SUB], True, True)
            last.then_inc(S("aux_done"), 1)
            dense_cols(6, hT, KD, 512)
            ada(9)
            pe.wait_ge(S("hg_kd"), 1)
            kd = at(A1MAP, "b").rearrange("p (h t) -> p h t", h=HH)
            kdT = at(A1MAP, "kdT").rearrange("p (t h k) -> p t h k", t=TT, h=HH)
            vals = at(A1MAP, "v").rearrange("p (t h v) -> p t h v", t=TT, h=HH)
            for i in range(TT):
                o = aux_bank()
                for hh in range(HH):
                    last = nc.tensor.transpose(o[:, hh * P:(hh + 1) * P], kd[:, hh, i * P:(i + 1) * P], ident)
                last.then_inc(S("aux_done"), 1)
            for c in range(3):
                i, q = c // 2, slice(64 * (c % 2), 64 * (c % 2) + 64)
                o = aux_bank()
                pe.wait_ge(S("hg_kdT"), i + 1)
                for hh in range(HH):
                    last = mm(o[:, hh * P:(hh + 1) * P], kdT[q, i, hh, :], vals[q, i, hh, :], True, True)
                last.then_inc(S("aux_done"), 1)
            dense_cols(7, hT, KD, 512)
            ada(10)
            st = at(A1MAP, "st").rearrange("p (h t i) -> p h t i", h=HH, t=TT)
            qb = at(A1MAP, "q").rearrange("p (h t) -> p h t", h=HH)
            states = at(A1MAP, "state").rearrange("p (c h v) -> p c h v", c=3, h=HH)
            pe.wait_ge(S("hg_st"), 1)
            for i in range(TT):
                o = aux_bank()
                for par in range(2):
                    c, q = 2 * i + par, slice(64 * par, 64 * par + 64)
                    if c:
                        pe.wait_ge(S("hg_state"), c)
                    for hh in range(HH):
                        oo = o[q, hh * P:(hh + 1) * P]
                        last = mm(oo, st[q, hh, i, :], vals[q, i, hh, :], True, c == 0)
                        if c:
                            last = mm(oo, qb[:, hh, c * CH:(c + 1) * CH], states[:, c - 1, hh, :], False, True)
                last.then_inc(S("aux_done"), 1)
            dense_cols(8, hT, KD, 512)
            ada(11)
            pe.wait_ge(S("hg_out"), 1)
            ho = at(A1MAP, "o").rearrange("p (t h v) -> p t h v", t=TT, h=HH)
            for r in range(2):
                o = aux_bank()
                for j in range(2):
                    for i in range(TT):
                        last = nc.tensor.transpose(o[:, (2 * j + i) * P:(2 * j + i + 1) * P], ho[:, i, 2 * r + j, :], ident)
                last.then_inc(S("aux_done"), 1)
            qk = at(A1MAP, "qk").rearrange("p (t b w) -> p t b w", t=TT, w=P)
            qkT = at(A1MAP, "qkT").rearrange("p (b t) -> p b t", b=6)
            pe.wait_ge(S("att_qk"), 1)
            for r in range(3):
                o = aux_bank()
                for j in range(2):
                    for i in range(TT):
                        last = nc.tensor.transpose(o[:, (2 * j + i) * P:(2 * j + i + 1) * P], qk[:, i, 2 * r + j, :], ident)
                last.then_inc(S("aux_done"), 1)
            dense_cols(9, hT, KD, 512)
            pe.wait_ge(S("att_qkT"), 3)

            def att_score(o, hh, qtile, keys):
                q = slice(64 * (hh % 2), 64 * (hh % 2) + 64)
                return mm(o, qkT[q, hh // 2, qtile * P:(qtile + 1) * P], qkT[q, 4 + hh // 4, 0:keys], True, True)

            for r in range(2):
                o = aux_bank()
                for j in range(4):
                    last = att_score(o[:, j * P:(j + 1) * P], 2 * j + r, 0, P)
                last.then_inc(S("aux_done"), 1)
            for r in range(4):
                o = aux_bank()
                for j in range(2):
                    last = att_score(o[:, j * 256:(j + 1) * 256], 4 * (r // 2) + r % 2 + 2 * j, 1, 256)
                last.then_inc(S("aux_done"), 1)
            s = at(A1MAP, "s").rearrange("p (h n) -> p h n", h=AH)
            pe.wait_ge(S("att_p"), 1)
            for b in range(3):
                for r in range(2):
                    o = aux_bank()
                    for j in range(4):
                        last = nc.tensor.transpose(o[:, j * P:(j + 1) * P], s[:, 4 * r + j, b * P:(b + 1) * P], ident)
                    last.then_inc(S("aux_done"), 1)
            pT0 = at(A1MAP, "pT0").rearrange("p (h q) -> p h q", h=AH)
            pT1 = at(A1MAP, "pT1").rearrange("p (h q) -> p h q", h=AH)
            vv = at(A1MAP, "vv").rearrange("p (t d) -> p t d", t=TT)
            pe.wait_ge(S("att_pT"), 6)
            for r in range(2):
                o = aux_bank().rearrange("p (m t) -> p m t", m=2)
                for j in range(4):
                    hh = 4 * r + j
                    q, kv = slice(64 * (hh % 2), 64 * (hh % 2) + 64), slice(HD * (hh // 4), HD * (hh // 4) + HD)
                    mm(o[q, j // 2, :], vv[:, 0, kv], pT0[:, hh, :], True, False)
                    last = mm(o[q, j // 2, P:256], vv[:, 1, kv], pT1[:, hh, :], False, True)
                last.then_inc(S("aux_done"), 1)
            pe.wait_ge(S("modrow"), 3)

            def spread(b, j):
                mm(aux_bank(), spread_row(j), modrow[:, b, :], True, True).then_inc(S("aux_done"), 1)

            spread(1, 0)
            spread(1, 1)
            pe.wait_ge(S("hg_oT"), 2)
            oT = at(A1MAP, "oT").rearrange("p (h t) -> p h t", h=HH)
            attT = at(A1MAP, "attT").rearrange("p (m t) -> p m t", m=4)
            dense_cols(10, oT, 4, D)
            dense_cols(11, oT, 4, D, 512)
            pe.wait_ge(S("att_oT"), 2)
            dense_cols(12, attT, 4, D)
            dense_cols(13, attT, 4, D, 512)
            for b, j in ((1, 2), (1, 3), (2, 0), (2, 1), (2, 2), (2, 3)):
                spread(b, j)
            pe.wait_ge(S("merged"), 1)
            merged = at(A1MAP, "gates", 0, 2048).rearrange("p (k t) -> p k t", k=KD)
            dense_tokens(14, src=merged)
            dense_tokens(15, src=merged)
            transpose_h(pe, "n2")
            router_mm(pe, "n2", sm("w_r1").rearrange("p (k n) -> p k n", k=KD), NE)
            positions_mm(pe, "n2")
            for i in range(TT):
                last = nc.tensor.transpose(PS[0:NE, 6, i * P:(i + 1) * P], G[:, i, 0:NE], ident)
            last.then_inc(S("gT"), 1)
            pe.wait_ge(S("gT_copy"), 1)
            pe.wait_ge(S("bdown"), 16)
            for i in range(TT):
                for b in range(2):
                    last = mm(PS[:, 2 * i + b, :], GT[:, i * P:(i + 1) * P],
                              at(MMAP, "bdown")[0:NE, b * 512:(b + 1) * 512], True, True)
            last.then_inc(S("bias_rows"), 1)
            pe.wait_ge(S("m1_acc"), 1)
            moe1_gather(pe, "m1", 0)
            with pe.Fori(0, NE) as e:
                def arrived(pe, i):
                    if i == "bias":
                        pe.wait_ge(S("m1_brow"), 16 * e + 16)
                    else:
                        sl, n = loaded(MOE1 + i)
                        pe.wait_ge(sl, 16 * e + n)
                moe1_pe(pe, "m1", e, e, arrived)
            pe.wait_ge(S("m1_flag"), 1)
            more = pe.value_load(flag[0:1, 0:1], min_val=0, max_val=SEQ)
            with pe.If(more > CAP):
                with pe.Fori(0, EXTRA) as p:
                    moe1_gather(pe, "m1", (NE + 1) * (p + 1))
                    with pe.Fori(0, NE) as e:
                        def arrived(pe, i):
                            if i == "bias":
                                pe.wait_ge(S("x1_loaded"), 112 * (NE * p + e) + 112)
                        moe1_pe(pe, "m1", NE * (p + 1) + e, (NE + 1) * (p + 1) + e, arrived)
            transpose_h(pe, "n3")
            pe.wait_ge(S("hT_V"), 3)
            pe.wait_ge(S("hT_A"), 3)
            r = R2
            dense_tokens(r)
            dense_tokens(r + 1)
            dense_tokens(r + 2)
            for n in range(3, 5):
                dense_cols(r + n, hT, KD, 512)
            qk2 = at(A2MAP, "qk").rearrange("p (t b w) -> p t b w", t=TT, w=P)
            qkT2 = at(A2MAP, "qkT").rearrange("p (b t) -> p b t", b=8)
            pe.wait_ge(S("sb_qk"), 1)
            for n in range(4):
                o = aux_bank()
                for j in range(2):
                    for i in range(TT):
                        last = nc.tensor.transpose(o[:, (2 * j + i) * P:(2 * j + i + 1) * P], qk2[:, i, 2 * n + j, :], ident)
                last.then_inc(S("aux_done"), 1)
            dense_cols(r + 5, hT, KD, 512)
            pe.wait_ge(S("sb_qkT"), 4)
            for hh in range(8):
                q, m = slice(64 * (hh % 2), 64 * (hh % 2) + 64), hh // 2
                o = aux_bank()
                mm(o[:, 0:256], qkT2[q, 4 + m, 0:P], qkT2[q, m, :], True, True)
                mm(o[:, 256:384], qkT2[q, 4 + m, P:256], qkT2[q, m, P:256], True, True).then_inc(S("aux_done"), 1)
            for n in range(6, 8):
                dense_cols(r + n, hT, KD, 512)
            spv = at(A2MAP, "sp").rearrange("p (h n) -> p h n", h=8)
            for hh in range(8):
                if hh % 4 == 0:
                    pe.wait_ge(S("sb_sp"), hh // 4 + 1)
                o = aux_bank()
                mm(o[:, 0:256], C("from_here"), spv[:, hh, 0:256], True, False)
                mm(o[:, P:256], C("ones"), spv[:, hh, 256:384], False, True)
                mm(o[:, 256:384], C("from_here"), spv[:, hh, 256:384], True, True).then_inc(S("aux_done"), 1)
            for n in range(8, 10):
                dense_cols(r + n, hT, KD, 512)
            za = at(A2MAP, "z").rearrange("p (h n) -> p h n", h=8)
            v2 = at(A2MAP, "v").rearrange("p (t d) -> p t d", t=TT)
            for n in range(2):
                pe.wait_ge(S("sb_w"), n + 1)
                o = aux_bank().rearrange("p (m t) -> p m t", m=2)
                for j in range(4):
                    hh = 4 * n + j
                    q = slice(64 * (hh % 2), 64 * (hh % 2) + 64)
                    mm(o[q, j // 2, :], v2[:, 0, hh * HD:(hh + 1) * HD], za[:, hh, 0:256], True, False)
                    last = mm(o[q, j // 2, P:256], v2[:, 1, hh * HD:(hh + 1) * HD], za[:, hh, 256:384], False, True)
                last.then_inc(S("aux_done"), 1)
            pe.wait_ge(S("sb_oT"), 2)
            sbT = at(A2MAP, "attT").rearrange("p (m t) -> p m t", m=4)
            cvT = at(A2MAP, "cv").rearrange("p (m t) -> p m t", m=4)
            dense_cols(r + 10, sbT, 4, D)
            dense_cols(r + 11, sbT, 4, D, 512)
            pe.wait_ge(S("conv"), 1)
            dense_cols(r + 12, cvT, 4, D)
            dense_cols(r + 13, cvT, 4, D, 512)
            pe.wait_ge(S("merged"), 2)
            dense_tokens(r + 14, src=merged)
            dense_tokens(r + 15, src=merged)
            transpose_h(pe, "n4")
            router_mm(pe, "n4", sm("w_r2").rearrange("p (k n) -> p k n", k=KD), 36)
            positions_mm(pe, "n4")
            pe.wait_ge(S("m2_sel"), 1)
            moe2_gather(pe, "m2", 0)
            with pe.Fori(0, NE // 4) as q:
                for j in range(2):
                    def arrived(pe, i):
                        sl, n = loaded(MOE2 + 3 * j + i)
                        pe.wait_ge(sl, 16 * q + n)
                    moe2_pe(pe, "m2", 2 * q + j, 2 * q + j, j, arrived)
            pe.wait_ge(S("m2_flag"), 1)
            more = pe.value_load(flag[0:1, 1:2], min_val=0, max_val=SEQ)
            with pe.If(more > CAP):
                with pe.Fori(0, EXTRA) as p:
                    moe2_gather(pe, "m2", (NE // 2 + 1) * (p + 1))
                    with pe.Fori(0, NE // 2) as q:
                        def arrived(pe, i):
                            if i == 0:
                                pe.wait_ge(S("x2_loaded"), 48 * ((NE // 2) * p + q) + 48)
                        moe2_pe(pe, "m2", (NE // 2) * (p + 1) + q, (NE // 2 + 1) * (p + 1) + q, 0, arrived)

        @block.vector
        def _(v):
            count, aux = {}, [0]

            def sig(ins, name):
                count[name] = count.get(name, 0) + 1
                ins.then_inc(S(name), 1)
                v.wait_ge(S(name), count[name])

            def L(ins):
                sig(ins, "v_step")

            def aux_bank():
                r = aux[0]
                aux[0] += 1
                v.wait_ge(S("aux_done"), r + 1)
                return PS[:, 4 + r % 2, :]

            def begin(r):
                v.wait_ge(S("big_done"), r + 1)
                return PS[:, banks(r), :]

            TS, TV, STT, CP = V.tensor_scalar, V.tensor_tensor, V.scalar_tensor_tensor, V.tensor_copy

            sig(V.memset(modrow[:, :, :], 0.0), "modrow_zero")
            v.wait_ge(S("pos"), 16)
            sig(CP(rows[32:34, :], pos[32:34, :]), "posf")
            v.wait_ge(S("rowsT"), 1)
            cols = sm("cols")
            L(CP(cols, PS[:, 0, 0:28]))
            sig(TV(sm("lbd"), cols[:, 8:12], cols[:, 12:16], ALU.subtract), "lbd")
            sig(CP(sm("one_lb"), sm("lbd")), "cols")
            v.wait_ge(S("sig_c"), 1)
            L(TV(sm("cond"), sm("cond"), cols[:, 0:8], ALU.mult))
            sig(CP(sm("cond32").rearrange("p (k m) -> p k m", k=KD), bc_last(sm("cond"), 32)), "cond32")
            v.wait_ge(S("lb"), 1)
            L(TS(sm("one_lb"), sm("lb"), -1.0, 1.0, ALU.mult, ALU.add))
            v.wait_ge(S("squares"), 2)
            sig(TS(sm("ss"), sm("ss"), 1.0 / D, EPS, ALU.mult, ALU.add), "mean_square")
            v.wait_ge(S("rms"), 1)
            L(V.reciprocal(sm("rs"), sm("rs")))
            v.wait_ge(S("consts"), 16)
            L(CP(sm("posf"), PS[:, 1, 0:2]))
            ang, rr, rn = sm("ang"), sm("rr"), sm("rn")
            for i in range(TT):
                last = TS(ang[:, 8 * i:8 * i + 8], C("inv_freq"), sm("posf")[:, i:i + 1], None, ALU.mult)
            L(last)
            ROUND = 12582912.0
            C1 = 6.28125
            C2 = float(np.float32(2 * np.pi - C1))
            C3 = float(np.float32(2 * np.pi - C1 - np.float64(C2)))
            for dst, turn, add in ((rr, 0.0, 0.0), (rn, 0.25, float(np.float32(np.pi / 2)))):
                t_ = sm("cos")
                L(TS(t_, ang, float(np.float32(1 / (2 * np.pi))), turn, ALU.mult, ALU.add))
                L(TS(t_, t_, ROUND, None, ALU.add))
                L(TS(t_, t_, ROUND, None, ALU.subtract))
                L(STT(out=dst, in0=t_, scalar=-C1, in1=ang, op0=ALU.mult, op1=ALU.add))
                L(STT(out=dst, in0=t_, scalar=-C2, in1=dst, op0=ALU.mult, op1=ALU.add))
                L(STT(out=dst, in0=t_, scalar=-C3, in1=dst, op0=ALU.mult, op1=ALU.add))
                L(TS(dst, dst, add, None, ALU.add))
                sig(TS(dst, dst, 3.1415925, -3.1415925, ALU.min, ALU.max), "angles")
            v.wait_ge(S("b_ada"), 64)
            v.wait_ge(S("ada_done"), 4)
            sig(TV(modrow[:, 0, :], modrow[:, 0, :], PS[:, 7, :], ALU.add), "modrow")
            v.wait_ge(S("mod1"), 4)
            v.wait_ge(S("gain"), 16)
            CP(SH1, PS[:, 0:2, :].rearrange("p b n -> p (b n)"))
            L(STT(out=A1, in0=PS[:, 2:4, :].rearrange("p b n -> p (b n)"), scalar=1.0, in1=gain, op0=ALU.add, op1=ALU.mult))

            def modulated(name, a, sh):
                for i in range(TT):
                    last = STT(out=h[:, i, :], in0=x[:, i, :], scalar=sm("rs")[:, i:i + 1], in1=a, op0=ALU.mult, op1=ALU.mult)
                L(last)
                for i in range(TT):
                    sig(TV(h[:, i, :], h[:, i, :], sh, ALU.add), "h")

            def hT_copy_dve(name):
                v.wait_ge(S("h_transposed"), 2 * int(name[1]) - 1)
                sig(CP(hT[:, 0:4, :].rearrange("p k t -> p (k t)"), PS[:, 0:2, :].rearrange("p b n -> p (b n)")),
                    "hT_V")

            modulated("n1", A1, SH1)
            hT_copy_dve("n1")
            flat = "p b n -> p (b n)"
            q, k, b, tmp = (at(A1MAP, n) for n in ("q", "k", "b", "tmp"))
            o = begin(0)
            v.wait_ge(S("sig_q"), 1)
            sig(TV(q, o.rearrange(flat), tmp, ALU.mult), "big_free_V")
            v.wait_ge(S("big_free_A"), 1)
            for i in range(HH):
                c = slice(256 * i, 256 * (i + 1))
                sig(TS(k[:, c], b[:, c], sm("one_lb")[:, i:i + 1], sm("lb")[:, i:i + 1], ALU.mult, ALU.add), "forget")
            reset = at(A1MAP, "reset")
            L(V.memset(reset, 1.0))
            L(V.memset(reset.rearrange("p (g j) -> p g j", g=16)[:, :, 0:1], 0.0))
            v.wait_ge(S("log_f"), 1)
            TS(k, k, -1.0, 1.0, ALU.mult, ALU.add)
            sig(V.tensor_tensor_scan(b, reset, b, 0.0, ALU.mult, ALU.add), "b_ready")
            bg = b.rearrange("p (g j) -> p g j", j=SUB)
            bc_ = b.rearrange("p (g j) -> p g j", j=CH)
            kc = k.rearrange("p (g j) -> p g j", j=CH)
            decay = sm("decay")
            CP(decay, bc_[:, :, CH - 1])
            qt = at(A1MAP, "qt")
            L(TV(qt.rearrange("p (g j) -> p g j", j=SUB), bg, bg[:, :, SUB // 2 - 1:SUB // 2].broadcast_to([P, 64, SUB]),
                 ALU.subtract))
            sig(TS(qt, qt, EXP_CAP, None, ALU.min), "hg_arg")
            for i in range(4):
                n = SUB * (i + 1)
                mid = SUB * i + SUB // 2 - 1
                L(TV(kt_view(i), bc_[:, :, mid:mid + 1].broadcast_to([P, 16, n]), bc_[:, :, 0:n], ALU.subtract))
                sig(TS(kt_view(i), kt_view(i), EXP_CAP, None, ALU.min), "hg_arg")
            v.wait_ge(S("hg_expb"), 1)
            sig(TV(bc_, bc_last(decay, CH), bc_, ALU.subtract), "hg_arg")
            v.wait_ge(S("sig_g"), 1)
            gs = at(A1MAP, "gs")
            o = begin(3)
            sig(TV(gs, o.rearrange(flat), gs, ALU.mult), "big_free_V")
            v.wait_ge(S("smalls"), NSMALLS)
            L(TV(gs.rearrange("p (g v) -> p g v", g=8), gs.rearrange("p (g v) -> p g v", g=8), bc_mid(sm("hg_gain"), 8),
                 ALU.mult))
            v.wait_ge(S("hg_exp"), 1)
            L(TV(qt, qt, q, ALU.mult))
            L(TV(q, q, tmp, ALU.mult))
            for i in range(4):
                v.wait_ge(S("hg_exp"), i + 2)
                last = TV(kt_view(i), kt_view(i), kc[:, :, 0:SUB * (i + 1)], ALU.mult)
            sig(last, "hg_scores_in")
            v.wait_ge(S("hg_exp"), 6)
            sig(TV(b, b, k, ALU.mult), "hg_kd")
            qk = at(A1MAP, "qk").rearrange("p (t g d) -> p t g d", t=TT, d=HD)
            vv = at(A1MAP, "vv").rearrange("p (t d) -> p t d", t=TT)
            o = begin(4)
            sig(CP(qk[:, :, 0:8, :], o.rearrange("p t (g d) -> p t g d", d=HD)), "big_free_V")
            o = begin(5)
            for i in range(TT):
                for c in range(2):
                    CP(qk[:, i, 8 + c:12:2, :], o[:, i, 0:128].rearrange("p (g d) -> p g d", d=HD))
            sig(CP(vv, o[:, :, 128:256]), "big_free_V")

            def head_norm(qk, nh, sq, gains, name):
                w = TT * nh
                flat3 = qk.rearrange("p t g d -> p (t g) d")
                s3 = sq.rearrange("p (g d) -> p g d", d=HD)
                L(TV(s3, flat3, flat3, ALU.mult))
                L(V.reduce_sum(sm("ssa", w), s3, axis=AX))
                sig(TS(sm("ssa", w), sm("ssa", w), 1.0 / HD, EPS, ALU.mult, ALU.add), f"{name}_ms")
                v.wait_ge(S(f"{name}_std"), 1)
                L(V.reciprocal(sm("rsa", w), sm("rsa", w)))
                L(TV(flat3, flat3, bc_last(sm("rsa", w), HD), ALU.mult))
                for i in range(TT):
                    for a, n, g_ in gains:
                        last = TV(qk[:, i, a:a + n, :], qk[:, i, a:a + n, :], bc_mid(sm(g_), n), ALU.mult)
                return last

            L(head_norm(qk, 12, at(A1MAP, "qkT"), [(0, 8, "q_gain"), (8, 4, "k_gain")], "att"))
            v.wait_ge(S("sincos"), 2)
            rt_ = at(A1MAP, "rt")
            for i in range(TT):
                x1, x2 = qk[:, i, :, 0:8], qk[:, i, :, 8:16]
                cs, sn = bc_mid(sm("cos")[:, 8 * i:8 * i + 8], 12), bc_mid(sm("sin")[:, 8 * i:8 * i + 8], 12)
                p4 = [rt_[:, 96 * n + 384 * i:96 * n + 96 + 384 * i].rearrange("p (g d) -> p g d", d=8) for n in range(4)]
                TV(p4[0], x1, cs, ALU.mult)
                TV(p4[1], x2, sn, ALU.mult)
                TV(p4[2], x2, cs, ALU.mult)
                L(TV(p4[3], x1, sn, ALU.mult))
                TV(x1, p4[0], p4[1], ALU.subtract)
                last = TV(x2, p4[2], p4[3], ALU.add)
            sig(last, "att_qk")
            st = at(A1MAP, "st")
            st8 = st.rearrange("p (g i) -> p g i", g=8)
            L(V.memset(st, 0.0))
            o = aux_bank().rearrange("p (g i) -> p g i", g=8)
            for par in range(2):
                for i in range(4):
                    q_, c = slice(64 * par, 64 * par + SUB * (i + 1)), slice(SUB * i, SUB * (i + 1))
                    mk = C("chunk_causal")[q_, c]
                    last = TV(st8[q_, :, c], o[q_, :, c], bc_mid(mk, 8), ALU.mult)
            last.then_inc(S("hg_st"), 1)
            v.wait_ge(S("hg_st"), 1)
            sig(V.memset(sm("ang"), 0.0), "aux_free")
            kdT = at(A1MAP, "kdT")
            for i in range(TT):
                o = aux_bank()
                last = CP(kdT[:, 512 * i:512 * (i + 1)], o)
                sig(last, "hg_kdT")
                sig(V.memset(sm("ang"), 0.0), "aux_free")
            states = at(A1MAP, "state").rearrange("p (c h v) -> p c h v", c=3, h=HH)
            for c in range(3):
                o = aux_bank().rearrange("p (h v) -> p h v", h=HH)
                if c == 0:
                    sig(CP(states[:, 0], o), "hg_state")
                else:
                    for hh in range(HH):
                        last = STT(out=states[:, c, hh, :], in0=states[:, c - 1, hh, :], scalar=decay[:, 4 * hh + c:4 * hh + c + 1],
                                   in1=o[:, hh, :], op0=ALU.mult, op1=ALU.add)
                    sig(last, "hg_state")
                sig(V.memset(sm("ang"), 0.0), "aux_free")
            ho = at(A1MAP, "o")
            for i in range(TT):
                sig(CP(ho[:, 512 * i:512 * (i + 1)], aux_bank()), "aux_free")
            o8 = ho.rearrange("p (g v) -> p g v", g=8)
            sq8 = at(A1MAP, "qt").rearrange("p (g v) -> p g v", g=8)
            L(TV(sq8, o8, o8, ALU.mult))
            L(V.reduce_sum(sm("ssh"), sq8, axis=AX))
            sig(TS(sm("ssh"), sm("ssh"), 1.0 / 128, EPS, ALU.mult, ALU.add), "hgo_ms")
            v.wait_ge(S("hgo_std"), 1)
            L(V.reciprocal(sm("rsh"), sm("rsh")))
            for g in range(8):
                c = slice(128 * g, 128 * (g + 1))
                last = STT(out=ho[:, c], in0=ho[:, c], scalar=sm("rsh")[:, g:g + 1], in1=gs[:, c], op0=ALU.mult, op1=ALU.mult)
            sig(last, "hg_out")
            for r in range(2):
                sig(CP(at(A1MAP, "oT", 512 * r, 512), aux_bank()), "hg_oT")
                sig(V.memset(sm("ang"), 0.0), "aux_free")
            for r in range(3):
                sig(CP(at(A1MAP, "qkT", 512 * r, 512), aux_bank()), "att_qkT")
                sig(V.memset(sm("ang"), 0.0), "aux_free")
            s = at(A1MAP, "s").rearrange("p (h n) -> p h n", h=AH)
            wb = C("win_bias")
            for r in range(2):
                o = aux_bank().rearrange("p (h n) -> p h n", h=4)
                sig(STT(out=s[:, r:8:2, 0:P], in0=o, scalar=HD ** -0.5, in1=bc_mid(wb[:, P:256], 4),
                        op0=ALU.mult, op1=ALU.add), "aux_free")
            for r in range(4):
                o = aux_bank().rearrange("p (h n) -> p h n", h=2)
                h0 = 4 * (r // 2) + r % 2
                sig(STT(out=s[:, h0:h0 + 3:2, P:384], in0=o, scalar=HD ** -0.5, in1=bc_mid(wb, 2),
                        op0=ALU.mult, op1=ALU.add), "aux_free")
            m_ = sm("m")
            V.reduce_max(m_[:, 0:8], s[:, :, 0:P], axis=AX)
            L(V.reduce_max(m_[:, 8:16], s[:, :, P:384], axis=AX))
            m2, sink2 = m_.rearrange("p (a h) -> p a h", a=2), bc_mid(sm("sink"), 2)
            L(TV(m2, m2, sink2, ALU.max))
            L(TV(sm("es").rearrange("p (a h) -> p a h", a=2), sink2, m2, ALU.subtract))
            sig(TS(sm("nm"), m_, -1.0, None, ALU.mult), "att_nm")
            v.wait_ge(S("att_exp"), 17)
            L(TV(sm("den"), sm("den"), sm("es"), ALU.add))
            L(V.reciprocal(sm("den"), sm("den")))
            TV(s[:, :, 0:P], s[:, :, 0:P], bc_last(sm("den")[:, 0:8], P), ALU.mult)
            sig(TV(s[:, :, P:384], s[:, :, P:384], bc_last(sm("den")[:, 8:16], 256), ALU.mult), "att_p")
            pT0 = at(A1MAP, "pT0").rearrange("p (h q) -> p h q", h=AH)
            pT1 = at(A1MAP, "pT1").rearrange("p (h q) -> p h q", h=AH)
            for b_ in range(3):
                for r in range(2):
                    dst = pT1[:, 4 * r:4 * r + 4, :] if b_ == 2 else pT0[:, 4 * r:4 * r + 4, b_ * P:(b_ + 1) * P]
                    o = aux_bank().rearrange("p (h n) -> p h n", h=4)
                    sig(CP(dst, o), "att_pT")
                    sig(V.memset(sm("ang"), 0.0), "aux_free")
            for r in range(2):
                sig(CP(at(A1MAP, "attT", 512 * r, 512), aux_bank()), "att_oT")
                sig(V.memset(sm("ang"), 0.0), "aux_free")
            sig(V.memset(sm("ang"), 0.0), "gain_free")
            sig(V.memset(sm("ang"), 0.0), "m1_brow_free")
            v.wait_ge(S("ada_done"), 12)
            sig(TV(modrow[:, 1, :], modrow[:, 1, :], PS[:, 6, :], ALU.add), "modrow")
            sig(TV(modrow[:, 2, :], modrow[:, 2, :], PS[:, 7, :], ALU.add), "modrow")
            for j in range(2):
                sig(CP(G1[:, 512 * j:512 * (j + 1)], aux_bank()), "aux_free")

            def merge(r0, m):
                g = at(m, "gates")
                for n in range(4):
                    c = slice(1024 * n, 1024 * (n + 1))
                    o = begin(r0 + n)
                    if n < 2:
                        sig(TV(g[:, c], g[:, c], o.rearrange(flat), ALU.mult), "big_free_V")
                    else:
                        sig(TV(g[:, c], g[:, c], o.rearrange(flat), ALU.mult), "big_free_V")
                sig(TV(g[:, 0:2048], g[:, 0:2048], g[:, 2048:4096], ALU.add), "merged")

            v.wait_ge(S("big_free_A"), 6)
            merge(10, A1MAP)
            for j in range(2):
                sig(CP(SH2[:, 512 * j:512 * (j + 1)], aux_bank()), "aux_free")
            v.wait_ge(S("gain"), 32)
            for j in range(2):
                c = slice(512 * j, 512 * (j + 1))
                sig(STT(out=A2[:, c], in0=aux_bank(), scalar=1.0, in1=gain[:, c], op0=ALU.add, op1=ALU.mult), "aux_free")
            for j in range(2):
                sig(CP(G2[:, 512 * j:512 * (j + 1)], aux_bank()), "aux_free")
            sig(V.memset(sm("ang"), 0.0), "gain_free")
            xt = at(A1MAP, "v")
            for j in range(2):
                c = slice(512 * j, 512 * (j + 1))
                o = begin(14 + j)
                sig(TV(xt.rearrange("p (t n) -> p t n", t=TT), o, bc_mid(G1[:, c], TT), ALU.mult), "big_free_V")
                L(TV(x[:, :, c], x[:, :, c], xt.rearrange("p (t n) -> p t n", t=TT), ALU.add))
            def rms(name):
                sig(V.memset(sm("ang"), 0.0), "x_ready")
                v.wait_ge(S("squares"), 2 * int(name[1]))
                sig(TS(sm("ss"), sm("ss"), 1.0 / D, EPS, ALU.mult, ALU.add), "mean_square")
                v.wait_ge(S("rms"), int(name[1]))
                L(V.reciprocal(sm("rs"), sm("rs")))

            rms("n2")
            modulated("n2", A2, SH2)
            hT_copy_dve("n2")
            iota32 = C("iota")[:, 0:NE]
            L(V.memset(rt, 0.0))
            L(V.memset(SL, 512.0))
            v.wait_ge(S("logits"), 1)
            for i in range(TT):
                L(TV(LG[:, i, 0:NE], PS[:, 4, 64 * i:64 * i + NE], sm("b_r1"), ALU.add))
                L(V.max(V8[:, i, :], LG[:, i, 0:NE]))
                L(V.max_index(idx[:, i, :], V8[:, i, :], LG[:, i, 0:NE]))
                CP(IDF[:, i, :], idx[:, i, :])
                sig(TS(EX[:, i, :], V8[:, i, :], V8[:, i, 0:1], None, ALU.subtract), "r1_arg")
            v.wait_ge(S("r1_exp"), TT)
            L(V.reciprocal(ESUM, ESUM))
            for i in range(TT):
                L(TS(EX[:, i, 0:4], EX[:, i, 0:4], ESUM[:, i:i + 1], None, ALU.mult))
                for kk in range(4):
                    TS(TMPE[:, i, :], iota32, IDF[:, i, kk:kk + 1], EX[:, i, kk:kk + 1], ALU.is_equal, ALU.mult)
                    L(STT(out=M[:, i, :], in0=iota32, scalar=IDF[:, i, kk:kk + 1], in1=M[:, i, :], op0=ALU.is_equal,
                          op1=ALU.add))
                    L(TV(G[:, i, 0:NE], G[:, i, 0:NE], TMPE[:, i, :], ALU.add))

            def slot_numbers(name, f, m):
                sig(V.memset(sm("ang"), 0.0), "mask")
                v.wait_ge(S("positions"), int(name[1]) // 2)
                for i in range(TT):
                    L(STT(out=SL[:, i, 0:NE], in0=PS[:, 5, 64 * i:64 * i + NE], scalar=-512.0, in1=M[:, i, :],
                          op0=ALU.add, op1=ALU.mult))
                    L(TS(SL[:, i, 0:NE], SL[:, i, 0:NE], 512.0, None, ALU.add))
                L(V.reduce_max(CMAX, PS[:, 5, 128:160], axis=AX))
                sig(CP(flag[:, f:f + 1], CMAX), f"{m}_flag")

            slot_numbers("n2", 0, "m1")
            v.wait_ge(S("gT"), 1)
            sig(CP(GT, PS[0:NE, 6, 0:256]), "gT_copy")
            v.wait_ge(S("bias_rows"), 1)
            sig(CP(acc, PS[:, 0:4, :].rearrange(flat)), "m1_acc")
            iota0 = C("iota")[:, 0:CAP]
            moe1_select("m1", 0, iota0)
            with v.Fori(0, NE) as e:
                moe1_dve(v, "m1", e, e, e, iota0)
            v.wait_ge(S("m1_acc"), NE + 1)
            more = v.value_load(flag[0:1, 0:1], min_val=0, max_val=SEQ)
            with v.If(more > CAP):
                with v.Fori(0, EXTRA) as p:
                    iop = C("iota")[:, bass.ds(CAP * p + CAP, CAP)]
                    moe1_select("m1", 0, iop)
                    with v.Fori(0, NE) as e:
                        moe1_dve(v, "m1", NE * (p + 1) + e, e, (NE + 1) * (p + 1) + e, iop)
                v.wait_ge(S("m1_acc"), NE * (EXTRA + 1) + 1)
            for i in range(TT):
                c = slice(D * i, D * (i + 1))
                L(TV(acc[:, c], acc[:, c], G2, ALU.mult))
                L(TV(x[:, i, :], x[:, i, :], acc[:, c], ALU.add))
            sig(V.memset(sm("ang"), 0.0), "gain_free")

            def gained(name, g):
                for i in range(TT):
                    sig(STT(out=h[:, i, :], in0=x[:, i, :], scalar=sm("rs")[:, i:i + 1], in1=g, op0=ALU.mult, op1=ALU.mult),
                        "h")

            rms("n3")
            v.wait_ge(S("gain"), 48)
            gained("n3", gain)
            hT_copy_dve("n3")
            qk = at(A2MAP, "qk").rearrange("p (t g d) -> p t g d", t=TT, d=HD)
            for n in range(2):
                o = begin(R2 + n)
                sig(CP(qk[:, :, 8 * n:8 * n + 8, :], o.rearrange("p t (g d) -> p t g d", d=HD)), "big_free_V")
            sig(head_norm(qk, 16, at(A2MAP, "sp", 0, 2048), [(0, 8, "q_gain2"), (8, 8, "k_gain2")], "sb"), "sb_qk")
            cb, tmp2, cv = at(A2MAP, "cb"), at(A2MAP, "tmp"), at(A2MAP, "cv")
            o = begin(R2 + 3)
            sig(CP(cb, o.rearrange(flat)), "big_free_V")
            o = begin(R2 + 4)
            sig(CP(tmp2, o.rearrange(flat)), "big_free_V")
            for n in range(4):
                sig(CP(at(A2MAP, "qkT", 512 * n, 512), aux_bank()), "sb_qkT")
                sig(V.memset(sm("ang"), 0.0), "aux_free")
            cu = at(A2MAP, "cu", 0, 4 * 258).rearrange("p (m t) -> p m t", m=4)
            L(V.memset(cu[:, :, 0:2], 0.0))
            o = begin(R2 + 5)
            sig(TV(cu[:, :, 2:258], o.rearrange("p b (c t) -> p (b c) t", c=2), tmp2.rearrange("p (m t) -> p m t", m=4),
                   ALU.mult), "big_free_V")
            z = at(A2MAP, "z")
            z3 = z.rearrange("p (h n) -> p h n", h=8)
            sp_ = at(A2MAP, "sp")
            sp3 = sp_.rearrange("p (h n) -> p h n", h=8)
            before = C("before")
            for hh in range(8):
                o = aux_bank()
                sig(TS(z3[:, hh, :], o[:, 0:384], HD ** -0.5, None, ALU.mult), "aux_free")
                if hh % 4 == 3:
                    sig(V.memset(sm("ang"), 0.0), "sb_z")
            cv3 = cv.rearrange("p (m t) -> p m t", m=4)
            for m in range(4):
                w = [cols[:, 16 + 4 * j + m:17 + 4 * j + m] for j in range(3)]
                L(TS(cv3[:, m, :], cu[:, m, 0:256], w[0], None, ALU.mult))
                L(STT(out=cv3[:, m, :], in0=cu[:, m, 1:257], scalar=w[1], in1=cv3[:, m, :], op0=ALU.mult, op1=ALU.add))
                L(STT(out=cv3[:, m, :], in0=cu[:, m, 2:258], scalar=w[2], in1=cv3[:, m, :], op0=ALU.mult, op1=ALU.add))
            sig(TV(cv, cv, cb, ALU.mult), "conv")
            for g in range(2):
                c, hs = slice(1536 * g, 1536 * (g + 1)), slice(4 * g, 4 * g + 4)
                v.wait_ge(S("sb_ln"), g + 1)
                L(STT(out=sp_[:, c], in0=z[:, c], scalar=0.0, in1=sp_[:, c], op0=ALU.max, op1=ALU.add))
                TV(sp3[:, hs, 0:P], sp3[:, hs, 0:P], bc_mid(before, 4), ALU.mult)
                sig(TV(sp3[:, hs, 256:384], sp3[:, hs, 256:384], bc_mid(before, 4), ALU.mult), "sb_sp")
            for hh in range(8):
                o = aux_bank()
                sig(TV(z3[:, hh, :], z3[:, hh, :], o[:, 0:384], ALU.subtract), "aux_free")
                if hh % 4 == 3:
                    c = slice(1536 * (hh // 4), 1536 * (hh // 4 + 1))
                    sig(TS(z[:, c], z[:, c], 0.0, None, ALU.min), "sb_d")
            for g in range(2):
                hs = slice(4 * g, 4 * g + 4)
                v.wait_ge(S("sb_a"), g + 1)
                TV(z3[:, hs, 0:P], z3[:, hs, 0:P], bc_mid(before, 4), ALU.mult)
                sig(TV(z3[:, hs, 256:384], z3[:, hs, 256:384], bc_mid(before, 4), ALU.mult), "sb_w")
            for n in range(2):
                sig(CP(at(A2MAP, "attT", 512 * n, 512), aux_bank()), "sb_oT")
                sig(V.memset(sm("ang"), 0.0), "aux_free")
            v.wait_ge(S("big_free_A"), 11)
            merge(R2 + 10, A2MAP)
            for j in range(2):
                c = slice(512 * j, 512 * (j + 1))
                o = begin(R2 + 14 + j)
                sig(TV(x[:, :, c], x[:, :, c], o, ALU.add), "big_free_V")
            rms("n4")
            v.wait_ge(S("ffn_gain"), 16)
            gained("n4", at(A2MAP, "gain"))
            hT_copy_dve("n4")
            L(V.memset(rt, 0.0))
            L(V.memset(SL, 512.0))
            L(V.memset(GL, NEG))
            v.wait_ge(S("logits"), 2)
            iota8 = C("iota")[:, 0:8]
            for i in range(TT):
                L(TV(LG[:, i, :], PS[:, 4, 64 * i:64 * i + 36], sm("b_r2"), ALU.add))
                L(CP(GL[:, i, 0:4], LG[:, i, 0:4]))
                L(V.max(GV8[:, i, :], GL[:, i, :]))
                L(V.max_index(idx[:, i, :], GV8[:, i, :], GL[:, i, :]))
                L(CP(GID[:, i, :], idx[:, i, :]))
                L(TS(GEX[:, i, 0:4], GL[:, i, 0:4], GV8[:, i, 0:1], None, ALU.subtract))
                L(TS(OH[:, i, :], C("iota")[:, 0:4], GID[:, i, 0:1], None, ALU.is_equal))
                for g in range(4):
                    L(STT(out=EIG[:, i, :], in0=LG[:, i, 4 + 8 * g:12 + 8 * g], scalar=OH[:, i, g:g + 1], in1=EIG[:, i, :],
                          op0=ALU.mult, op1=ALU.add))
                L(V.max(V8[:, i, :], EIG[:, i, :]))
                L(V.max_index(idx2[:, i, :], V8[:, i, :], EIG[:, i, :]))
                CP(IDF[:, i, :], idx2[:, i, :])
                sig(TS(EX[:, i, :], V8[:, i, :], V8[:, i, 0:1], None, ALU.subtract), "r2_arg")
            v.wait_ge(S("r2_exp"), 2 * TT)
            L(TV(ESUM, ESUM, GSUM, ALU.mult))
            L(V.reciprocal(ESUM, ESUM))
            for i in range(TT):
                L(TS(EX[:, i, 0:2], EX[:, i, 0:2], ESUM[:, i:i + 1], None, ALU.mult))
                for kk in range(2):
                    TS(TMPE[:, i, 0:8], iota8, IDF[:, i, kk:kk + 1], EX[:, i, kk:kk + 1], ALU.is_equal, ALU.mult)
                    L(STT(out=M8[:, i, :], in0=iota8, scalar=IDF[:, i, kk:kk + 1], in1=M8[:, i, :], op0=ALU.is_equal,
                          op1=ALU.add))
                    L(TV(W8[:, i, :], W8[:, i, :], TMPE[:, i, 0:8], ALU.add))
                for dst, src in ((G, W8), (M, M8)):
                    last = TV(dst[:, i, 0:NE].rearrange("p (g e) -> p g e", g=4), bc_mid(src[:, i, :], 4),
                              bc_last(OH[:, i, :], 8), ALU.mult)
                L(last)
            slot_numbers("n4", 1, "m2")
            sig(V.memset(acc, 0.0), "m2_acc")
            moe2_select("m2", 0, iota0)
            with v.Fori(0, NE // 4) as q:
                for j in range(2):
                    moe2_dve(v, "m2", 2 * q + j, 2 * q + j, 2 * q + j, iota0)
            v.wait_ge(S("m2_acc"), NE // 2 + 1)
            more = v.value_load(flag[0:1, 1:2], min_val=0, max_val=SEQ)
            with v.If(more > CAP):
                with v.Fori(0, EXTRA) as p:
                    iop = C("iota")[:, bass.ds(CAP * p + CAP, CAP)]
                    moe2_select("m2", 0, iop)
                    with v.Fori(0, NE // 2) as q:
                        moe2_dve(v, "m2", (NE // 2) * (p + 1) + q, q, (NE // 2 + 1) * (p + 1) + q, iop)
                v.wait_ge(S("m2_acc"), (NE // 2) * (EXTRA + 1) + 1)
            TV(x[:, :, :].rearrange("p t d -> p (t d)"), x[:, :, :].rearrange("p t d -> p (t d)"), acc, ALU.add)\
                .then_inc(S("result"), 1)


_INS = ["x", "c", "positions", "w_ada", "b_ada", "norm1_gain", "w_in", "lower_bound_logits", "hg_norm_gain", "w_hg_branch",
        "q_norm_gain", "k_norm_gain", "attn_sinks", "w_attn_branch", "w_out", "norm2_gain", "w_router", "b_router", "w_up",
        "b_up", "w_down", "b_down", "norm_mix_g_2", "w_in_2", "q_norm_g_2", "k_norm_g_2", "conv_w_2", "w_sb_branch_2",
        "w_conv_branch_2", "w_out_2", "norm_ffn_g_2", "w_router_group_2", "b_router_group_2", "w_router_expert_2",
        "b_router_expert_2", "w_gate_e_2", "w_up_e_2", "w_down_e_2"]


def kernel(**inputs):
    import concourse.bacc as _bacc
    from concourse.bass_utils import run_bass_kernel_spmd as _run

    nc = _bacc.Bacc("TRN2", target_bir_lowering=False, num_devices=1)
    arrays, t = {}, {}
    for name in _INS + ["consts"]:
        a = CONSTS if name == "consts" else np.ascontiguousarray(inputs[name])
        arrays[f"in_{name}"] = a
        t[name] = nc.dram_tensor(f"in_{name}", a.shape, mybir.dt.from_np(a.dtype), kind="ExternalInput").ap()
    out = nc.dram_tensor("out_0", (1, SEQ, D), F32, kind="ExternalOutput").ap()
    program(nc, t, out)
    r = _run(nc, [arrays], core_ids=[0])
    return r.results[0]["out_0"]
```

```python
import numpy as np
import concourse.bass as bass
from concourse import mybir
from contextlib import ExitStack

F32 = mybir.dt.float32
I32 = mybir.dt.int32
U32 = mybir.dt.uint32
ALU = mybir.AluOpType
ACT = mybir.ActivationFunctionType
AX = mybir.AxisListType.X

P = 128
SEQ, D = 256, 1024
TT, KD = SEQ // P, D // P
EPS = 1e-6
NSLOT, SLOTW = 6, 4096
CH, SUB = 64, 16
EXP_CAP = 80.0
HH, AH, KVH, HD = 4, 8, 2, 64
NE, CAP, CAP2 = 32, 64, 32
EXTRA, EXTRA2 = SEQ // CAP - 1, SEQ // CAP2 - 1
NEG = -1.0e30
C_IN, C_IN2 = 4864, 5120

CONST = {}
_cols = []


def _const(name, a):
    a = np.asarray(a, np.float32).reshape(P, -1)
    CONST[name] = (sum(c.shape[1] for c in _cols), a.shape[1])
    _cols.append(a)


_p = np.arange(P)[:, None]
_f = np.arange(P)[None, :]
_const("ident", _p == _f)
_const("before", _p < _f)
_const("from_here", _p >= _f)
_const("ones", np.ones((P, P)))
_const("win_bias", np.concatenate([np.where(_f > _p, 0.0, NEG), np.where(_f <= _p, 0.0, NEG)], 1))
_const("chunk_causal", (_p % CH) <= np.arange(CH)[None, :])
_const("iota", np.broadcast_to(np.arange(SEQ)[None, :], (P, SEQ)))
_const("inv_freq", np.broadcast_to((np.float32(500000.0) ** (-np.arange(8, dtype=np.float32) / 8))[None, :], (P, 8)))
CONSTS = np.concatenate(_cols, axis=1)
NCONST = CONSTS.shape[1]

SMALL = {}
_at = 0
for _n, _w in [("w_r1", KD * NE), ("w_r2", KD * 36), ("hg_gain", 128), ("q_gain", 64), ("k_gain", 64), ("sink", 8),
               ("b_r1", NE), ("b_r2", 36), ("q_gain2", 64), ("k_gain2", 64), ("cols", 36), ("shiftT", 8), ("scaleT", 8), ("cond", 8), ("lb", 4),
               ("one_lb", 4), ("lbd", 4), ("posf", 2), ("ss", 4), ("rs", 2), ("ang", 16), ("rn", 16), ("rr", 16), ("cos", 16),
               ("sin", 16), ("decay", 16), ("ssh", 8), ("rsh", 8), ("ssa", 32), ("rsa", 32), ("m", 16), ("nm", 16),
               ("es", 16), ("den", 16), ("cond32", KD * 32)]:
    SMALL[_n] = (_at, _w)
    _at += _w
NSMALL = _at

KB = 256
ARENA = 78.125
A1MAP = dict(h=(0, 8), acc=(8, 8), g1=(16, 4), a2=(20, 4), sh2=(24, 4), g2=(28, 4), gain=(32, 4),
             q=(0, 4), k=(4, 4), b=(8, 4), v=(12, 4), tmp=(16, 4), reset=(16, 4), qt=(20, 4), oT=(20, 4), vv=(24, 1),
             st=(24, 2), kt=(26, 10), kdT=(26, 4), o=(30, 4), qk=(36, 6), pT1=(36, 4), gates=(42, 16), s=(58, 12),
             attT=(58, 4), gs=(62, 4), rt=(66, 3), qkT=(70, 6), pT0=(70, 8), state=(70, 6))
MMAP = dict(h=(0, 8), acc=(8, 8), gain=(32, 4), xg=(42, 4), glu=(46, 2), lin=(48, 2), sg=(50, 2), act=(52, 2), aT=(54, 2),
            ye=(56, 4), swT=(60, 1), selS=(61, 1), selW=(62, 1), brow=(63, 8), bdown=(71, 4), rt=(75, 3))
A2MAP = dict(h=(0, 8), qkT=(0, 8), v=(8, 4), attT=(12, 4), qk=(16, 8), z=(16, 12), sp=(28, 12), gates=(42, 16),
             tmp=(58, 4), cu=(62, 4.125), cb=(66.125, 4), cv=(70.125, 4), gain=(16, 4))

PRE = ([("ada", 0, i) for i in range(4)] + [("in", 0), ("ada", 1, 0), ("in", 1), ("ada", 1, 1), ("in", 2), ("ada", 1, 2),
       ("in", 3), ("ada", 1, 3), ("in", 4), ("ada", 2, 0), ("in", 5), ("ada", 2, 1), ("in", 6), ("ada", 2, 2), ("in", 7),
       ("ada", 2, 3), ("in", 8), ("in", 9), ("at",), ("hg",), ("out", 0), ("out", 1)])
MOE1 = len(PRE)
MID0 = MOE1 + 6 * NE
MID = [("in", i) for i in range(10)] + [("sb",), ("cv",), ("out", 0), ("out", 1)]
MOE2 = MID0 + len(MID)
IN_COLS = [(2048, 512), (2560, 256), (512, 512), (0, 512), (1024, 512), (1536, 512), (3840, 512), (4352, 512),
           (2816, 512), (3328, 512)]
IN_COLS2 = [(512 * n, 512) for n in (0, 1, 2, 4, 5, 3, 6, 7, 8, 9)]


def program(nc, t, out):
    ctx = ExitStack()
    with ctx:
        def sb(name, shape, dt=F32):
            return ctx.enter_context(nc.sbuf_tensor(name, shape, dt))

        sems = {}

        def S(name):
            if name not in sems:
                sems[name] = ctx.enter_context(nc.semaphore(name))
            return sems[name]

        ring = sb("ring", [P, NSLOT, SLOTW])
        x = sb("x", [P, TT, D])
        hT = sb("hT", [P, KD, SEQ])
        modrow = sb("modrow", [P, 3, 512])
        consts = sb("consts", [P, NCONST])
        small = sb("small", [P, NSMALL])
        rows = sb("rows", [66, P])
        pos = sb("pos", [66, P], I32)
        idx = sb("idx", [P, TT, 8], U32)
        idx2 = sb("idx2", [P, TT, 8], U32)
        flag = sb("flag", [P, 2], I32)
        arena = sb("arena", [P, int(ARENA * KB)])
        PS = ctx.enter_context(nc.psum_tensor("PS", [P, 8, 512], F32))

        def C(name):
            a, n = CONST[name]
            return consts[:, a:a + n]

        def sm(name, n=None):
            a, w = SMALL[name]
            return small[:, a:a + (n or w)]

        def at(m, name, lo=0, n=None):
            a, w = m[name]
            a = int(a * KB) + lo
            return arena[:, a:a + (n if n else int(w * KB) - lo)]

        ident = C("ident")
        slots = [ring[:, i, :] for i in range(NSLOT)]

        h = at(A1MAP, "h").rearrange("p (t d) -> p t d", t=TT)
        acc = at(A1MAP, "acc")
        acc4 = acc.rearrange("p (t c n) -> p (t c) n", t=TT, c=2)
        gain = at(A1MAP, "gain")
        xres = x[:, :, :]
        A1 = at(A1MAP, "a2")
        SH1 = at(A1MAP, "sh2")
        G1 = at(A1MAP, "g1")
        A2 = at(A1MAP, "a2")
        SH2 = at(A1MAP, "sh2")
        G2 = at(A1MAP, "g2")

        def unit_load(eng, u, desc):
            s = u % NSLOT
            kind = desc[0]
            blk2 = u >= MID0
            if kind == "ada":
                _, b, kp = desc
                dst = slots[s].rearrange("p (k n) -> p k n", k=2)
                src = t["w_ada"][0, kp * 256:(kp + 1) * 256, b * 2048:(b + 1) * 2048].rearrange("(k p) n -> p k n", p=P)
            elif kind == "in":
                w = t["w_in_2"] if blk2 else t["w_in"]
                c0, cn = (IN_COLS2 if blk2 else IN_COLS)[desc[1]]
                dst = slots[s][:, 0:KD * cn].rearrange("p (k n) -> p k n", k=KD)
                src = w[0, :, c0:c0 + cn].rearrange("(k p) n -> p k n", p=P)
            elif kind in ("hg", "at", "sb", "cv"):
                w = t[{"hg": "w_hg_branch", "at": "w_attn_branch", "sb": "w_sb_branch_2", "cv": "w_conv_branch_2"}[kind]]
                dst = slots[s].rearrange("p (k n) -> p k n", k=4)
                src = w[0].rearrange("(k p) n -> p k n", p=P)
            else:
                w = t["w_out_2"] if blk2 else t["w_out"]
                dst = slots[s].rearrange("p (k n) -> p k n", k=KD)
                src = w[0, :, desc[1] * 512:(desc[1] + 1) * 512].rearrange("(k p) n -> p k n", p=P)
            eng.dma_start(dst, src).then_inc(S(f"loaded{s}"), 16)

        def loaded(u):
            return S(f"loaded{u % NSLOT}"), 16 * (u // NSLOT + 1)

        def big_rounds():
            out_ = []
            for base, units in ((0, PRE), (MID0, MID)):
                for n, d in enumerate(units):
                    if d[0] in ("in", "out"):
                        out_.append((base + n, d, 0, True))
                    elif d[0] != "ada":
                        out_ += [(base + n, d, 0, False), (base + n, d, 1, True)]
            return out_

        ROUNDS = big_rounds()
        R2 = sum(1 for r in ROUNDS if r[0] < MID0)
        ADA = [n for n, d in enumerate(PRE) if d[0] == "ada"]

        def unit_free(u):
            if u < MOE1 and PRE[u][0] == "ada":
                return S("ada_done"), ADA.index(u) + 1
            if MOE1 <= u < MID0:
                i = (u - MOE1) % 6
                e = (u - MOE1) // 6
                return (S("m1_up_done"), 4 * e + i + 1) if i < 4 else (S("m1_down_done"), 2 * e + i - 3)
            return S("big_done"), [n for n, r in enumerate(ROUNDS) if r[0] == u and r[3]][0] + 1

        EVAC = "VVAVAV" + "AAAA" + "VVVV" + "VV" + "VVA" + "VVV" + "AAAA" + "VVVV" + "VV"
        assert len(EVAC) == len(ROUNDS)

        def round_free(r):
            e = EVAC[r]
            return S(f"big_free_{e}"), EVAC[:r + 1].count(e)

        def wait(eng, sv):
            eng.wait_ge(sv[0], sv[1])

        block = ctx.enter_context(nc.Block())

        w_up_u = t["w_up"][0].rearrange("e (i k p) n -> e i p k n", p=P, k=2)
        w_dn_u = t["w_down"][0].rearrange("e (i k p) n -> e i p k n", p=P, k=4)

        def moe1_src(e, i):
            w = w_up_u if i < 4 else w_dn_u
            j = i if i < 4 else i - 4
            return w[bass.ds(e, 1), j, :, :, :].rearrange("o p k n -> p (o k) n")

        def moe1_dst(i):
            return slots[(MOE1 + i) % NSLOT].rearrange("p (k n) -> p k n", k=2 if i < 4 else 4)

        def moe2_src(quad, i):
            w = t[("w_gate_e_2", "w_up_e_2", "w_down_e_2")[i // 2]][0]
            return w[bass.ds(4 * quad + 2 * (i % 2), 2), :, :].rearrange("o (k p) n -> p (o k) n", p=P)

        def moe2_dst(i):
            return slots[(MOE2 + i) % NSLOT].rearrange("p (k n) -> p k n", k=16 if i < 4 else 4)

        brow = at(MMAP, "brow")[0:1, 0:2048]


        def banks(r):
            return slice(2 * (r % 2), 2 * (r % 2) + 2)

        def kt_view(i):
            lo = 8 * SUB * i * (i + 1)
            return at(A1MAP, "kt", lo, 256 * (i + 1)).rearrange("p (g j) -> p g j", g=16)

        HG_EXPS = [at(A1MAP, "qt")] + [at(A1MAP, "kt", 8 * SUB * i * (i + 1), 256 * (i + 1)) for i in range(4)] \
            + [at(A1MAP, "b"), sm("decay")]

        rt = at(MMAP, "rt")
        glu_ = at(MMAP, "glu")
        _o = [0]

        def rt_part(n, k=None):
            a = _o[0]
            _o[0] += n * (k or 1)
            return rt[:, a:a + n] if k is None else rt[:, a:a + n * k].rearrange("p (t e) -> p t e", t=n)

        G, SL = rt_part(TT, NE + 4), rt_part(TT, NE + 4)
        M, LG = rt_part(TT, NE), rt_part(TT, 36)
        V8, IDF, EX, GV8, GID, GEX, GL, EIG = (rt_part(TT, 8) for _ in range(8))
        W8, M8, OH = rt_part(TT, 8), rt_part(TT, 8), rt_part(TT, 4)
        ESUM, GSUM, CMAX = rt_part(2), rt_part(2), rt_part(2)
        EQ = rt_part(8 * NE)
        assert _o[0] <= 3 * KB
        GT = glu_[0:NE, 0:256]

        xg1 = at(MMAP, "xg", 0, 512)
        xg2 = at(MMAP, "xg", 0, 1024)
        glu, lin, sg, actb, aT = (at(MMAP, n) for n in ("glu", "lin", "sg", "act", "aT"))
        ye = at(MMAP, "ye")
        swT = at(MMAP, "swT")
        selS = at(MMAP, "selS")
        selW = at(MMAP, "selW")

        def gate_sig(act, r, n, m):
            act.wait_ge(S("big_done"), r + 1)
            nc.scalar.activation(at(m, "gates", 1024 * n, 1024), PS[:, banks(r), :], ACT.Sigmoid)\
                .then_inc(S("big_free_A"), 1)

        def rms_sums(act, n):
            k = int(n[1])
            for i in range(2):
                act.wait_ge(S("x_ready"), 2 * (k - 2) + i + 1)
                if k == 3:
                    nc.scalar.activation(hT[:, 4 * i:4 * i + 4, :], x[:, i, :].rearrange("p (k n) -> p k n", k=4),
                                         ACT.Square, accum_out=sm("ss")[:, i:i + 1]).then_inc(S("squares"), 1)
                else:
                    for tile in range(TT):
                        a = 4 * i + 2 * tile
                        nc.scalar.activation(hT[:, a:a + 2, :],
                                             x[:, tile, 512 * i:512 * (i + 1)].rearrange("p (k n) -> p k n", k=2),
                                             ACT.Square, accum_out=sm("ss")[:, 2 * i + tile:2 * i + tile + 1])\
                            .then_inc(S("squares"), 1)
            act.wait_ge(S("mean_square"), k)
            nc.scalar.sqrt(sm("rs"), sm("ss")[:, 0:2]).then_inc(S("rms"), 1)

        def hT_copy_act(act, n):
            act.wait_ge(S("h_transposed"), 2 * int(n[1]))
            nc.scalar.activation(hT[:, :, P:256], PS[:, 2:4, :].rearrange("p b (k n) -> p (b k) n", n=P), ACT.Copy)\
                .then_inc(S("hT_A"), 1)

        def moe1_act_gather(act, X, g):
            act.wait_ge(S(f"{X}_gath_done"), g + 1)
            nc.scalar.activation(xg1, PS[:, 0, :], ACT.Copy).then_inc(S(f"{X}_xg"), 1)

        def moe1_act(act, X, it, g):
            act.wait_ge(S(f"{X}_glu"), it + 1)
            nc.scalar.activation(sg, glu, ACT.Sigmoid, scale=1.702).then_inc(S(f"{X}_sg"), 1)
            moe1_act_gather(act, X, g + 1)
            act.wait_ge(S(f"{X}_down_done"), 2 * it + 2)
            nc.scalar.activation(ye[:, 0:512], PS[:, 1, :], ACT.Copy).then_inc(S(f"{X}_ye"), 1)

        def moe2_act_gather(act, X, g):
            act.wait_ge(S(f"{X}_gath_done"), g + 1)
            nc.scalar.activation(xg2, PS[:, 0:2, :], ACT.Copy).then_inc(S(f"{X}_xg"), 1)

        def moe2_act(act, X, it, g):
            act.wait_ge(S(f"{X}_gu_done"), 2 * it + 1)
            nc.scalar.activation(sg[:, 0:256], PS[:, 2, 0:256], ACT.Sigmoid).then_inc(S(f"{X}_sg"), 1)
            moe2_act_gather(act, X, g + 1)
            act.wait_ge(S(f"{X}_down_done"), it + 1)
            nc.scalar.activation(ye, PS[:, 0:2, :], ACT.Copy).then_inc(S(f"{X}_ye"), 1)

        def mm(o, w, m, first, last):
            return nc.tensor.matmul(o, w, m, start=first, stop=last)

        def transpose_h(pe, n):
            for i in range(TT):
                pe.wait_ge(S("h"), 2 * (int(n[1]) - 1) + i + 1)
                for k in range(KD):
                    c = (k % 4) * P
                    last = nc.tensor.transpose(PS[:, 2 * i + k // 4, c:c + P], h[:, i, k * P:(k + 1) * P], ident)
                last.then_inc(S("h_transposed"), 1)

        def router_mm(pe, n, w, ne):
            for i in range(TT):
                pe.wait_ge(S("hT_A" if i else "hT_V"), int(n[1]))
                for k in range(KD):
                    last = mm(PS[:, 4, 64 * i:64 * i + ne], hT[:, k, i * P:(i + 1) * P], w[:, k, :], k == 0, k == KD - 1)
            last.then_inc(S("logits"), 1)

        def positions_mm(pe, n):
            pe.wait_ge(S("mask"), int(n[1]) // 2)
            mm(PS[:, 5, 0:32], C("before"), M[:, 0, :], True, True)
            mm(PS[:, 5, 64:96], C("ones"), M[:, 0, :], True, False)
            mm(PS[:, 5, 64:96], C("before"), M[:, 1, :], False, True)
            mm(PS[:, 5, 128:160], C("ones"), M[:, 0, :], True, False)
            mm(PS[:, 5, 128:160], C("ones"), M[:, 1, :], False, True).then_inc(S("positions"), 1)

        def moe1_gather(pe, X, g):
            pe.wait_ge(S(f"{X}_sel"), g + 1)
            for k in range(KD):
                for i in range(TT):
                    last = mm(PS[:, 0, k * CAP:(k + 1) * CAP], h[:, i, k * P:(k + 1) * P],
                              selS[:, i * CAP:(i + 1) * CAP], i == 0, i == TT - 1)
            last.then_inc(S(f"{X}_gath_done"), 1)

        def moe1_pe(pe, X, it, g, arrived):
            pe.wait_ge(S(f"{X}_sel"), g + 1)
            pe.wait_ge(S(f"{X}_xg"), g + 1)
            for i in range(TT):
                last = nc.tensor.transpose(PS[:, 0, i * P:(i + 1) * P], selW[:, i * P:(i + 1) * P], ident)
            last.then_inc(S(f"{X}_swt_done"), 1)
            arrived(pe, "bias")
            for b in range(2):
                for half in range(2):
                    c = half * 1024 + b * 512
                    mm(PS[64 * half:64 * half + 64, 2 + b, :], C("ones")[0:1, 0:CAP], brow[:, c:c + 512], True, False)
            for i in range(4):
                arrived(pe, i)
                w = moe1_dst(i)
                for kk in range(2):
                    k = 2 * i + kk
                    for b in range(2):
                        for half in range(2):
                            c = half * 1024 + b * 512
                            last = mm(PS[64 * half:64 * half + 64, 2 + b, :], xg1[:, k * CAP:(k + 1) * CAP],
                                      w[:, kk, c:c + 512], False, k == KD - 1)
                last.then_inc(S(f"{X}_up_done"), 1)
            pe.wait_ge(S(f"{X}_swt"), it + 1)
            moe1_gather(pe, X, g + 1)
            pe.wait_ge(S(f"{X}_act"), it + 1)
            for i in range(4):
                last = nc.tensor.transpose(PS[:, 1, i * P:(i + 1) * P], actb[:, i * P:(i + 1) * P], ident)
            last.then_inc(S(f"{X}_at_done"), 1)
            pe.wait_ge(S(f"{X}_aT"), it + 1)
            for i in range(2):
                arrived(pe, 4 + i)
                w = moe1_dst(4 + i)
                for kk in range(4):
                    for dh in range(2):
                        c = kk * P + i * CAP
                        last = mm(PS[64 * dh:64 * dh + 64, 1, :], aT[:, c:c + CAP], w[:, kk, dh * 512:(dh + 1) * 512],
                                  i == 0 and kk == 0, i == 1 and kk == 3)
                last.then_inc(S(f"{X}_down_done"), 1)
            pe.wait_ge(S(f"{X}_ye"), it + 1)
            pe.wait_ge(S(f"{X}_acc"), it + 1)
            for i in range(TT):
                for dh in range(2):
                    q = slice(64 * dh, 64 * dh + 64)
                    last = mm(PS[:, 4 + 2 * i + dh, :], swT[q, i * P:(i + 1) * P], ye[q, 0:512], True, True)
            last.then_inc(S(f"{X}_scat_done"), 1)

        def moe2_gather(pe, X, g):
            pe.wait_ge(S(f"{X}_sel"), g + 1)
            for k in range(KD):
                for i in range(TT):
                    last = mm(PS[:, k // 4, (k % 4) * P:(k % 4 + 1) * P], h[:, i, k * P:(k + 1) * P],
                              selS[:, i * P:(i + 1) * P], i == 0, i == TT - 1)
            last.then_inc(S(f"{X}_gath_done"), 1)

        def moe2_pe(pe, X, it, g, arrived):
            pe.wait_ge(S(f"{X}_sel"), g + 1)
            pe.wait_ge(S(f"{X}_xg"), g + 1)
            for i in range(TT):
                last = nc.tensor.transpose(PS[:, 0, i * P:(i + 1) * P], selW[:, i * P:(i + 1) * P], ident)
            last.then_inc(S(f"{X}_swt_done"), 1)
            for i in range(2):
                arrived(pe, 2 * i)
                arrived(pe, 2 * i + 1)
                for k in range(KD):
                    for j in range(4):
                        q = slice(CAP2 * j, CAP2 * (j + 1))
                        last = nc.tensor.matmul(PS[q, 2 + i, 0:256], xg2[:, k * P + CAP2 * j:k * P + CAP2 * (j + 1)],
                                                moe2_dst(2 * i + j // 2)[:, 8 * (j % 2) + k, :],
                                                start=k == 0, stop=k == KD - 1, tile_position=(0, CAP2 * j))
                last.then_inc(S(f"{X}_gu_done"), 1)
            pe.wait_ge(S(f"{X}_swt"), it + 1)
            moe2_gather(pe, X, g + 1)
            pe.wait_ge(S(f"{X}_act"), it + 1)
            for i in range(2):
                last = nc.tensor.transpose(PS[:, 2, i * P:(i + 1) * P], actb[:, i * P:(i + 1) * P], ident)
            last.then_inc(S(f"{X}_at_done"), 1)
            pe.wait_ge(S(f"{X}_aT"), it + 1)
            pe.wait_ge(S(f"{X}_xg"), g + 2)
            arrived(pe, 4)
            arrived(pe, 5)
            for kk in range(2):
                for b in range(2):
                    for j in range(4):
                        q = slice(CAP2 * j, CAP2 * (j + 1))
                        last = nc.tensor.matmul(PS[q, b, :], aT[:, kk * P + CAP2 * j:kk * P + CAP2 * (j + 1)],
                                                moe2_dst(4 + j // 2)[:, 2 * (j % 2) + kk, b * 512:(b + 1) * 512],
                                                start=kk == 0, stop=kk == 1, tile_position=(0, CAP2 * j))
            last.then_inc(S(f"{X}_down_done"), 1)
            pe.wait_ge(S(f"{X}_ye"), it + 1)
            pe.wait_ge(S(f"{X}_acc"), it + 1)
            for i in range(TT):
                for b in range(2):
                    last = mm(PS[:, 4 + 2 * i + b, :], swT[:, i * P:(i + 1) * P], ye[:, b * 512:(b + 1) * 512], True, True)
            last.then_inc(S(f"{X}_scat_done"), 1)

        V = nc.vector

        def bc_mid(a, n):
            return a.rearrange("p (o w) -> p o w", o=1).broadcast_to([a.shape[0], n, a.shape[1]])

        def bc_last(a, n):
            return a.rearrange("p (g o) -> p g o", o=1).broadcast_to([a.shape[0], a.shape[1], n])

        def moe1_select(X, e, iota):
            for i in range(TT):
                V.tensor_scalar(selS[:, i * CAP:(i + 1) * CAP], iota, SL[:, i, bass.ds(e, 1)], None, ALU.is_equal)
                last = V.tensor_scalar(selW[:, i * P:(i + 1) * P].rearrange("p (a w) -> p a w", a=2), bc_mid(iota, 2),
                                       SL[:, i, bass.ds(e, 1)], G[:, i, bass.ds(e, 1)], ALU.is_equal, ALU.mult)
            last.then_inc(S(f"{X}_sel"), 1)

        def moe1_dve(v, X, it, e, g, iota):
            v.wait_ge(S(f"{X}_swt_done"), it + 1)
            V.tensor_copy(swT, PS[:, 0, 0:256]).then_inc(S(f"{X}_swt"), 1)
            v.wait_ge(S(f"{X}_gath_done"), g + 1)
            moe1_select(X, e + 1, iota)
            v.wait_ge(S(f"{X}_up_done"), 4 * it + 4)
            hu = PS[:, 2:4, :].rearrange("p b (n two) -> p b n two", two=2)
            V.tensor_scalar(glu.rearrange("p (b n) -> p b n", b=2), hu[:, :, :, 0], 7.0, None, ALU.min)\
                .then_inc(S(f"{X}_glu"), 1)
            V.tensor_scalar(lin.rearrange("p (b n) -> p b n", b=2), hu[:, :, :, 1], 7.0, -7.0, ALU.min, ALU.max)\
                .then_inc(S(f"{X}_lin"), 1)
            v.wait_ge(S(f"{X}_glu"), it + 1)
            v.wait_ge(S(f"{X}_lin"), 2 * it + 1)
            V.scalar_tensor_tensor(out=lin, in0=lin, scalar=1.0, in1=glu, op0=ALU.add, op1=ALU.mult)\
                .then_inc(S(f"{X}_lin"), 1)
            v.wait_ge(S(f"{X}_lin"), 2 * it + 2)
            v.wait_ge(S(f"{X}_sg"), it + 1)
            V.tensor_tensor(actb, lin, sg, ALU.mult).then_inc(S(f"{X}_act"), 1)
            v.wait_ge(S(f"{X}_at_done"), it + 1)
            V.tensor_copy(aT, PS[:, 1, :]).then_inc(S(f"{X}_aT"), 1)
            v.wait_ge(S(f"{X}_scat_done"), it + 1)
            v.wait_ge(S(f"{X}_acc"), it + 1)
            V.tensor_tensor(acc, acc, PS[:, 4:8, :].rearrange("p b n -> p (b n)"), ALU.add).then_inc(S(f"{X}_acc"), 1)

        def moe2_select(X, e0, iota):
            for i in range(TT):
                for j in range(4):
                    c = i * P + j * CAP2
                    col = bass.ds(e0 + j, 1)
                    V.tensor_scalar(selS[:, c:c + CAP2], iota, SL[:, i, col], None, ALU.is_equal)
                    last = V.tensor_scalar(selW[:, c:c + CAP2], iota, SL[:, i, col], G[:, i, col], ALU.is_equal, ALU.mult)
            last.then_inc(S(f"{X}_sel"), 1)

        def moe2_dve(v, X, it, quad, g, iota):
            v.wait_ge(S(f"{X}_swt_done"), it + 1)
            V.tensor_copy(swT, PS[:, 0, 0:256]).then_inc(S(f"{X}_swt"), 1)
            v.wait_ge(S(f"{X}_gath_done"), g + 1)
            moe2_select(X, 4 * quad + 4, iota)
            v.wait_ge(S(f"{X}_sg"), it + 1)
            V.tensor_tensor(glu[:, 0:256], PS[:, 2, 0:256], sg[:, 0:256], ALU.mult).then_inc(S(f"{X}_glu"), 1)
            v.wait_ge(S(f"{X}_glu"), it + 1)
            v.wait_ge(S(f"{X}_gu_done"), 2 * it + 2)
            V.tensor_tensor(actb[:, 0:256], glu[:, 0:256], PS[:, 3, 0:256], ALU.mult).then_inc(S(f"{X}_act"), 1)
            v.wait_ge(S(f"{X}_at_done"), it + 1)
            V.tensor_copy(aT[:, 0:256], PS[:, 2, 0:256]).then_inc(S(f"{X}_aT"), 1)
            v.wait_ge(S(f"{X}_scat_done"), it + 1)
            v.wait_ge(S(f"{X}_acc"), it + 1)
            V.tensor_tensor(acc, acc, PS[:, 4:8, :].rearrange("p b n -> p (b n)"), ALU.add).then_inc(S(f"{X}_acc"), 1)

        @block.sync
        def _(sp):
            sp.wait_ge(S("rows"), 64)
            sp.wait_ge(S("consts"), 16)
            for u, d in enumerate(PRE):
                if u >= NSLOT:
                    wait(sp, unit_free(u - NSLOT))
                unit_load(sp, u, d)
            for i in range(6):
                wait(sp, unit_free(MOE1 + i - NSLOT))
                sp.dma_start(moe1_dst(i), moe1_src(0, i)).then_inc(S(f"loaded{(MOE1 + i) % NSLOT}"), 16)
            sp.wait_ge(S("m1_brow_free"), 1)
            sp.dma_start(brow, t["b_up"][0, 0:1, :]).then_inc(S("m1_brow"), 16)
            with sp.Fori(1, NE) as e:
                for i in range(6):
                    if i < 4:
                        sp.wait_ge(S("m1_up_done"), 4 * e + (i - 3))
                    else:
                        sp.wait_ge(S("m1_down_done"), 2 * e + (i - 5))
                    if i == 0:
                        sp.dma_start(brow, t["b_up"][0, bass.ds(e, 1), :]).then_inc(S("m1_brow"), 16)
                    sp.dma_start(moe1_dst(i), moe1_src(e, i)).then_inc(S(f"loaded{(MOE1 + i) % NSLOT}"), 16)
            sp.wait_ge(S("m1_flag"), 1)
            more = sp.value_load(flag[0:1, 0:1], min_val=0, max_val=SEQ)
            sp.wait_ge(S("m1_down_done"), 2 * NE)
            with sp.If(more > CAP):
                with sp.Fori(0, EXTRA) as p:
                    with sp.Fori(0, NE) as e:
                        sp.wait_ge(S("m1_scat_done"), NE * (p + 1) + e)
                        sp.dma_start(brow, t["b_up"][0, bass.ds(e, 1), :]).then_inc(S("x1_loaded"), 16)
                        for i in range(6):
                            sp.dma_start(moe1_dst(i), moe1_src(e, i)).then_inc(S("x1_loaded"), 16)
                sp.wait_ge(S("m1_scat_done"), NE * (EXTRA + 1))
            for n, d in enumerate(MID):
                wait(sp, unit_free(MID0 + n - NSLOT))
                unit_load(sp, MID0 + n, d)
            for i in range(6):
                wait(sp, unit_free(MOE2 + i - NSLOT))
                sp.dma_start(moe2_dst(i), moe2_src(0, i)).then_inc(S(f"loaded{(MOE2 + i) % NSLOT}"), 16)
            with sp.Fori(1, NE // 4) as q:
                for i in range(6):
                    if i < 4:
                        sp.wait_ge(S("m2_gu_done"), 2 * q + (i // 2 - 1))
                    else:
                        sp.wait_ge(S("m2_down_done"), q)
                    sp.dma_start(moe2_dst(i), moe2_src(q, i)).then_inc(S(f"loaded{(MOE2 + i) % NSLOT}"), 16)
            sp.wait_ge(S("m2_flag"), 1)
            more = sp.value_load(flag[0:1, 1:2], min_val=0, max_val=SEQ)
            sp.wait_ge(S("m2_down_done"), NE // 4)
            with sp.If(more > CAP2):
                with sp.Fori(0, EXTRA2) as p:
                    with sp.Fori(0, NE // 4) as q:
                        sp.wait_ge(S("m2_scat_done"), (NE // 4) * (p + 1) + q)
                        for i in range(6):
                            sp.dma_start(moe2_dst(i), moe2_src(q, i)).then_inc(S("x2_loaded"), 16)
                sp.wait_ge(S("m2_scat_done"), (NE // 4) * (EXTRA2 + 1))
            sp.wait_ge(S("result"), 1)
            sp.dma_start(out[0].rearrange("(t p) d -> p t d", p=P), x[:, :, :]).then_inc(S("stored"), 16)
            sp.wait_ge(S("stored"), 16)

        @block.gpsimd
        def _(pool):
            def bc(src):
                return src.partition_broadcast(P)

            def small_load(dst, src, name):
                pool.dma_start(dst, src).then_inc(S(name), 16)

            small_load(sm("hg_gain"), bc(t["hg_norm_gain"][0]), "smalls")
            small_load(sm("q_gain"), bc(t["q_norm_gain"][0]), "smalls")
            small_load(sm("k_gain"), bc(t["k_norm_gain"][0]), "smalls")
            small_load(sm("q_gain2"), bc(t["q_norm_g_2"][0]), "smalls")
            small_load(sm("k_gain2"), bc(t["k_norm_g_2"][0]), "smalls")
            small_load(sm("sink"), bc(t["attn_sinks"][0]), "smalls")
            small_load(sm("b_r1"), bc(t["b_router"][0]), "smalls")
            small_load(sm("b_r2", 4), bc(t["b_router_group_2"][0]), "smalls")
            small_load(sm("b_r2")[:, 4:36], bc(t["b_router_expert_2"][0]), "smalls")
            small_load(sm("w_r1").rearrange("p (k n) -> p k n", k=KD),
                       t["w_router"][0].rearrange("(k p) n -> p k n", p=P), "smalls")
            wr2 = sm("w_r2").rearrange("p (k n) -> p k n", k=KD)
            small_load(wr2[:, :, 0:4], t["w_router_group_2"][0].rearrange("(k p) n -> p k n", p=P), "smalls")
            small_load(wr2[:, :, 4:36], t["w_router_expert_2"][0].rearrange("(k p) n -> p k n", p=P), "smalls")
            pool.wait_ge(S("gain_free"), 1)
            small_load(gain, bc(t["norm2_gain"][0]), "gain")
            pool.wait_ge(S("m1_brow_free"), 1)
            small_load(at(MMAP, "bdown")[0:NE, 0:D], t["b_down"][0], "bdown")
            pool.wait_ge(S("gain_free"), 2)
            small_load(gain, bc(t["norm_mix_g_2"][0]), "gain")
            pool.wait_ge(S("gain_free"), 3)
            small_load(at(A2MAP, "gain"), bc(t["norm_ffn_g_2"][0]), "ffn_gain")

        NSMALLS = 12 * 16
        lb_rows = t["lower_bound_logits"].rearrange("l (h k) -> (l h) k", k=P)
        conv_rows = t["conv_w_2"][0].rearrange("j (m k) -> (j m) k", k=P)

        @block.scalar
        def _(act):
            A = nc.scalar.activation
            act.dma_start(consts[:, :], t["consts"]).then_inc(S("consts"), 16)
            act.dma_start(rows[0:8, :], t["c"][0].rearrange("(k p) -> k p", p=P)).then_inc(S("rows"), 16)
            act.dma_start(rows[8:16, :], lb_rows).then_inc(S("rows"), 16)
            act.dma_start(rows[16:28, :], conv_rows).then_inc(S("rows"), 16)
            act.dma_start(rows[28:36, :], t["norm1_gain"][0].rearrange("(k p) -> k p", p=P)).then_inc(S("rows"), 16)
            act.dma_start(x[:, :, :], t["x"][0].rearrange("(t p) d -> p t d", p=P)).then_inc(S("x"), 16)
            act.dma_start(pos[64:66, :], t["positions"][0].rearrange("(t p) -> t p", p=P)).then_inc(S("pos"), 16)
            act.wait_ge(S("modrow_zero"), 1)
            for j in range(4):
                act.dma_start(modrow[32 * j:32 * j + 1, :, :],
                              t["b_ada"].rearrange("o (b j n) -> o b j n", b=3, j=4)[:, :, j, :]).then_inc(S("b_ada"), 16)

            act.wait_ge(S("x"), 16)
            for i in range(TT):
                A(hT[:, 4 * i:4 * i + 4, :], x[:, i, :].rearrange("p (k n) -> p k n", k=4), ACT.Square,
                  accum_out=sm("ss")[:, i:i + 1]).then_inc(S("squares"), 1)
            act.wait_ge(S("cols"), 1)
            A(sm("cond"), sm("cols", 8), ACT.Sigmoid).then_inc(S("sig_c"), 1)
            act.wait_ge(S("lbd"), 1)
            A(sm("lb"), sm("lbd"), ACT.Sigmoid).then_inc(S("lb"), 1)
            act.wait_ge(S("mean_square"), 1)
            nc.scalar.sqrt(sm("rs"), sm("ss")[:, 0:2]).then_inc(S("rms"), 1)
            act.wait_ge(S("angles"), 2)
            A(sm("sin"), sm("rr"), ACT.Sin).then_inc(S("sincos"), 1)
            A(sm("cos"), sm("rn"), ACT.Sin).then_inc(S("sincos"), 1)
            act.wait_ge(S("h_transposed"), 2)
            act.wait_ge(S("modT"), 1)
            for k in range(KD):
                last = A(hT[:, k, P:SEQ], PS[:, 2 + k // 4, (k % 4) * P:(k % 4 + 1) * P], ACT.Identity,
                         scale=sm("scaleT")[:, k:k + 1], bias=sm("shiftT")[:, k:k + 1])
            last.then_inc(S("hT_A"), 1)
            act.wait_ge(S("att_ms"), 1)
            nc.scalar.sqrt(sm("rsa", 24), sm("ssa", 24)).then_inc(S("att_std"), 1)
            act.wait_ge(S("big_done"), 3)
            A(at(A1MAP, "b"), PS[:, banks(2), :], ACT.Sigmoid).then_inc(S("big_free_A"), 1)
            act.wait_ge(S("forget"), 4)
            A(at(A1MAP, "b"), at(A1MAP, "k"), ACT.Ln).then_inc(S("log_f"), 1)
            act.wait_ge(S("b_ready"), 1)
            A(at(A1MAP, "tmp"), at(A1MAP, "b"), ACT.Exp).then_inc(S("hg_expb"), 1)
            for n in range(5):
                act.wait_ge(S("hg_arg"), n + 1)
                A(HG_EXPS[n], HG_EXPS[n], ACT.Exp).then_inc(S("hg_exp"), 1)
            act.wait_ge(S("big_done"), 4)
            A(at(A1MAP, "q"), PS[:, banks(3), :], ACT.Sigmoid).then_inc(S("sig_q"), 1)
            act.wait_ge(S("att_nm"), 1)
            s = at(A1MAP, "s").rearrange("p (h n) -> p h n", h=AH)
            for hh in range(AH):
                A(s[:, hh, 0:P], s[:, hh, 0:P], ACT.Exp, bias=sm("nm")[:, hh:hh + 1],
                  accum_out=sm("den")[:, hh:hh + 1]).then_inc(S("att_exp"), 1)
                A(s[:, hh, P:3 * P], s[:, hh, P:3 * P], ACT.Exp, bias=sm("nm")[:, 8 + hh:9 + hh],
                  accum_out=sm("den")[:, 8 + hh:9 + hh]).then_inc(S("att_exp"), 1)
            A(sm("es"), sm("es"), ACT.Exp).then_inc(S("att_exp"), 1)
            act.wait_ge(S("hg_arg"), 6)
            for buf in HG_EXPS[5:]:
                A(buf, buf, ACT.Exp).then_inc(S("hg_exp"), 1)
            act.wait_ge(S("big_done"), 5)
            A(at(A1MAP, "v"), PS[:, banks(4), :], ACT.Copy).then_inc(S("big_free_A"), 1)
            act.wait_ge(S("big_done"), 6)
            act.wait_ge(S("att_pT"), 6)
            A(at(A1MAP, "gs"), PS[:, banks(5), :], ACT.Sigmoid).then_inc(S("sig_g"), 1)
            for n in range(3):
                gate_sig(act, 6 + n, n, A1MAP)
            act.wait_ge(S("hgo_ms"), 1)
            nc.scalar.sqrt(sm("rsh"), sm("ssh")).then_inc(S("hgo_std"), 1)
            gate_sig(act, 9, 3, A1MAP)
            rms_sums(act, "n2")
            hT_copy_act(act, "n2")
            for i in range(TT):
                act.wait_ge(S("r1_arg"), i + 1)
                A(EX[:, i, 0:4], EX[:, i, 0:4], ACT.Exp, accum_out=ESUM[:, i:i + 1])\
                    .then_inc(S("r1_exp"), 1)
            moe1_act_gather(act, "m1", 0)
            with act.Fori(0, NE) as e:
                moe1_act(act, "m1", e, e)
            act.wait_ge(S("m1_flag"), 1)
            more = act.value_load(flag[0:1, 0:1], min_val=0, max_val=SEQ)
            with act.If(more > CAP):
                with act.Fori(0, EXTRA) as p:
                    moe1_act_gather(act, "m1", (NE + 1) * (p + 1))
                    with act.Fori(0, NE) as e:
                        moe1_act(act, "m1", NE * (p + 1) + e, (NE + 1) * (p + 1) + e)
            rms_sums(act, "n3")
            hT_copy_act(act, "n3")
            act.wait_ge(S("big_done"), R2 + 3)
            A(at(A2MAP, "v"), PS[:, banks(R2 + 2), :], ACT.Copy).then_inc(S("big_free_A"), 1)
            act.wait_ge(S("sb_ms"), 1)
            nc.scalar.sqrt(sm("rsa"), sm("ssa")).then_inc(S("sb_std"), 1)
            z = at(A2MAP, "z")
            sp_ = at(A2MAP, "sp")
            for g in range(2):
                act.wait_ge(S("sb_z"), g + 1)
                c = slice(1536 * g, 1536 * (g + 1))
                A(sp_[:, c], z[:, c], ACT.Abs).then_inc(S("sb_e"), 1)
                act.wait_ge(S("sb_e"), 2 * g + 1)
                A(sp_[:, c], sp_[:, c], ACT.Exp, scale=-1.0).then_inc(S("sb_e"), 1)
                act.wait_ge(S("sb_e"), 2 * g + 2)
                A(sp_[:, c], sp_[:, c], ACT.Ln, bias=C("ones")[:, 0:1]).then_inc(S("sb_ln"), 1)
            for n in range(3):
                gate_sig(act, R2 + 6 + n, n, A2MAP)
            for g in range(2):
                act.wait_ge(S("sb_d"), g + 1)
                c = slice(1536 * g, 1536 * (g + 1))
                A(z[:, c], z[:, c], ACT.Exp).then_inc(S("sb_a"), 1)
            gate_sig(act, R2 + 9, 3, A2MAP)
            rms_sums(act, "n4")
            hT_copy_act(act, "n4")
            act.wait_ge(S("r2_arg"), TT)
            for i in range(TT):
                A(GEX[:, i, 0:4], GEX[:, i, 0:4], ACT.Exp, accum_out=GSUM[:, i:i + 1])\
                    .then_inc(S("r2_exp"), 1)
                A(EX[:, i, 0:2], EX[:, i, 0:2], ACT.Exp, accum_out=ESUM[:, i:i + 1])\
                    .then_inc(S("r2_exp"), 1)
            moe2_act_gather(act, "m2", 0)
            with act.Fori(0, NE // 4) as q:
                moe2_act(act, "m2", q, q)
            act.wait_ge(S("m2_flag"), 1)
            more = act.value_load(flag[0:1, 1:2], min_val=0, max_val=SEQ)
            with act.If(more > CAP2):
                with act.Fori(0, EXTRA2) as p:
                    moe2_act_gather(act, "m2", (NE // 4 + 1) * (p + 1))
                    with act.Fori(0, NE // 4) as q:
                        moe2_act(act, "m2", (NE // 4) * (p + 1) + q, (NE // 4 + 1) * (p + 1) + q)

        @block.tensor
        def _(pe):
            aux = [0]

            def aux_bank():
                r = aux[0]
                aux[0] += 1
                if r >= 2:
                    pe.wait_ge(S("aux_free"), r - 1)
                return PS[:, 4 + r % 2, :]

            def begin(r):
                wait(pe, loaded(ROUNDS[r][0]))
                if r >= 2:
                    wait(pe, round_free(r - 2))
                return PS[:, banks(r), :], slots[ROUNDS[r][0] % NSLOT]

            def dense_tokens(r, n=512, src=hT):
                o, w = begin(r)
                w = w[:, 0:KD * n].rearrange("p (k n) -> p k n", k=KD)
                for i in range(TT):
                    for k in range(KD):
                        last = mm(o[:, i, 0:n], src[:, k, i * P:(i + 1) * P], w[:, k, :], k == 0, k == KD - 1)
                last.then_inc(S("big_done"), 1)

            def dense_cols(r, src, nk, n, c0=0):
                o, w = begin(r)
                o = o.rearrange("p b (c t) -> p (b c) t", c=2)
                w = w.rearrange("p (k n) -> p k n", k=nk)
                for c in range(4):
                    for k in range(nk):
                        last = mm(o[:, c, :], w[:, k, c0 + c * P:c0 + (c + 1) * P], src[:, k, :], k == 0, k == nk - 1)
                last.then_inc(S("big_done"), 1)

            def ada(n):
                u = ADA[n]
                b, kp = PRE[u][1:]
                wait(pe, loaded(u))
                w = slots[u % NSLOT].rearrange("p (k n) -> p k n", k=2)
                for kk in range(2):
                    k = 2 * kp + kk
                    for j in range(4):
                        last = nc.tensor.matmul(PS[32 * j:32 * j + 32, 7 if b != 1 else 6, :],
                                                sm("cond32")[:, 32 * k:32 * k + 32], w[:, kk, 512 * j:512 * (j + 1)],
                                                start=k == 0, stop=k == KD - 1, tile_position=(0, 32 * j))
                last.then_inc(S("ada_done"), 1)

            def spread_row(j):
                return ident[:, 32 * j:32 * j + 1].broadcast_to([P, P])

            pe.wait_ge(S("consts"), 16)
            pe.wait_ge(S("rows"), 64)
            nc.tensor.transpose(PS[:, 0, 0:36], rows[0:36, :], ident[0:36, 0:36])
            pe.wait_ge(S("posf"), 1)
            nc.tensor.transpose(PS[:, 1, 0:2], rows[64:66, :], ident[64:66, 64:66]).then_inc(S("rowsT"), 1)
            transpose_h(pe, "n1")
            pe.wait_ge(S("cond32"), 1)
            for n in range(4):
                ada(n)
            pe.wait_ge(S("modrow"), 1)
            for c in range(4):
                last = nc.tensor.transpose(PS[:, 4, c * P:(c + 1) * P], modrow[:, 0, c * P:(c + 1) * P], ident)
            last.then_inc(S("mod1"), 1)
            pe.wait_ge(S("hT_V"), 1)
            pe.wait_ge(S("hT_A"), 1)
            dense_tokens(0)
            ada(4)
            dense_tokens(1, 256)
            ada(5)
            dense_cols(2, hT, KD, 512)
            ada(6)
            qk = at(A1MAP, "qk").rearrange("p (t b w) -> p t b w", t=TT, w=P)
            qkT = at(A1MAP, "qkT").rearrange("p (b t) -> p b t", b=6)
            pe.wait_ge(S("att_qk"), 1)
            for r in range(3):
                o = aux_bank()
                for j in range(2):
                    for i in range(TT):
                        last = nc.tensor.transpose(o[:, (2 * j + i) * P:(2 * j + i + 1) * P], qk[:, i, 2 * r + j, :], ident)
                last.then_inc(S("aux_done"), 1)
            dense_cols(3, hT, KD, 512)
            ada(7)
            pe.wait_ge(S("att_qkT"), 3)

            def att_score(o, hh, qtile, keys):
                q = slice(64 * (hh % 2), 64 * (hh % 2) + 64)
                return mm(o, qkT[q, hh // 2, qtile * P:(qtile + 1) * P], qkT[q, 4 + hh // 4, 0:keys], True, True)

            for r in range(2):
                o = aux_bank()
                for j in range(4):
                    last = att_score(o[:, j * P:(j + 1) * P], 2 * j + r, 0, P)
                last.then_inc(S("aux_done"), 1)
            for r in range(4):
                o = aux_bank()
                for j in range(2):
                    last = att_score(o[:, j * 256:(j + 1) * 256], 4 * (r // 2) + r % 2 + 2 * j, 1, 256)
                last.then_inc(S("aux_done"), 1)
            dense_tokens(4)
            ada(8)
            dense_tokens(5)
            ada(9)
            s = at(A1MAP, "s").rearrange("p (h n) -> p h n", h=AH)
            pe.wait_ge(S("att_p"), 1)
            for b in range(3):
                for r in range(2):
                    o = aux_bank()
                    for j in range(4):
                        last = nc.tensor.transpose(o[:, j * P:(j + 1) * P], s[:, 4 * r + j, b * P:(b + 1) * P], ident)
                    last.then_inc(S("aux_done"), 1)
            dense_cols(6, hT, KD, 512)
            ada(10)
            pT0 = at(A1MAP, "pT0").rearrange("p (h q) -> p h q", h=AH)
            pT1 = at(A1MAP, "pT1").rearrange("p (h q) -> p h q", h=AH)
            vv = at(A1MAP, "vv").rearrange("p (t d) -> p t d", t=TT)
            pe.wait_ge(S("att_pT"), 6)
            for r in range(2):
                o = aux_bank().rearrange("p (m t) -> p m t", m=2)
                for j in range(4):
                    hh = 4 * r + j
                    q, kv = slice(64 * (hh % 2), 64 * (hh % 2) + 64), slice(HD * (hh // 4), HD * (hh // 4) + HD)
                    mm(o[q, j // 2, :], vv[:, 0, kv], pT0[:, hh, :], True, False)
                    last = mm(o[q, j // 2, P:256], vv[:, 1, kv], pT1[:, hh, :], False, True)
                last.then_inc(S("aux_done"), 1)
            pe.wait_ge(S("hg_scores_in"), 1)
            o = aux_bank().rearrange("p (g i) -> p g i", g=8)
            qt = at(A1MAP, "qt").rearrange("p (g i) -> p g i", g=16)
            for hc in range(16):
                q0 = 64 * (hc % 2)
                for i in range(4):
                    n = SUB * (i + 1)
                    last = mm(o[q0:q0 + n, hc // 2, SUB * i:SUB * i + SUB], kt_view(i)[:, hc, :],
                              qt[:, hc, SUB * i:SUB * i + SUB], True, True)
            last.then_inc(S("aux_done"), 1)
            dense_cols(7, hT, KD, 512)
            ada(11)
            pe.wait_ge(S("hg_kd"), 1)
            kd = at(A1MAP, "b").rearrange("p (h t) -> p h t", h=HH)
            kdT = at(A1MAP, "kdT").rearrange("p (t h k) -> p t h k", t=TT, h=HH)
            vals = at(A1MAP, "v").rearrange("p (t h v) -> p t h v", t=TT, h=HH)
            for i in range(TT):
                o = aux_bank()
                for hh in range(HH):
                    last = nc.tensor.transpose(o[:, hh * P:(hh + 1) * P], kd[:, hh, i * P:(i + 1) * P], ident)
                last.then_inc(S("aux_done"), 1)
            for c in range(3):
                i, q = c // 2, slice(64 * (c % 2), 64 * (c % 2) + 64)
                o = aux_bank()
                pe.wait_ge(S("hg_kdT"), i + 1)
                for hh in range(HH):
                    last = mm(o[:, hh * P:(hh + 1) * P], kdT[q, i, hh, :], vals[q, i, hh, :], True, True)
                last.then_inc(S("aux_done"), 1)
            dense_cols(8, hT, KD, 512)
            st = at(A1MAP, "st").rearrange("p (h t i) -> p h t i", h=HH, t=TT)
            qb = at(A1MAP, "q").rearrange("p (h t) -> p h t", h=HH)
            states = at(A1MAP, "state").rearrange("p (c h v) -> p c h v", c=3, h=HH)
            pe.wait_ge(S("hg_st"), 1)
            for i in range(TT):
                o = aux_bank()
                for par in range(2):
                    c, q = 2 * i + par, slice(64 * par, 64 * par + 64)
                    if c:
                        pe.wait_ge(S("hg_state"), c)
                    for hh in range(HH):
                        oo = o[q, hh * P:(hh + 1) * P]
                        last = mm(oo, st[q, hh, i, :], vals[q, i, hh, :], True, c == 0)
                        if c:
                            last = mm(oo, qb[:, hh, c * CH:(c + 1) * CH], states[:, c - 1, hh, :], False, True)
                last.then_inc(S("aux_done"), 1)
            dense_cols(9, hT, KD, 512)

            def spread(b, j):
                mm(aux_bank(), spread_row(j), modrow[:, b, :], True, True).then_inc(S("aux_done"), 1)

            pe.wait_ge(S("modrow"), 3)
            for j in range(4):
                spread(1, j)
            pe.wait_ge(S("hg_out"), 1)
            ho = at(A1MAP, "o").rearrange("p (t h v) -> p t h v", t=TT, h=HH)
            for r in range(2):
                o = aux_bank()
                for j in range(2):
                    for i in range(TT):
                        last = nc.tensor.transpose(o[:, (2 * j + i) * P:(2 * j + i + 1) * P], ho[:, i, 2 * r + j, :], ident)
                last.then_inc(S("aux_done"), 1)
            for j in range(2, 4):
                spread(2, j)
            pe.wait_ge(S("att_oT"), 2)
            attT = at(A1MAP, "attT").rearrange("p (m t) -> p m t", m=4)
            dense_cols(10, attT, 4, D)
            dense_cols(11, attT, 4, D, 512)
            pe.wait_ge(S("hg_oT"), 2)
            oT = at(A1MAP, "oT").rearrange("p (h t) -> p h t", h=HH)
            dense_cols(12, oT, 4, D)
            dense_cols(13, oT, 4, D, 512)
            for j in range(2):
                spread(2, j)
            pe.wait_ge(S("merged"), 1)
            merged = at(A1MAP, "gates", 0, 2048).rearrange("p (k t) -> p k t", k=KD)
            dense_tokens(14, src=merged)
            dense_tokens(15, src=merged)
            transpose_h(pe, "n2")
            router_mm(pe, "n2", sm("w_r1").rearrange("p (k n) -> p k n", k=KD), NE)
            positions_mm(pe, "n2")
            pe.wait_ge(S("weights"), 1)
            for i in range(TT):
                last = nc.tensor.transpose(PS[0:NE, 6, i * P:(i + 1) * P], G[:, i, 0:NE], ident)
            last.then_inc(S("gT"), 1)
            moe1_gather(pe, "m1", 0)
            pe.wait_ge(S("gT_copy"), 1)
            pe.wait_ge(S("bdown"), 16)
            for i in range(TT):
                for b in range(2):
                    last = mm(PS[:, 4 + 2 * i + b, :], GT[:, i * P:(i + 1) * P],
                              at(MMAP, "bdown")[0:NE, b * 512:(b + 1) * 512], True, True)
            last.then_inc(S("bias_rows"), 1)
            with pe.Fori(0, NE) as e:
                def arrived(pe, i):
                    if i == "bias":
                        pe.wait_ge(S("m1_brow"), 16 * e + 16)
                    else:
                        sl, n = loaded(MOE1 + i)
                        pe.wait_ge(sl, 16 * e + n)
                moe1_pe(pe, "m1", e, e, arrived)
            pe.wait_ge(S("m1_flag"), 1)
            more = pe.value_load(flag[0:1, 0:1], min_val=0, max_val=SEQ)
            with pe.If(more > CAP):
                with pe.Fori(0, EXTRA) as p:
                    moe1_gather(pe, "m1", (NE + 1) * (p + 1))
                    with pe.Fori(0, NE) as e:
                        def arrived(pe, i):
                            if i == "bias":
                                pe.wait_ge(S("x1_loaded"), 112 * (NE * p + e) + 112)
                        moe1_pe(pe, "m1", NE * (p + 1) + e, (NE + 1) * (p + 1) + e, arrived)
            transpose_h(pe, "n3")
            pe.wait_ge(S("hT_V"), 3)
            pe.wait_ge(S("hT_A"), 3)
            r = R2
            dense_tokens(r)
            dense_tokens(r + 1)
            dense_tokens(r + 2)
            dense_cols(r + 3, hT, KD, 512)
            qk2 = at(A2MAP, "qk").rearrange("p (t b w) -> p t b w", t=TT, w=P)
            qkT2 = at(A2MAP, "qkT").rearrange("p (b t) -> p b t", b=8)
            pe.wait_ge(S("sb_qk"), 1)
            for n in range(4):
                o = aux_bank()
                for j in range(2):
                    for i in range(TT):
                        last = nc.tensor.transpose(o[:, (2 * j + i) * P:(2 * j + i + 1) * P], qk2[:, i, 2 * n + j, :], ident)
                last.then_inc(S("aux_done"), 1)
            dense_cols(r + 4, hT, KD, 512)
            pe.wait_ge(S("sb_qkT"), 4)
            for hh in range(8):
                q, m = slice(64 * (hh % 2), 64 * (hh % 2) + 64), hh // 2
                o = aux_bank()
                mm(o[:, 0:256], qkT2[q, 4 + m, 0:P], qkT2[q, m, :], True, True)
                mm(o[:, 256:384], qkT2[q, 4 + m, P:256], qkT2[q, m, P:256], True, True).then_inc(S("aux_done"), 1)
            for n in range(5, 8):
                dense_cols(r + n, hT, KD, 512)
            spv = at(A2MAP, "sp").rearrange("p (h n) -> p h n", h=8)
            for hh in range(8):
                if hh % 4 == 0:
                    pe.wait_ge(S("sb_sp"), hh // 4 + 1)
                o = aux_bank()
                mm(o[:, 0:256], C("from_here"), spv[:, hh, 0:256], True, False)
                mm(o[:, P:256], C("ones"), spv[:, hh, 256:384], False, True)
                mm(o[:, 256:384], C("from_here"), spv[:, hh, 256:384], True, True).then_inc(S("aux_done"), 1)
            for n in range(8, 10):
                dense_cols(r + n, hT, KD, 512)
            za = at(A2MAP, "z").rearrange("p (h n) -> p h n", h=8)
            v2 = at(A2MAP, "v").rearrange("p (t d) -> p t d", t=TT)
            for n in range(2):
                pe.wait_ge(S("sb_w"), n + 1)
                o = aux_bank().rearrange("p (m t) -> p m t", m=2)
                for j in range(4):
                    hh = 4 * n + j
                    q = slice(64 * (hh % 2), 64 * (hh % 2) + 64)
                    mm(o[q, j // 2, :], v2[:, 0, hh * HD:(hh + 1) * HD], za[:, hh, 0:256], True, False)
                    last = mm(o[q, j // 2, P:256], v2[:, 1, hh * HD:(hh + 1) * HD], za[:, hh, 256:384], False, True)
                last.then_inc(S("aux_done"), 1)
            pe.wait_ge(S("sb_oT"), 2)
            sbT = at(A2MAP, "attT").rearrange("p (m t) -> p m t", m=4)
            cvT = at(A2MAP, "cv").rearrange("p (m t) -> p m t", m=4)
            dense_cols(r + 10, sbT, 4, D)
            dense_cols(r + 11, sbT, 4, D, 512)
            pe.wait_ge(S("conv"), 1)
            dense_cols(r + 12, cvT, 4, D)
            dense_cols(r + 13, cvT, 4, D, 512)
            pe.wait_ge(S("merged"), 2)
            dense_tokens(r + 14, src=merged)
            dense_tokens(r + 15, src=merged)
            transpose_h(pe, "n4")
            router_mm(pe, "n4", sm("w_r2").rearrange("p (k n) -> p k n", k=KD), 36)
            positions_mm(pe, "n4")
            moe2_gather(pe, "m2", 0)
            with pe.Fori(0, NE // 4) as q:
                def arrived(pe, i):
                    sl, n = loaded(MOE2 + i)
                    pe.wait_ge(sl, 16 * q + n)
                moe2_pe(pe, "m2", q, q, arrived)
            pe.wait_ge(S("m2_flag"), 1)
            more = pe.value_load(flag[0:1, 1:2], min_val=0, max_val=SEQ)
            with pe.If(more > CAP2):
                with pe.Fori(0, EXTRA2) as p:
                    moe2_gather(pe, "m2", (NE // 4 + 1) * (p + 1))
                    with pe.Fori(0, NE // 4) as q:
                        def arrived(pe, i):
                            if i == 0:
                                pe.wait_ge(S("x2_loaded"), 96 * ((NE // 4) * p + q) + 96)
                        moe2_pe(pe, "m2", (NE // 4) * (p + 1) + q, (NE // 4 + 1) * (p + 1) + q, arrived)

        @block.vector
        def _(v):
            count, aux = {}, [0]

            def sig(ins, name):
                count[name] = count.get(name, 0) + 1
                ins.then_inc(S(name), 1)
                v.wait_ge(S(name), count[name])

            def L(ins):
                sig(ins, "v_step")

            def aux_bank():
                r = aux[0]
                aux[0] += 1
                v.wait_ge(S("aux_done"), r + 1)
                return PS[:, 4 + r % 2, :]

            def begin(r):
                v.wait_ge(S("big_done"), r + 1)
                return PS[:, banks(r), :]

            TS, TV, STT, CP = V.tensor_scalar, V.tensor_tensor, V.scalar_tensor_tensor, V.tensor_copy

            sig(V.memset(modrow[:, :, :], 0.0), "modrow_zero")
            v.wait_ge(S("pos"), 16)
            sig(CP(rows[64:66, :], pos[64:66, :]), "posf")
            v.wait_ge(S("rowsT"), 1)
            cols = sm("cols")
            CP(sm("posf"), PS[:, 1, 0:2])
            L(CP(cols, PS[:, 0, 0:36]))
            sig(TV(sm("lbd"), cols[:, 8:12], cols[:, 12:16], ALU.subtract), "lbd")
            sig(CP(sm("one_lb"), sm("lbd")), "cols")
            v.wait_ge(S("sig_c"), 1)
            L(TV(sm("cond"), sm("cond"), cols[:, 0:8], ALU.mult))
            sig(CP(sm("cond32").rearrange("p (k m) -> p k m", k=KD), bc_last(sm("cond"), 32)), "cond32")
            v.wait_ge(S("lb"), 1)
            L(TS(sm("one_lb"), sm("lb"), -1.0, 1.0, ALU.mult, ALU.add))
            v.wait_ge(S("squares"), 2)
            sig(TS(sm("ss")[:, 0:2], sm("ss")[:, 0:2], 1.0 / D, EPS, ALU.mult, ALU.add), "mean_square")
            v.wait_ge(S("rms"), 1)
            L(V.reciprocal(sm("rs"), sm("rs")))
            for i in range(TT):
                sig(TS(h[:, i, :], x[:, i, :], sm("rs")[:, i:i + 1], None, ALU.mult), "h")
            v.wait_ge(S("consts"), 16)
            ang, rr, rn = sm("ang"), sm("rr"), sm("rn")
            for i in range(TT):
                last = TS(ang[:, 8 * i:8 * i + 8], C("inv_freq"), sm("posf")[:, i:i + 1], None, ALU.mult)
            L(last)
            ROUND = 12582912.0
            C1 = 6.28125
            C2 = float(np.float32(2 * np.pi - C1))
            C3 = float(np.float32(2 * np.pi - C1 - np.float64(C2)))
            for dst, turn, add in ((rr, 0.0, 0.0), (rn, 0.25, float(np.float32(np.pi / 2)))):
                t_ = sm("cos")
                L(TS(t_, ang, float(np.float32(1 / (2 * np.pi))), turn, ALU.mult, ALU.add))
                L(TS(t_, t_, ROUND, None, ALU.add))
                L(TS(t_, t_, ROUND, None, ALU.subtract))
                L(STT(out=dst, in0=t_, scalar=-C1, in1=ang, op0=ALU.mult, op1=ALU.add))
                L(STT(out=dst, in0=t_, scalar=-C2, in1=dst, op0=ALU.mult, op1=ALU.add))
                L(STT(out=dst, in0=t_, scalar=-C3, in1=dst, op0=ALU.mult, op1=ALU.add))
                L(TS(dst, dst, add, None, ALU.add))
                sig(TS(dst, dst, 3.1415925, -3.1415925, ALU.min, ALU.max), "angles")
            v.wait_ge(S("b_ada"), 64)
            v.wait_ge(S("ada_done"), 4)
            sig(TV(modrow[:, 0, :], modrow[:, 0, :], PS[:, 7, :], ALU.add), "modrow")
            v.wait_ge(S("mod1"), 1)
            mT = PS[:, 4, :].rearrange("p (c n) -> p n c", c=4)
            for j in range(2):
                CP(sm("shiftT")[:, 4 * j:4 * j + 4], mT[:, 32 * j, :])
                last = STT(out=sm("scaleT")[:, 4 * j:4 * j + 4], in0=mT[:, 64 + 32 * j, :], scalar=1.0,
                           in1=cols[:, 28 + 4 * j:32 + 4 * j], op0=ALU.add, op1=ALU.mult)
            sig(last, "modT")
            v.wait_ge(S("h_transposed"), 2)
            for k in range(KD):
                last = TS(hT[:, k, 0:P], PS[:, k // 4, (k % 4) * P:(k % 4 + 1) * P],
                          sm("scaleT")[:, k:k + 1], sm("shiftT")[:, k:k + 1], ALU.mult, ALU.add)
            sig(last, "hT_V")

            def modulated(name, a, sh):
                for i in range(TT):
                    last = STT(out=h[:, i, :], in0=x[:, i, :], scalar=sm("rs")[:, i:i + 1], in1=a, op0=ALU.mult, op1=ALU.mult)
                L(last)
                for i in range(TT):
                    sig(TV(h[:, i, :], h[:, i, :], sh, ALU.add), "h")

            def hT_copy_dve(name):
                v.wait_ge(S("h_transposed"), 2 * int(name[1]) - 1)
                sig(CP(hT[:, :, 0:P], PS[:, 0:2, :].rearrange("p b (k n) -> p (b k) n", n=P)), "hT_V")

            flat = "p b n -> p (b n)"
            q, k, b, tmp = (at(A1MAP, n) for n in ("q", "k", "b", "tmp"))
            qk = at(A1MAP, "qk").rearrange("p (t g d) -> p t g d", t=TT, d=HD)
            vv = at(A1MAP, "vv").rearrange("p (t d) -> p t d", t=TT)
            o = begin(0)
            sig(CP(qk[:, :, 0:8, :], o.rearrange("p t (g d) -> p t g d", d=HD)), "big_free_V")
            o = begin(1)
            for i in range(TT):
                for c in range(2):
                    CP(qk[:, i, 8 + c:12:2, :], o[:, i, 0:128].rearrange("p (g d) -> p g d", d=HD))
            sig(CP(vv, o[:, :, 128:256]), "big_free_V")
            v.wait_ge(S("smalls"), NSMALLS)

            def head_norm(qk, nh, sq, gains, name):
                w = TT * nh
                flat3 = qk.rearrange("p t g d -> p (t g) d")
                s3 = sq.rearrange("p (g d) -> p g d", d=HD)
                L(TV(s3, flat3, flat3, ALU.mult))
                L(V.reduce_sum(sm("ssa", w), s3, axis=AX))
                sig(TS(sm("ssa", w), sm("ssa", w), 1.0 / HD, EPS, ALU.mult, ALU.add), f"{name}_ms")
                v.wait_ge(S(f"{name}_std"), 1)
                L(V.reciprocal(sm("rsa", w), sm("rsa", w)))
                L(TV(flat3, flat3, bc_last(sm("rsa", w), HD), ALU.mult))
                for i in range(TT):
                    for a, n, g_ in gains:
                        last = TV(qk[:, i, a:a + n, :], qk[:, i, a:a + n, :], bc_mid(sm(g_), n), ALU.mult)
                return last

            L(head_norm(qk, 12, at(A1MAP, "qkT"), [(0, 8, "q_gain"), (8, 4, "k_gain")], "att"))
            v.wait_ge(S("sincos"), 2)
            rt_ = at(A1MAP, "rt")
            for i in range(TT):
                x1, x2 = qk[:, i, :, 0:8], qk[:, i, :, 8:16]
                cs, sn = bc_mid(sm("cos")[:, 8 * i:8 * i + 8], 12), bc_mid(sm("sin")[:, 8 * i:8 * i + 8], 12)
                p4 = [rt_[:, 96 * n + 384 * i:96 * n + 96 + 384 * i].rearrange("p (g d) -> p g d", d=8) for n in range(4)]
                TV(p4[0], x1, cs, ALU.mult)
                TV(p4[1], x2, sn, ALU.mult)
                TV(p4[2], x2, cs, ALU.mult)
                L(TV(p4[3], x1, sn, ALU.mult))
                TV(x1, p4[0], p4[1], ALU.subtract)
                last = TV(x2, p4[2], p4[3], ALU.add)
            sig(last, "att_qk")
            v.wait_ge(S("big_free_A"), 1)
            for i in range(HH):
                c = slice(256 * i, 256 * (i + 1))
                sig(TS(k[:, c], b[:, c], sm("one_lb")[:, i:i + 1], sm("lb")[:, i:i + 1], ALU.mult, ALU.add), "forget")
            for r in range(3):
                sig(CP(at(A1MAP, "qkT", 512 * r, 512), aux_bank()), "att_qkT")
                sig(V.memset(sm("ang"), 0.0), "aux_free")
            reset = at(A1MAP, "reset")
            L(V.memset(reset, 1.0))
            L(V.memset(reset.rearrange("p (g j) -> p g j", g=16)[:, :, 0:1], 0.0))
            v.wait_ge(S("log_f"), 1)
            TS(k, k, -1.0, 1.0, ALU.mult, ALU.add)
            sig(V.tensor_tensor_scan(b, reset, b, 0.0, ALU.mult, ALU.add), "b_ready")
            bg = b.rearrange("p (g j) -> p g j", j=SUB)
            bc_ = b.rearrange("p (g j) -> p g j", j=CH)
            kc = k.rearrange("p (g j) -> p g j", j=CH)
            decay = sm("decay")
            CP(decay, bc_[:, :, CH - 1])
            qt = at(A1MAP, "qt")
            L(TV(qt.rearrange("p (g j) -> p g j", j=SUB), bg, bg[:, :, SUB // 2 - 1:SUB // 2].broadcast_to([P, 64, SUB]),
                 ALU.subtract))
            sig(TS(qt, qt, EXP_CAP, None, ALU.min), "hg_arg")
            for i in range(4):
                n = SUB * (i + 1)
                mid = SUB * i + SUB // 2 - 1
                L(TV(kt_view(i), bc_[:, :, mid:mid + 1].broadcast_to([P, 16, n]), bc_[:, :, 0:n], ALU.subtract))
                sig(TS(kt_view(i), kt_view(i), EXP_CAP, None, ALU.min), "hg_arg")
            s = at(A1MAP, "s").rearrange("p (h n) -> p h n", h=AH)
            wb = C("win_bias")
            for r in range(2):
                o = aux_bank().rearrange("p (h n) -> p h n", h=4)
                sig(STT(out=s[:, r:8:2, 0:P], in0=o, scalar=HD ** -0.5, in1=bc_mid(wb[:, P:256], 4),
                        op0=ALU.mult, op1=ALU.add), "aux_free")
            for r in range(4):
                o = aux_bank().rearrange("p (h n) -> p h n", h=2)
                h0 = 4 * (r // 2) + r % 2
                sig(STT(out=s[:, h0:h0 + 3:2, P:384], in0=o, scalar=HD ** -0.5, in1=bc_mid(wb, 2),
                        op0=ALU.mult, op1=ALU.add), "aux_free")
            m_ = sm("m")
            V.reduce_max(m_[:, 0:8], s[:, :, 0:P], axis=AX)
            L(V.reduce_max(m_[:, 8:16], s[:, :, P:384], axis=AX))
            m2, sink2 = m_.rearrange("p (a h) -> p a h", a=2), bc_mid(sm("sink"), 2)
            L(TV(m2, m2, sink2, ALU.max))
            L(TV(sm("es").rearrange("p (a h) -> p a h", a=2), sink2, m2, ALU.subtract))
            sig(TS(sm("nm"), m_, -1.0, None, ALU.mult), "att_nm")
            o = begin(3)
            v.wait_ge(S("sig_q"), 1)
            sig(TV(q, o.rearrange(flat), q, ALU.mult), "big_free_V")
            v.wait_ge(S("hg_expb"), 1)
            sig(TV(bc_, bc_last(decay, CH), bc_, ALU.subtract), "hg_arg")
            v.wait_ge(S("hg_exp"), 1)
            L(TV(qt, qt, q, ALU.mult))
            L(TV(q, q, tmp, ALU.mult))
            for i in range(4):
                v.wait_ge(S("hg_exp"), i + 2)
                last = TV(kt_view(i), kt_view(i), kc[:, :, 0:SUB * (i + 1)], ALU.mult)
            sig(last, "hg_scores_in")
            v.wait_ge(S("att_exp"), 17)
            L(TV(sm("den"), sm("den"), sm("es"), ALU.add))
            L(V.reciprocal(sm("den"), sm("den")))
            TV(s[:, :, 0:P], s[:, :, 0:P], bc_last(sm("den")[:, 0:8], P), ALU.mult)
            sig(TV(s[:, :, P:384], s[:, :, P:384], bc_last(sm("den")[:, 8:16], 256), ALU.mult), "att_p")
            v.wait_ge(S("hg_exp"), 6)
            sig(TV(b, b, k, ALU.mult), "hg_kd")
            pT0 = at(A1MAP, "pT0").rearrange("p (h q) -> p h q", h=AH)
            pT1 = at(A1MAP, "pT1").rearrange("p (h q) -> p h q", h=AH)
            for b_ in range(3):
                for r in range(2):
                    dst = pT1[:, 4 * r:4 * r + 4, :] if b_ == 2 else pT0[:, 4 * r:4 * r + 4, b_ * P:(b_ + 1) * P]
                    o = aux_bank().rearrange("p (h n) -> p h n", h=4)
                    sig(CP(dst, o), "att_pT")
                    sig(V.memset(sm("ang"), 0.0), "aux_free")
            v.wait_ge(S("sig_g"), 1)
            gs = at(A1MAP, "gs")
            o = begin(5)
            sig(TV(gs, o.rearrange(flat), gs, ALU.mult), "big_free_V")
            L(TV(gs.rearrange("p (g v) -> p g v", g=8), gs.rearrange("p (g v) -> p g v", g=8), bc_mid(sm("hg_gain"), 8),
                 ALU.mult))
            for r in range(2):
                sig(CP(at(A1MAP, "attT", 512 * r, 512), aux_bank()), "att_oT")
                sig(V.memset(sm("ang"), 0.0), "aux_free")
            st = at(A1MAP, "st")
            st8 = st.rearrange("p (g i) -> p g i", g=8)
            L(V.memset(st, 0.0))
            o = aux_bank().rearrange("p (g i) -> p g i", g=8)
            for par in range(2):
                for i in range(4):
                    q_, c = slice(64 * par, 64 * par + SUB * (i + 1)), slice(SUB * i, SUB * (i + 1))
                    mk = C("chunk_causal")[q_, c]
                    last = TV(st8[q_, :, c], o[q_, :, c], bc_mid(mk, 8), ALU.mult)
            last.then_inc(S("hg_st"), 1)
            v.wait_ge(S("hg_st"), 1)
            sig(V.memset(sm("ang"), 0.0), "aux_free")
            kdT = at(A1MAP, "kdT")
            for i in range(TT):
                o = aux_bank()
                last = CP(kdT[:, 512 * i:512 * (i + 1)], o)
                sig(last, "hg_kdT")
                sig(V.memset(sm("ang"), 0.0), "aux_free")
            states = at(A1MAP, "state").rearrange("p (c h v) -> p c h v", c=3, h=HH)
            for c in range(3):
                o = aux_bank().rearrange("p (h v) -> p h v", h=HH)
                if c == 0:
                    sig(CP(states[:, 0], o), "hg_state")
                else:
                    for hh in range(HH):
                        last = STT(out=states[:, c, hh, :], in0=states[:, c - 1, hh, :], scalar=decay[:, 4 * hh + c:4 * hh + c + 1],
                                   in1=o[:, hh, :], op0=ALU.mult, op1=ALU.add)
                    sig(last, "hg_state")
                sig(V.memset(sm("ang"), 0.0), "aux_free")
            v.wait_ge(S("ada_done"), 12)
            sig(TV(modrow[:, 1, :], modrow[:, 1, :], PS[:, 6, :], ALU.add), "modrow")
            sig(TV(modrow[:, 2, :], modrow[:, 2, :], PS[:, 7, :], ALU.add), "modrow")
            ho = at(A1MAP, "o")
            for i in range(TT):
                sig(CP(ho[:, 512 * i:512 * (i + 1)], aux_bank()), "aux_free")
            o8 = ho.rearrange("p (g v) -> p g v", g=8)
            sq8 = at(A1MAP, "qt").rearrange("p (g v) -> p g v", g=8)
            L(TV(sq8, o8, o8, ALU.mult))
            L(V.reduce_sum(sm("ssh"), sq8, axis=AX))
            sig(TS(sm("ssh"), sm("ssh"), 1.0 / 128, EPS, ALU.mult, ALU.add), "hgo_ms")
            v.wait_ge(S("hgo_std"), 1)
            L(V.reciprocal(sm("rsh"), sm("rsh")))
            for g in range(8):
                c = slice(128 * g, 128 * (g + 1))
                last = STT(out=ho[:, c], in0=ho[:, c], scalar=sm("rsh")[:, g:g + 1], in1=gs[:, c], op0=ALU.mult, op1=ALU.mult)
            sig(last, "hg_out")
            sig(V.memset(sm("ang"), 0.0), "m1_brow_free")
            for j in range(2):
                sig(CP(G1[:, 512 * j:512 * (j + 1)], aux_bank()), "aux_free")
            for j in range(2):
                sig(CP(SH2[:, 512 * j:512 * (j + 1)], aux_bank()), "aux_free")
            for r in range(2):
                sig(CP(at(A1MAP, "oT", 512 * r, 512), aux_bank()), "hg_oT")
                sig(V.memset(sm("ang"), 0.0), "aux_free")
            sig(V.memset(sm("ang"), 0.0), "gain_free")
            for j in range(2):
                sig(CP(G2[:, 512 * j:512 * (j + 1)], aux_bank()), "aux_free")

            def merge(r0, m):
                g = at(m, "gates")
                for n in range(4):
                    c = slice(1024 * n, 1024 * (n + 1))
                    o = begin(r0 + n)
                    if n < 2:
                        sig(TV(g[:, c], g[:, c], o.rearrange(flat), ALU.mult), "big_free_V")
                    else:
                        sig(TV(g[:, c], g[:, c], o.rearrange(flat), ALU.mult), "big_free_V")
                sig(TV(g[:, 0:2048], g[:, 0:2048], g[:, 2048:4096], ALU.add), "merged")

            v.wait_ge(S("big_free_A"), 6)
            merge(10, A1MAP)
            v.wait_ge(S("gain"), 16)
            for j in range(2):
                c = slice(512 * j, 512 * (j + 1))
                sig(STT(out=A2[:, c], in0=aux_bank(), scalar=1.0, in1=gain[:, c], op0=ALU.add, op1=ALU.mult), "aux_free")
            sig(V.memset(sm("ang"), 0.0), "gain_free")
            xt = at(A1MAP, "v")
            for j in range(2):
                c = slice(512 * j, 512 * (j + 1))
                o = begin(14 + j)
                sig(TV(xt.rearrange("p (t n) -> p t n", t=TT), o, bc_mid(G1[:, c], TT), ALU.mult), "big_free_V")
                sig(TV(x[:, :, c], x[:, :, c], xt.rearrange("p (t n) -> p t n", t=TT), ALU.add), "x_ready")

            def rms(name, squares):
                v.wait_ge(S("squares"), squares)
                ss = sm("ss")
                if name != "n3":
                    L(TV(ss[:, 0:2], ss[:, 0:2], ss[:, 2:4], ALU.add))
                sig(TS(ss[:, 0:2], ss[:, 0:2], 1.0 / D, EPS, ALU.mult, ALU.add), "mean_square")
                v.wait_ge(S("rms"), int(name[1]))
                L(V.reciprocal(sm("rs"), sm("rs")))

            L(V.memset(rt, 0.0))
            L(V.memset(SL, 512.0))
            rms("n2", 6)
            modulated("n2", A2, SH2)
            hT_copy_dve("n2")
            v.wait_ge(S("logits"), 1)
            logits = PS[:, 4, 0:64 * TT].rearrange("p (t e) -> p t e", t=TT)
            L(TV(LG[:, :, 0:NE], logits[:, :, 0:NE], bc_mid(sm("b_r1"), TT), ALU.add))
            for i in range(TT):
                L(V.max(V8[:, i, :], LG[:, i, 0:NE]))
                sig(TS(EX[:, i, :], V8[:, i, :], V8[:, i, 0:1], None, ALU.subtract), "r1_arg")
            for i in range(TT):
                last = V.max_index(idx[:, i, :], V8[:, i, :], LG[:, i, 0:NE])
            L(last)
            L(CP(IDF[:, :, :], idx[:, :, :]))

            def ranks(n, e):
                return EQ[:, 0:TT * n * e].rearrange("p (t k e) -> p t k e", t=TT, k=n)

            def one_hots(n, e, mask, weights, done):
                eq = ranks(n, e)
                for i in range(TT):
                    last = TV(eq[:, i], bc_mid(C("iota")[:, 0:e], n), bc_last(IDF[:, i, 0:n], e), ALU.is_equal)
                L(last)
                L(V.reduce_sum(mask, eq.rearrange("p t k e -> p t e k"), axis=AX))
                done()
                for i in range(TT):
                    last = TV(eq[:, i], eq[:, i], bc_last(EX[:, i, 0:n], e), ALU.mult)
                L(last)
                sig(V.reduce_sum(weights, eq.rearrange("p t k e -> p t e k"), axis=AX), "weights")

            def r1_weights():
                sig(V.memset(sm("ang"), 0.0), "mask")
                v.wait_ge(S("r1_exp"), TT)
                L(V.reciprocal(ESUM, ESUM))
                for i in range(TT):
                    last = TS(EX[:, i, 0:4], EX[:, i, 0:4], ESUM[:, i:i + 1], None, ALU.mult)
                L(last)

            one_hots(4, NE, M[:, :, :], G[:, :, 0:NE], r1_weights)

            def slot_numbers(n):
                v.wait_ge(S("positions"), n)
                L(STT(out=SL[:, :, 0:NE], in0=PS[:, 5, 0:64 * TT].rearrange("p (t e) -> p t e", t=TT)[:, :, 0:NE],
                      scalar=-512.0, in1=M[:, :, :], op0=ALU.add, op1=ALU.mult))
                L(TS(SL[:, :, 0:NE], SL[:, :, 0:NE], 512.0, None, ALU.add))

            def largest_count(f, m):
                L(V.reduce_max(CMAX[:, 0:1], PS[:, 5, 128:160], axis=AX))
                sig(CP(flag[:, f:f + 1], CMAX[:, 0:1]), f"{m}_flag")

            slot_numbers(1)
            iota0 = C("iota")[:, 0:CAP]
            moe1_select("m1", 0, iota0)
            largest_count(0, "m1")
            v.wait_ge(S("gT"), 1)
            sig(CP(GT, PS[0:NE, 6, 0:256]), "gT_copy")
            v.wait_ge(S("bias_rows"), 1)
            sig(CP(acc, PS[:, 4:8, :].rearrange(flat)), "m1_acc")
            with v.Fori(0, NE) as e:
                moe1_dve(v, "m1", e, e, e, iota0)
            v.wait_ge(S("m1_acc"), NE + 1)
            more = v.value_load(flag[0:1, 0:1], min_val=0, max_val=SEQ)
            with v.If(more > CAP):
                with v.Fori(0, EXTRA) as p:
                    iop = C("iota")[:, bass.ds(CAP * p + CAP, CAP)]
                    moe1_select("m1", 0, iop)
                    with v.Fori(0, NE) as e:
                        moe1_dve(v, "m1", NE * (p + 1) + e, e, (NE + 1) * (p + 1) + e, iop)
                v.wait_ge(S("m1_acc"), NE * (EXTRA + 1) + 1)
            for i in range(TT):
                c = slice(D * i, D * (i + 1))
                L(TV(acc[:, c], acc[:, c], G2, ALU.mult))
                sig(TV(x[:, i, :], x[:, i, :], acc[:, c], ALU.add), "x_ready")

            def gained(name, g):
                for i in range(TT):
                    sig(STT(out=h[:, i, :], in0=x[:, i, :], scalar=sm("rs")[:, i:i + 1], in1=g, op0=ALU.mult, op1=ALU.mult),
                        "h")

            rms("n3", 8)
            v.wait_ge(S("gain"), 32)
            gained("n3", gain)
            hT_copy_dve("n3")
            qk = at(A2MAP, "qk").rearrange("p (t g d) -> p t g d", t=TT, d=HD)
            for n in range(2):
                o = begin(R2 + n)
                sig(CP(qk[:, :, 8 * n:8 * n + 8, :], o.rearrange("p t (g d) -> p t g d", d=HD)), "big_free_V")
            sig(head_norm(qk, 16, at(A2MAP, "sp", 0, 2048), [(0, 8, "q_gain2"), (8, 8, "k_gain2")], "sb"), "sb_qk")
            cb, tmp2, cv = at(A2MAP, "cb"), at(A2MAP, "tmp"), at(A2MAP, "cv")
            o = begin(R2 + 3)
            sig(CP(tmp2, o.rearrange(flat)), "big_free_V")
            for n in range(4):
                sig(CP(at(A2MAP, "qkT", 512 * n, 512), aux_bank()), "sb_qkT")
                sig(V.memset(sm("ang"), 0.0), "aux_free")
            cu = at(A2MAP, "cu", 0, 4 * 258).rearrange("p (m t) -> p m t", m=4)
            L(V.memset(cu[:, :, 0:2], 0.0))
            o = begin(R2 + 4)
            sig(TV(cu[:, :, 2:258], o.rearrange("p b (c t) -> p (b c) t", c=2), tmp2.rearrange("p (m t) -> p m t", m=4),
                   ALU.mult), "big_free_V")
            z = at(A2MAP, "z")
            z3 = z.rearrange("p (h n) -> p h n", h=8)
            sp_ = at(A2MAP, "sp")
            sp3 = sp_.rearrange("p (h n) -> p h n", h=8)
            before = C("before")
            for hh in range(8):
                o = aux_bank()
                sig(TS(z3[:, hh, :], o[:, 0:384], HD ** -0.5, None, ALU.mult), "aux_free")
                if hh % 4 == 3:
                    sig(V.memset(sm("ang"), 0.0), "sb_z")
            o = begin(R2 + 5)
            sig(CP(cb, o.rearrange(flat)), "big_free_V")
            cv3 = cv.rearrange("p (m t) -> p m t", m=4)
            for m in range(4):
                w = [cols[:, 16 + 4 * j + m:17 + 4 * j + m] for j in range(3)]
                L(TS(cv3[:, m, :], cu[:, m, 0:256], w[0], None, ALU.mult))
                L(STT(out=cv3[:, m, :], in0=cu[:, m, 1:257], scalar=w[1], in1=cv3[:, m, :], op0=ALU.mult, op1=ALU.add))
                L(STT(out=cv3[:, m, :], in0=cu[:, m, 2:258], scalar=w[2], in1=cv3[:, m, :], op0=ALU.mult, op1=ALU.add))
            sig(TV(cv, cv, cb, ALU.mult), "conv")
            for g in range(2):
                c, hs = slice(1536 * g, 1536 * (g + 1)), slice(4 * g, 4 * g + 4)
                v.wait_ge(S("sb_ln"), g + 1)
                L(STT(out=sp_[:, c], in0=z[:, c], scalar=0.0, in1=sp_[:, c], op0=ALU.max, op1=ALU.add))
                TV(sp3[:, hs, 0:P], sp3[:, hs, 0:P], bc_mid(before, 4), ALU.mult)
                sig(TV(sp3[:, hs, 256:384], sp3[:, hs, 256:384], bc_mid(before, 4), ALU.mult), "sb_sp")
            for hh in range(8):
                o = aux_bank()
                sig(TV(z3[:, hh, :], z3[:, hh, :], o[:, 0:384], ALU.subtract), "aux_free")
                if hh % 4 == 3:
                    c = slice(1536 * (hh // 4), 1536 * (hh // 4 + 1))
                    sig(TS(z[:, c], z[:, c], 0.0, None, ALU.min), "sb_d")
            for g in range(2):
                hs = slice(4 * g, 4 * g + 4)
                v.wait_ge(S("sb_a"), g + 1)
                TV(z3[:, hs, 0:P], z3[:, hs, 0:P], bc_mid(before, 4), ALU.mult)
                sig(TV(z3[:, hs, 256:384], z3[:, hs, 256:384], bc_mid(before, 4), ALU.mult), "sb_w")
            for n in range(2):
                sig(CP(at(A2MAP, "attT", 512 * n, 512), aux_bank()), "sb_oT")
                sig(V.memset(sm("ang"), 0.0), "aux_free")
            sig(V.memset(sm("ang"), 0.0), "gain_free")
            v.wait_ge(S("big_free_A"), 11)
            merge(R2 + 10, A2MAP)
            for j in range(2):
                c = slice(512 * j, 512 * (j + 1))
                o = begin(R2 + 14 + j)
                sig(TV(x[:, :, c], x[:, :, c], o, ALU.add), "big_free_V")
                sig(V.memset(sm("ang"), 0.0), "x_ready")
            L(V.memset(rt, 0.0))
            L(V.memset(SL, 512.0))
            L(V.memset(GL, NEG))
            rms("n4", 12)
            v.wait_ge(S("ffn_gain"), 16)
            gained("n4", at(A2MAP, "gain"))
            hT_copy_dve("n4")
            v.wait_ge(S("logits"), 2)
            L(TV(LG[:, :, :], logits[:, :, 0:36], bc_mid(sm("b_r2"), TT), ALU.add))
            L(CP(GL[:, :, 0:4], LG[:, :, 0:4]))
            for i in range(TT):
                last = V.max(GV8[:, i, :], GL[:, i, :])
            L(last)
            for i in range(TT):
                TS(GEX[:, i, 0:4], GL[:, i, 0:4], GV8[:, i, 0:1], None, ALU.subtract)
                last = V.max_index(idx[:, i, :], GV8[:, i, :], GL[:, i, :])
            L(last)
            L(CP(GID[:, :, :], idx[:, :, :]))
            L(TV(OH[:, :, :], bc_mid(C("iota")[:, 0:4], TT), bc_last(GID[:, :, 0], 4), ALU.is_equal))
            for i in range(TT):
                last = TV(EQ[:, 32 * i:32 * i + 32].rearrange("p (g e) -> p g e", g=4),
                          LG[:, i, 4:36].rearrange("p (g e) -> p g e", g=4), bc_last(OH[:, i, :], 8), ALU.mult)
            L(last)
            L(V.reduce_sum(EIG[:, :, :], EQ[:, 0:64].rearrange("p (t g e) -> p t e g", t=TT, g=4), axis=AX))
            for i in range(TT):
                last = V.max(V8[:, i, :], EIG[:, i, :])
            L(last)
            for i in range(TT):
                sig(TS(EX[:, i, :], V8[:, i, :], V8[:, i, 0:1], None, ALU.subtract), "r2_arg")
            for i in range(TT):
                last = V.max_index(idx2[:, i, :], V8[:, i, :], EIG[:, i, :])
            L(last)
            L(CP(IDF[:, :, :], idx2[:, :, :]))

            def to_all(dst, src):
                for i in range(TT):
                    last = TV(dst[:, i, 0:NE].rearrange("p (g e) -> p g e", g=4), bc_mid(src[:, i, :], 4),
                              bc_last(OH[:, i, :], 8), ALU.mult)
                return last

            def r2_weights():
                sig(to_all(M, M8), "mask")
                v.wait_ge(S("r2_exp"), 2 * TT)
                L(TV(ESUM, ESUM, GSUM, ALU.mult))
                L(V.reciprocal(ESUM, ESUM))
                for i in range(TT):
                    last = TS(EX[:, i, 0:2], EX[:, i, 0:2], ESUM[:, i:i + 1], None, ALU.mult)
                L(last)

            one_hots(2, 8, M8[:, :, :], W8[:, :, :], r2_weights)
            L(to_all(G, W8))
            slot_numbers(2)
            iota2 = C("iota")[:, 0:CAP2]
            moe2_select("m2", 0, iota2)
            largest_count(1, "m2")
            sig(V.memset(acc, 0.0), "m2_acc")
            with v.Fori(0, NE // 4) as q:
                moe2_dve(v, "m2", q, q, q, iota2)
            v.wait_ge(S("m2_acc"), NE // 4 + 1)
            more = v.value_load(flag[0:1, 1:2], min_val=0, max_val=SEQ)
            with v.If(more > CAP2):
                with v.Fori(0, EXTRA2) as p:
                    iop = C("iota")[:, bass.ds(CAP2 * p + CAP2, CAP2)]
                    moe2_select("m2", 0, iop)
                    with v.Fori(0, NE // 4) as q:
                        moe2_dve(v, "m2", (NE // 4) * (p + 1) + q, q, (NE // 4 + 1) * (p + 1) + q, iop)
                v.wait_ge(S("m2_acc"), (NE // 4) * (EXTRA2 + 1) + 1)
            TV(x[:, :, :].rearrange("p t d -> p (t d)"), x[:, :, :].rearrange("p t d -> p (t d)"), acc, ALU.add)\
                .then_inc(S("result"), 1)


_INS = ["x", "c", "positions", "w_ada", "b_ada", "norm1_gain", "w_in", "lower_bound_logits", "hg_norm_gain", "w_hg_branch",
        "q_norm_gain", "k_norm_gain", "attn_sinks", "w_attn_branch", "w_out", "norm2_gain", "w_router", "b_router", "w_up",
        "b_up", "w_down", "b_down", "norm_mix_g_2", "w_in_2", "q_norm_g_2", "k_norm_g_2", "conv_w_2", "w_sb_branch_2",
        "w_conv_branch_2", "w_out_2", "norm_ffn_g_2", "w_router_group_2", "b_router_group_2", "w_router_expert_2",
        "b_router_expert_2", "w_gate_e_2", "w_up_e_2", "w_down_e_2"]


def kernel(**inputs):
    import concourse.bacc as _bacc
    from concourse.bass_utils import run_bass_kernel_spmd as _run

    nc = _bacc.Bacc("TRN2", target_bir_lowering=False, num_devices=1)
    arrays, t = {}, {}
    for name in _INS + ["consts"]:
        a = CONSTS if name == "consts" else np.ascontiguousarray(inputs[name])
        arrays[f"in_{name}"] = a
        t[name] = nc.dram_tensor(f"in_{name}", a.shape, mybir.dt.from_np(a.dtype), kind="ExternalInput").ap()
    out = nc.dram_tensor("out_0", (1, SEQ, D), F32, kind="ExternalOutput").ap()
    program(nc, t, out)
    r = _run(nc, [arrays], core_ids=[0])
    return r.results[0]["out_0"]
```

```python
import numpy as np
import concourse.bass as bass
from concourse import mybir
from contextlib import ExitStack

F32 = mybir.dt.float32
F32R = mybir.dt.float32r
I32 = mybir.dt.int32
U32 = mybir.dt.uint32
ALU = mybir.AluOpType
ACT = mybir.ActivationFunctionType
AX = mybir.AxisListType.X

P = 128
SEQ, D = 256, 1024
TT, KD = SEQ // P, D // P
EPS = 1e-6
NSLOT, SLOTW = 6, 4096
CH, SUB = 64, 16
EXP_CAP = 80.0
HH, AH, KVH, HD = 4, 8, 2, 64
NE, CAP, CAP2 = 32, 64, 32
EXTRA, EXTRA2 = SEQ // CAP - 1, SEQ // CAP2 - 1
NEG = -1.0e30
C_IN, C_IN2 = 4864, 5120

CONST = {}
_cols = []


def _const(name, a):
    a = np.asarray(a, np.float32).reshape(P, -1)
    CONST[name] = (sum(c.shape[1] for c in _cols), a.shape[1])
    _cols.append(a)


_p = np.arange(P)[:, None]
_f = np.arange(P)[None, :]
_const("ident", _p == _f)
_const("before", _p < _f)
_const("from_here", _p >= _f)
_const("ones", np.ones((P, P)))
_const("win_bias", np.concatenate([np.where(_f > _p, 0.0, NEG), np.where(_f <= _p, 0.0, NEG)], 1))
_const("chunk_causal", (_p % CH) <= np.arange(CH)[None, :])
_const("iota", np.broadcast_to(np.arange(SEQ)[None, :], (P, SEQ)))
_const("inv_freq", np.broadcast_to((np.float32(500000.0) ** (-np.arange(8, dtype=np.float32) / 8))[None, :], (P, 8)))
CONSTS = np.concatenate(_cols, axis=1)
NCONST = CONSTS.shape[1]

SMALL = {}
_at = 0
for _n, _w in [("w_r1", KD * NE), ("w_r2", KD * 36), ("hg_gain", 128), ("q_gain", 64), ("k_gain", 64), ("sink", 8),
               ("b_r1", NE), ("b_r2", 36), ("q_gain2", 64), ("k_gain2", 64), ("cols", 36), ("shiftT", 8), ("scaleT", 8), ("cond", 8), ("lb", 4),
               ("one_lb", 4), ("lbd", 4), ("posf", 2), ("ss", 4), ("rs", 2), ("ang", 16), ("rn", 16), ("rr", 16), ("cos", 16),
               ("sin", 16), ("decay", 16), ("ssh", 8), ("rsh", 8), ("ssa", 32), ("rsa", 32), ("m", 16), ("nm", 16),
               ("es", 16), ("den", 16), ("cond32", KD * 32)]:
    SMALL[_n] = (_at, _w)
    _at += _w
NSMALL = _at

KB = 256
ARENA = 78.125
A1MAP = dict(h=(0, 8), acc=(8, 8), g1=(16, 4), a2=(20, 4), sh2=(24, 4), g2=(28, 4), gain=(32, 4),
             q=(0, 4), k=(4, 4), b=(8, 4), v=(12, 4), tmp=(16, 4), reset=(16, 4), qt=(20, 4), oT=(20, 4), vv=(24, 1),
             st=(24, 2), kt=(26, 10), kdT=(26, 4), o=(30, 4), qk=(36, 6), pT1=(36, 4), gates=(42, 16), s=(58, 12),
             attT=(58, 4), gs=(62, 4), rt=(66, 3), qkT=(70, 6), pT0=(70, 8), state=(70, 6))
MMAP = dict(h=(0, 8), acc=(8, 8), gain=(32, 4), xg=(42, 4), glu=(46, 2), lin=(48, 2), sg=(50, 2), act=(52, 2), aT=(54, 2),
            ye=(56, 4), swT=(60, 1), selS=(61, 1), selW=(62, 1), brow=(63, 8), gT=(40, 1), bdown=(71, 4), rt=(75, 3))
A2MAP = dict(h=(0, 8), qkT=(0, 8), v=(8, 4), attT=(12, 4), qk=(16, 8), z=(16, 12), sp=(28, 12), gates=(42, 16),
             tmp=(58, 4), cu=(62, 4.125), cb=(66.125, 4), cv=(70.125, 4), gain=(16, 4))

PRE = ([("ada", 0, i) for i in range(4)] + [("in", 0), ("ada", 1, 0), ("in", 1), ("ada", 1, 1), ("in", 2), ("ada", 1, 2),
       ("in", 3), ("ada", 1, 3), ("in", 4), ("ada", 2, 0), ("in", 5), ("ada", 2, 1), ("in", 6), ("ada", 2, 2), ("in", 7),
       ("ada", 2, 3), ("in", 8), ("in", 9), ("at",), ("hg",), ("out", 0), ("out", 1)])
MOE1 = len(PRE)
MID0 = MOE1 + 6 * NE
MID = [("in", i) for i in range(10)] + [("cv",), ("sb",), ("out", 0), ("out", 1)]
MOE2 = MID0 + len(MID)
IN_COLS = [(2048, 512), (2560, 256), (512, 512), (0, 512), (1024, 512), (1536, 512), (3840, 512), (4352, 512),
           (2816, 512), (3328, 512)]
IN_COLS2 = [(512 * n, 512) for n in (0, 1, 2, 4, 5, 3, 8, 9, 6, 7)]


def program(nc, t, out):
    ctx = ExitStack()
    with ctx:
        def sb(name, shape, dt=F32):
            return ctx.enter_context(nc.sbuf_tensor(name, shape, dt))

        sems = {}

        def S(name):
            if name not in sems:
                sems[name] = ctx.enter_context(nc.semaphore(name))
            return sems[name]

        def sb_twice(name, shape):
            with nc.sbuf_tensor(name, shape, F32) as a:
                pass
            return a, sb(name + "_r", shape, F32R)

        ring4, ring4_r = sb_twice("ring4", [P, 4, SLOTW])
        ring2, ring2_r = sb_twice("ring2", [P, 2, SLOTW])
        x = sb("x", [P, TT, D])
        hT, hT_r = sb_twice("hT", [P, KD, SEQ])
        modrow = sb("modrow", [P, 3, 512])
        consts = sb("consts", [P, NCONST])
        small = sb("small", [P, NSMALL])
        rows = sb("rows", [66, P])
        pos = sb("pos", [66, P], I32)
        idx = sb("idx", [P, TT, 8], U32)
        idx2 = sb("idx2", [P, TT, 8], U32)
        flag = sb("flag", [P, 2], I32)
        arena, arena_r = sb_twice("arena", [P, int(ARENA * KB)])
        PS = ctx.enter_context(nc.psum_tensor("PS", [P, 8, 512], F32))

        def C(name):
            a, n = CONST[name]
            return consts[:, a:a + n]

        def sm(name, n=None):
            a, w = SMALL[name]
            return small[:, a:a + (n or w)]

        def at(m, name, lo=0, n=None, mem=arena):
            a, w = m[name]
            a = int(a * KB) + lo
            return mem[:, a:a + (n if n else int(w * KB) - lo)]

        ident = C("ident")
        slots = [ring4[:, i, :] for i in range(4)] + [ring2[:, i, :] for i in range(2)]

        h = at(A1MAP, "h").rearrange("p (t d) -> p t d", t=TT)
        acc = at(A1MAP, "acc")
        acc4 = acc.rearrange("p (t c n) -> p (t c) n", t=TT, c=2)
        gain = at(A1MAP, "gain")
        xres = x[:, :, :]
        A1 = at(A1MAP, "a2")
        SH1 = at(A1MAP, "sh2")
        G1 = at(A1MAP, "g1")
        A2 = at(A1MAP, "a2")
        SH2 = at(A1MAP, "sh2")
        G2 = at(A1MAP, "g2")

        def slot_of(u):
            if MID0 <= u < MOE2:
                return (2, 3, 0, 1)[(u - MID0) % 4]
            return (u - MOE2) % NSLOT if u >= MOE2 else u % NSLOT

        SLOT_OF = [slot_of(u) for u in range(MOE2 + NSLOT)]

        def before_in_slot(u):
            return max(v for v in range(u) if SLOT_OF[v] == SLOT_OF[u])

        def unit_load(eng, u, desc):
            s = SLOT_OF[u]
            kind = desc[0]
            blk2 = u >= MID0
            if kind == "ada":
                _, b, kp = desc
                dst = slots[s].rearrange("p (k n) -> p k n", k=2)
                src = t["w_ada"][0, kp * 256:(kp + 1) * 256, b * 2048:(b + 1) * 2048].rearrange("(k p) n -> p k n", p=P)
            elif kind == "in":
                w = t["w_in_2"] if blk2 else t["w_in"]
                c0, cn = (IN_COLS2 if blk2 else IN_COLS)[desc[1]]
                dst = slots[s][:, 0:KD * cn].rearrange("p (k n) -> p k n", k=KD)
                src = w[0, :, c0:c0 + cn].rearrange("(k p) n -> p k n", p=P)
            elif kind in ("hg", "at", "sb", "cv"):
                w = t[{"hg": "w_hg_branch", "at": "w_attn_branch", "sb": "w_sb_branch_2", "cv": "w_conv_branch_2"}[kind]]
                dst = slots[s].rearrange("p (k n) -> p k n", k=4)
                src = w[0].rearrange("(k p) n -> p k n", p=P)
            else:
                w = t["w_out_2"] if blk2 else t["w_out"]
                dst = slots[s].rearrange("p (k n) -> p k n", k=KD)
                src = w[0, :, desc[1] * 512:(desc[1] + 1) * 512].rearrange("(k p) n -> p k n", p=P)
            eng.dma_start(dst, src).then_inc(S(f"loaded{s}"), 16)

        def loaded(u):
            return S(f"loaded{SLOT_OF[u]}"), 16 * SLOT_OF[:u + 1].count(SLOT_OF[u])

        def big_rounds():
            out_ = []
            for base, units in ((0, PRE), (MID0, MID)):
                for n, d in enumerate(units):
                    if d[0] in ("in", "out"):
                        out_.append((base + n, d, 0, True))
                    elif d[0] != "ada":
                        out_ += [(base + n, d, 0, False), (base + n, d, 1, True)]
            return out_

        ROUNDS = big_rounds()
        R2 = sum(1 for r in ROUNDS if r[0] < MID0)
        ADA = [n for n, d in enumerate(PRE) if d[0] == "ada"]

        def unit_free(u):
            if u < MOE1 and PRE[u][0] == "ada":
                return S("ada_done"), ADA.index(u) + 1
            if MOE1 <= u < MID0:
                i = (u - MOE1) % 6
                e = (u - MOE1) // 6
                return (S("m1_up_done"), 4 * e + i + 1) if i < 4 else (S("m1_down_done"), 2 * e + i - 3)
            return S("big_done"), [n for n, r in enumerate(ROUNDS) if r[0] == u and r[3]][0] + 1

        EVAC = "VVAVAV" + "AAAA" + "VVVV" + "VV" + "VVA" + "VVV" + "AAAA" + "VVVV" + "VV"
        assert len(EVAC) == len(ROUNDS)

        def round_free(r):
            e = EVAC[r]
            return S(f"big_free_{e}"), EVAC[:r + 1].count(e)

        def wait(eng, sv):
            eng.wait_ge(sv[0], sv[1])

        PIECES = []
        for r_ in range(R2, len(ROUNDS)):
            u_, d_, half_, _ = ROUNDS[r_]
            w_, wr_ = slots[SLOT_OF[u_]], ring4_r[:, SLOT_OF[u_], :]
            if d_[0] in ("in", "out"):
                for i_ in range(2):
                    if 3 <= r_ - R2 < 10:
                        PIECES.append((r_, i_ == 1) + tuple(a.rearrange("p (k n) -> p k n", k=KD)
                                                            [:, :, 256 * i_:256 * (i_ + 1)] for a in (w_, wr_)))
                    else:
                        PIECES.append((r_, i_ == 1) + tuple(a[:, 2048 * i_:2048 * (i_ + 1)]
                                                            .rearrange("p (k n) -> p k n", n=512) for a in (w_, wr_)))
            else:
                PIECES.append((r_, True) + tuple(a.rearrange("p (k n) -> p k n", k=4)[:, :, 512 * half_:512 * (half_ + 1)]
                                                 for a in (w_, wr_)))

        def pieces_of(r):
            return [n for n, p in enumerate(PIECES) if p[0] == r]

        def piece_used(n):
            r, last = PIECES[n][:2]
            if last:
                return S("big_done"), r + 1
            return S("half_done"), 1 + sum(1 for p in PIECES[:n] if not p[1])

        def upper(n):
            m = n % 3
            return ring2_r[:, m // 2, 2048 * (m % 2):2048 * (m % 2) + 2048]\
                .rearrange("p (k n) -> p k n", k=PIECES[n][2].shape[1])

        sb_up = at(A2MAP, "attT", mem=arena_r).rearrange("p (m t) -> p m t", m=4)
        cv_up = at(A2MAP, "tmp", mem=arena_r).rearrange("p (m t) -> p m t", m=4)
        cv_low = at(A2MAP, "cb", mem=arena_r).rearrange("p (m t) -> p m t", m=4)
        hT_up = hT_r[:, :, :]
        hT_low = ring2_r[:, 1, 2048:4096].rearrange("p (k t) -> p k t", k=KD)

        def split_upper(act, n):
            wait(act, loaded(ROUNDS[PIECES[n][0]][0]))
            if n >= 3:
                wait(act, piece_used(n - 3))
            nc.scalar.activation(upper(n), PIECES[n][2], ACT.Copy).then_inc(S("w_upper"), 1)

        def split_lower(v, n):
            v.wait_ge(S("w_upper"), n + 1)
            _, _, w, w_r = PIECES[n]
            nc.vector.tensor_tensor(w_r, w, upper(n), ALU.subtract).then_inc(S("w_lower"), 1)

        block = ctx.enter_context(nc.Block())

        w_up_u = t["w_up"][0].rearrange("e (i k p) n -> e i p k n", p=P, k=2)
        w_dn_u = t["w_down"][0].rearrange("e (i k p) n -> e i p k n", p=P, k=4)

        def moe1_src(e, i):
            w = w_up_u if i < 4 else w_dn_u
            j = i if i < 4 else i - 4
            return w[bass.ds(e, 1), j, :, :, :].rearrange("o p k n -> p (o k) n")

        def moe1_dst(i):
            return slots[SLOT_OF[MOE1 + i]].rearrange("p (k n) -> p k n", k=2 if i < 4 else 4)

        def moe2_src(quad, i):
            w = t[("w_gate_e_2", "w_up_e_2", "w_down_e_2")[i // 2]][0]
            return w[bass.ds(4 * quad + 2 * (i % 2), 2), :, :].rearrange("o (k p) n -> p (o k) n", p=P)

        def moe2_dst(i):
            return slots[SLOT_OF[MOE2 + i]].rearrange("p (k n) -> p k n", k=16 if i < 4 else 4)

        brow = at(MMAP, "brow")[0:1, 0:2048]


        def banks(r):
            return slice(2 * (r % 2), 2 * (r % 2) + 2)

        def kt_view(i):
            lo = 8 * SUB * i * (i + 1)
            return at(A1MAP, "kt", lo, 256 * (i + 1)).rearrange("p (g j) -> p g j", g=16)

        HG_EXPS = [at(A1MAP, "qt")] + [at(A1MAP, "kt", 8 * SUB * i * (i + 1), 256 * (i + 1)) for i in range(4)] \
            + [at(A1MAP, "b"), sm("decay")]

        rt = at(MMAP, "rt")
        glu_ = at(MMAP, "glu")
        _o = [0]

        def rt_part(n, k=None):
            a = _o[0]
            _o[0] += n * (k or 1)
            return rt[:, a:a + n] if k is None else rt[:, a:a + n * k].rearrange("p (t e) -> p t e", t=n)

        G, SL = rt_part(TT, NE + 4), rt_part(TT, NE + 4)
        M, LG = rt_part(TT, NE), rt_part(TT, 36)
        V8, IDF, EX, GV8, GID, GEX, GL, EIG = (rt_part(TT, 8) for _ in range(8))
        W8, M8, OH = rt_part(TT, 8), rt_part(TT, 8), rt_part(TT, 4)
        ESUM, GSUM, CMAX = rt_part(2), rt_part(2), rt_part(2)
        EQ = rt_part(8 * NE)
        assert _o[0] <= 3 * KB
        GT = at(MMAP, "gT")[0:NE, :]

        xg1 = at(MMAP, "xg", 0, 512)
        xg2 = at(MMAP, "xg", 0, 1024)
        glu, lin, sg, actb, aT = (at(MMAP, n) for n in ("glu", "lin", "sg", "act", "aT"))
        ye = at(MMAP, "ye")
        swT = at(MMAP, "swT")
        selS = at(MMAP, "selS")
        selW = at(MMAP, "selW")

        def gate_sig(act, r, n, m):
            act.wait_ge(S("big_done"), r + 1)
            nc.scalar.activation(at(m, "gates", 1024 * n, 1024), PS[:, banks(r), :], ACT.Sigmoid)\
                .then_inc(S("big_free_A"), 1)

        def rms_sums(act, n, squares):
            k = int(n[1])
            for i in range(2):
                act.wait_ge(S("x_ready"), 2 * (k - 2) + i + 1)
                if k == 3:
                    nc.scalar.activation(squares[:, 4 * i:4 * i + 4, :], x[:, i, :].rearrange("p (k n) -> p k n", k=4),
                                         ACT.Square, accum_out=sm("ss")[:, i:i + 1]).then_inc(S("squares"), 1)
                    if i == 0:
                        split_upper(act, 0)
                else:
                    for tile in range(TT):
                        a = 4 * i + 2 * tile
                        nc.scalar.activation(squares[:, a:a + 2, :],
                                             x[:, tile, 512 * i:512 * (i + 1)].rearrange("p (k n) -> p k n", k=2),
                                             ACT.Square, accum_out=sm("ss")[:, 2 * i + tile:2 * i + tile + 1])\
                            .then_inc(S("squares"), 1)
            act.wait_ge(S("mean_square"), k)
            nc.scalar.sqrt(sm("rs"), sm("ss")[:, 0:2]).then_inc(S("rms"), 1)

        def hT_copy_act(act, n):
            act.wait_ge(S("h_transposed"), 2 * int(n[1]))
            nc.scalar.activation(hT[:, :, P:256], PS[:, 2:4, :].rearrange("p b (k n) -> p (b k) n", n=P), ACT.Copy)\
                .then_inc(S("hT_A"), 1)

        def moe1_act_gather(act, X, g):
            act.wait_ge(S(f"{X}_gath_done"), g + 1)
            nc.scalar.activation(xg1, PS[:, 0, :], ACT.Copy).then_inc(S(f"{X}_xg"), 1)

        def moe1_act(act, X, it, g):
            act.wait_ge(S(f"{X}_glu"), it + 1)
            nc.scalar.activation(sg, glu, ACT.Sigmoid, scale=1.702).then_inc(S(f"{X}_sg"), 1)
            moe1_act_gather(act, X, g + 1)
            act.wait_ge(S(f"{X}_down_done"), 2 * it + 2)
            nc.scalar.activation(ye[:, 0:512], PS[:, 1, :], ACT.Copy).then_inc(S(f"{X}_ye"), 1)

        def moe2_act_gather(act, X, g):
            act.wait_ge(S(f"{X}_gath_done"), g + 1)
            nc.scalar.activation(xg2, PS[:, 0:2, :], ACT.Copy).then_inc(S(f"{X}_xg"), 1)

        def moe2_act(act, X, it, g):
            act.wait_ge(S(f"{X}_gu_done"), 2 * it + 1)
            nc.scalar.activation(sg[:, 0:256], PS[:, 2, 0:256], ACT.Sigmoid).then_inc(S(f"{X}_sg"), 1)
            moe2_act_gather(act, X, g + 1)
            act.wait_ge(S(f"{X}_down_done"), it + 1)
            nc.scalar.activation(ye, PS[:, 0:2, :], ACT.Copy).then_inc(S(f"{X}_ye"), 1)

        def mm(o, w, m, first, last):
            return nc.tensor.matmul(o, w, m, start=first, stop=last)

        def keep_warm(n, bank):
            for _ in range(n):
                mm(PS[:, bank, :], ident, consts[:, 0:512], True, True)

        def transpose_h(pe, n):
            for i in range(TT):
                pe.wait_ge(S("h"), 2 * (int(n[1]) - 1) + i + 1)
                for k in range(KD):
                    c = (k % 4) * P
                    last = nc.tensor.transpose(PS[:, 2 * i + k // 4, c:c + P], h[:, i, k * P:(k + 1) * P], ident)
                last.then_inc(S("h_transposed"), 1)

        def router_mm(pe, n, w, ne):
            for i in range(TT):
                pe.wait_ge(S("hT_A" if i else "hT_V"), int(n[1]))
                for k in range(KD):
                    last = mm(PS[:, 4, 64 * i:64 * i + ne], hT[:, k, i * P:(i + 1) * P], w[:, k, :], k == 0, k == KD - 1)
            last.then_inc(S("logits"), 1)

        def positions_mm(pe, n):
            pe.wait_ge(S("mask"), int(n[1]) // 2)
            mm(PS[:, 5, 0:32], C("before"), M[:, 0, :], True, True)
            mm(PS[:, 5, 64:96], C("ones"), M[:, 0, :], True, False)
            mm(PS[:, 5, 64:96], C("before"), M[:, 1, :], False, True)
            mm(PS[:, 5, 128:160], C("ones"), M[:, 0, :], True, False)
            mm(PS[:, 5, 128:160], C("ones"), M[:, 1, :], False, True).then_inc(S("positions"), 1)

        def moe1_gather(pe, X, g):
            pe.wait_ge(S(f"{X}_sel"), g + 1)
            for k in range(KD):
                for i in range(TT):
                    last = mm(PS[:, 0, k * CAP:(k + 1) * CAP], h[:, i, k * P:(k + 1) * P],
                              selS[:, i * CAP:(i + 1) * CAP], i == 0, i == TT - 1)
            last.then_inc(S(f"{X}_gath_done"), 1)

        def moe1_pe(pe, X, it, g, arrived, meanwhile=None):
            pe.wait_ge(S(f"{X}_sel"), g + 1)
            pe.wait_ge(S(f"{X}_xg"), g + 1)
            for i in range(TT):
                last = nc.tensor.transpose(PS[:, 0, i * P:(i + 1) * P], selW[:, i * P:(i + 1) * P], ident)
            last.then_inc(S(f"{X}_swt_done"), 1)
            arrived(pe, "bias")
            for b in range(2):
                for half in range(2):
                    c = half * 1024 + b * 512
                    mm(PS[64 * half:64 * half + 64, 2 + b, :], C("ones")[0:1, 0:CAP], brow[:, c:c + 512], True, False)
            for i in range(4):
                arrived(pe, i)
                w = moe1_dst(i)
                for kk in range(2):
                    k = 2 * i + kk
                    for b in range(2):
                        for half in range(2):
                            c = half * 1024 + b * 512
                            last = mm(PS[64 * half:64 * half + 64, 2 + b, :], xg1[:, k * CAP:(k + 1) * CAP],
                                      w[:, kk, c:c + 512], False, k == KD - 1)
                last.then_inc(S(f"{X}_up_done"), 1)
            pe.wait_ge(S(f"{X}_swt"), it + 1)
            moe1_gather(pe, X, g + 1)
            pe.wait_ge(S(f"{X}_act"), it + 1)
            for i in range(4):
                last = nc.tensor.transpose(PS[:, 1, i * P:(i + 1) * P], actb[:, i * P:(i + 1) * P], ident)
            last.then_inc(S(f"{X}_at_done"), 1)
            if meanwhile:
                meanwhile()
            pe.wait_ge(S(f"{X}_aT"), it + 1)
            for i in range(2):
                arrived(pe, 4 + i)
                w = moe1_dst(4 + i)
                for kk in range(4):
                    for dh in range(2):
                        c = kk * P + i * CAP
                        last = mm(PS[64 * dh:64 * dh + 64, 1, :], aT[:, c:c + CAP], w[:, kk, dh * 512:(dh + 1) * 512],
                                  i == 0 and kk == 0, i == 1 and kk == 3)
                last.then_inc(S(f"{X}_down_done"), 1)
            pe.wait_ge(S(f"{X}_ye"), it + 1)
            pe.wait_ge(S(f"{X}_acc"), it + 1)
            for i in range(TT):
                for dh in range(2):
                    q = slice(64 * dh, 64 * dh + 64)
                    last = mm(PS[:, 4 + 2 * i + dh, :], swT[q, i * P:(i + 1) * P], ye[q, 0:512], True, True)
            last.then_inc(S(f"{X}_scat_done"), 1)

        def moe2_gather(pe, X, g):
            pe.wait_ge(S(f"{X}_sel"), g + 1)
            for k in range(KD):
                for i in range(TT):
                    last = mm(PS[:, k // 4, (k % 4) * P:(k % 4 + 1) * P], h[:, i, k * P:(k + 1) * P],
                              selS[:, i * P:(i + 1) * P], i == 0, i == TT - 1)
            last.then_inc(S(f"{X}_gath_done"), 1)

        def moe2_pe(pe, X, it, g, arrived):
            pe.wait_ge(S(f"{X}_sel"), g + 1)
            pe.wait_ge(S(f"{X}_xg"), g + 1)
            for i in range(TT):
                last = nc.tensor.transpose(PS[:, 0, i * P:(i + 1) * P], selW[:, i * P:(i + 1) * P], ident)
            last.then_inc(S(f"{X}_swt_done"), 1)
            for i in range(2):
                arrived(pe, 2 * i)
                arrived(pe, 2 * i + 1)
                for k in range(KD):
                    for j in range(4):
                        q = slice(CAP2 * j, CAP2 * (j + 1))
                        last = nc.tensor.matmul(PS[q, 2 + i, 0:256], xg2[:, k * P + CAP2 * j:k * P + CAP2 * (j + 1)],
                                                moe2_dst(2 * i + j // 2)[:, 8 * (j % 2) + k, :],
                                                start=k == 0, stop=k == KD - 1, tile_position=(0, CAP2 * j))
                last.then_inc(S(f"{X}_gu_done"), 1)
            pe.wait_ge(S(f"{X}_swt"), it + 1)
            moe2_gather(pe, X, g + 1)
            pe.wait_ge(S(f"{X}_act"), it + 1)
            for i in range(2):
                last = nc.tensor.transpose(PS[:, 2, i * P:(i + 1) * P], actb[:, i * P:(i + 1) * P], ident)
            last.then_inc(S(f"{X}_at_done"), 1)
            pe.wait_ge(S(f"{X}_aT"), it + 1)
            pe.wait_ge(S(f"{X}_xg"), g + 2)
            arrived(pe, 4)
            arrived(pe, 5)
            for kk in range(2):
                for b in range(2):
                    for j in range(4):
                        q = slice(CAP2 * j, CAP2 * (j + 1))
                        last = nc.tensor.matmul(PS[q, b, :], aT[:, kk * P + CAP2 * j:kk * P + CAP2 * (j + 1)],
                                                moe2_dst(4 + j // 2)[:, 2 * (j % 2) + kk, b * 512:(b + 1) * 512],
                                                start=kk == 0, stop=kk == 1, tile_position=(0, CAP2 * j))
            last.then_inc(S(f"{X}_down_done"), 1)
            pe.wait_ge(S(f"{X}_ye"), it + 1)
            pe.wait_ge(S(f"{X}_acc"), it + 1)
            for i in range(TT):
                for b in range(2):
                    last = mm(PS[:, 4 + 2 * i + b, :], swT[:, i * P:(i + 1) * P], ye[:, b * 512:(b + 1) * 512], True, True)
            last.then_inc(S(f"{X}_scat_done"), 1)

        V = nc.vector

        def bc_mid(a, n):
            return a.rearrange("p (o w) -> p o w", o=1).broadcast_to([a.shape[0], n, a.shape[1]])

        def bc_last(a, n):
            return a.rearrange("p (g o) -> p g o", o=1).broadcast_to([a.shape[0], a.shape[1], n])

        def moe1_select(X, e, iota):
            for i in range(TT):
                V.tensor_scalar(selS[:, i * CAP:(i + 1) * CAP], iota, SL[:, i, bass.ds(e, 1)], None, ALU.is_equal)
                last = V.tensor_scalar(selW[:, i * P:(i + 1) * P].rearrange("p (a w) -> p a w", a=2), bc_mid(iota, 2),
                                       SL[:, i, bass.ds(e, 1)], G[:, i, bass.ds(e, 1)], ALU.is_equal, ALU.mult)
            last.then_inc(S(f"{X}_sel"), 1)

        def moe1_dve(v, X, it, e, g, iota, meanwhile=None):
            v.wait_ge(S(f"{X}_swt_done"), it + 1)
            V.tensor_copy(swT, PS[:, 0, 0:256]).then_inc(S(f"{X}_swt"), 1)
            v.wait_ge(S(f"{X}_gath_done"), g + 1)
            moe1_select(X, e + 1, iota)
            v.wait_ge(S(f"{X}_up_done"), 4 * it + 4)
            hu = PS[:, 2:4, :].rearrange("p b (n two) -> p b n two", two=2)
            V.tensor_scalar(glu.rearrange("p (b n) -> p b n", b=2), hu[:, :, :, 0], 7.0, None, ALU.min)\
                .then_inc(S(f"{X}_glu"), 1)
            V.tensor_scalar(lin.rearrange("p (b n) -> p b n", b=2), hu[:, :, :, 1], 7.0, -7.0, ALU.min, ALU.max)\
                .then_inc(S(f"{X}_lin"), 1)
            v.wait_ge(S(f"{X}_glu"), it + 1)
            v.wait_ge(S(f"{X}_lin"), 2 * it + 1)
            V.scalar_tensor_tensor(out=lin, in0=lin, scalar=1.0, in1=glu, op0=ALU.add, op1=ALU.mult)\
                .then_inc(S(f"{X}_lin"), 1)
            v.wait_ge(S(f"{X}_lin"), 2 * it + 2)
            v.wait_ge(S(f"{X}_sg"), it + 1)
            V.tensor_tensor(actb, lin, sg, ALU.mult).then_inc(S(f"{X}_act"), 1)
            v.wait_ge(S(f"{X}_at_done"), it + 1)
            V.tensor_copy(aT, PS[:, 1, :]).then_inc(S(f"{X}_aT"), 1)
            if meanwhile:
                meanwhile()
            v.wait_ge(S(f"{X}_scat_done"), it + 1)
            v.wait_ge(S(f"{X}_acc"), it + 1)
            V.tensor_tensor(acc, acc, PS[:, 4:8, :].rearrange("p b n -> p (b n)"), ALU.add).then_inc(S(f"{X}_acc"), 1)

        def moe2_select(X, e0, iota):
            for i in range(TT):
                for j in range(4):
                    c = i * P + j * CAP2
                    col = bass.ds(e0 + j, 1)
                    V.tensor_scalar(selS[:, c:c + CAP2], iota, SL[:, i, col], None, ALU.is_equal)
                    last = V.tensor_scalar(selW[:, c:c + CAP2], iota, SL[:, i, col], G[:, i, col], ALU.is_equal, ALU.mult)
            last.then_inc(S(f"{X}_sel"), 1)

        def moe2_dve(v, X, it, quad, g, iota):
            v.wait_ge(S(f"{X}_swt_done"), it + 1)
            V.tensor_copy(swT, PS[:, 0, 0:256]).then_inc(S(f"{X}_swt"), 1)
            v.wait_ge(S(f"{X}_gath_done"), g + 1)
            moe2_select(X, 4 * quad + 4, iota)
            v.wait_ge(S(f"{X}_sg"), it + 1)
            V.tensor_tensor(glu[:, 0:256], PS[:, 2, 0:256], sg[:, 0:256], ALU.mult).then_inc(S(f"{X}_glu"), 1)
            v.wait_ge(S(f"{X}_glu"), it + 1)
            v.wait_ge(S(f"{X}_gu_done"), 2 * it + 2)
            V.tensor_tensor(actb[:, 0:256], glu[:, 0:256], PS[:, 3, 0:256], ALU.mult).then_inc(S(f"{X}_act"), 1)
            v.wait_ge(S(f"{X}_at_done"), it + 1)
            V.tensor_copy(aT[:, 0:256], PS[:, 2, 0:256]).then_inc(S(f"{X}_aT"), 1)
            v.wait_ge(S(f"{X}_scat_done"), it + 1)
            v.wait_ge(S(f"{X}_acc"), it + 1)
            V.tensor_tensor(acc, acc, PS[:, 4:8, :].rearrange("p b n -> p (b n)"), ALU.add).then_inc(S(f"{X}_acc"), 1)

        @block.sync
        def _(sp):
            sp.wait_ge(S("rows"), 64)
            sp.wait_ge(S("consts"), 16)
            for u, d in enumerate(PRE):
                if u >= NSLOT:
                    wait(sp, unit_free(before_in_slot(u)))
                unit_load(sp, u, d)
            for i in range(6):
                wait(sp, unit_free(before_in_slot(MOE1 + i)))
                sp.dma_start(moe1_dst(i), moe1_src(0, i)).then_inc(S(f"loaded{SLOT_OF[MOE1 + i]}"), 16)
            sp.wait_ge(S("m1_brow_free"), 1)
            sp.dma_start(brow, t["b_up"][0, 0:1, :]).then_inc(S("m1_brow"), 16)
            with sp.Fori(1, NE) as e:
                for i in range(6):
                    if i < 4:
                        sp.wait_ge(S("m1_up_done"), 4 * e + (i - 3))
                    else:
                        sp.wait_ge(S("m1_down_done"), 2 * e + (i - 5))
                    if i == 0:
                        sp.dma_start(brow, t["b_up"][0, bass.ds(e, 1), :]).then_inc(S("m1_brow"), 16)
                    sp.dma_start(moe1_dst(i), moe1_src(e, i)).then_inc(S(f"loaded{SLOT_OF[MOE1 + i]}"), 16)
            sp.wait_ge(S("m1_flag"), 1)
            more = sp.value_load(flag[0:1, 0:1], min_val=0, max_val=SEQ)
            sp.wait_ge(S("m1_down_done"), 2 * NE)
            with sp.If(more > CAP):
                with sp.Fori(0, EXTRA) as p:
                    with sp.Fori(0, NE) as e:
                        sp.wait_ge(S("m1_scat_done"), NE * (p + 1) + e)
                        sp.dma_start(brow, t["b_up"][0, bass.ds(e, 1), :]).then_inc(S("x1_loaded"), 16)
                        for i in range(6):
                            sp.dma_start(moe1_dst(i), moe1_src(e, i)).then_inc(S("x1_loaded"), 16)
                sp.wait_ge(S("m1_scat_done"), NE * (EXTRA + 1))
            for n, d in enumerate(MID):
                wait(sp, unit_free(before_in_slot(MID0 + n)))
                unit_load(sp, MID0 + n, d)
            for i in range(6):
                if i < 4:
                    wait(sp, unit_free(before_in_slot(MOE2 + i)))
                elif i == 4:
                    sp.wait_ge(S("big_done"), len(ROUNDS))
                sp.dma_start(moe2_dst(i), moe2_src(0, i)).then_inc(S(f"loaded{SLOT_OF[MOE2 + i]}"), 16)
            with sp.Fori(1, NE // 4) as q:
                for i in range(6):
                    if i < 4:
                        sp.wait_ge(S("m2_gu_done"), 2 * q + (i // 2 - 1))
                    else:
                        sp.wait_ge(S("m2_down_done"), q)
                    sp.dma_start(moe2_dst(i), moe2_src(q, i)).then_inc(S(f"loaded{SLOT_OF[MOE2 + i]}"), 16)
            sp.wait_ge(S("m2_flag"), 1)
            more = sp.value_load(flag[0:1, 1:2], min_val=0, max_val=SEQ)
            sp.wait_ge(S("m2_down_done"), NE // 4)
            with sp.If(more > CAP2):
                with sp.Fori(0, EXTRA2) as p:
                    with sp.Fori(0, NE // 4) as q:
                        sp.wait_ge(S("m2_scat_done"), (NE // 4) * (p + 1) + q)
                        for i in range(6):
                            sp.dma_start(moe2_dst(i), moe2_src(q, i)).then_inc(S("x2_loaded"), 16)
                sp.wait_ge(S("m2_scat_done"), (NE // 4) * (EXTRA2 + 1))
            sp.wait_ge(S("result"), 1)
            sp.dma_start(out[0].rearrange("(t p) d -> p t d", p=P), x[:, :, :]).then_inc(S("stored"), 16)
            sp.wait_ge(S("stored"), 16)

        @block.gpsimd
        def _(pool):
            def bc(src):
                return src.partition_broadcast(P)

            def small_load(dst, src, name):
                pool.dma_start(dst, src).then_inc(S(name), 16)

            small_load(sm("hg_gain"), bc(t["hg_norm_gain"][0]), "smalls")
            small_load(sm("q_gain"), bc(t["q_norm_gain"][0]), "smalls")
            small_load(sm("k_gain"), bc(t["k_norm_gain"][0]), "smalls")
            small_load(sm("q_gain2"), bc(t["q_norm_g_2"][0]), "smalls")
            small_load(sm("k_gain2"), bc(t["k_norm_g_2"][0]), "smalls")
            small_load(sm("sink"), bc(t["attn_sinks"][0]), "smalls")
            small_load(sm("b_r1"), bc(t["b_router"][0]), "smalls")
            small_load(sm("b_r2", 4), bc(t["b_router_group_2"][0]), "smalls")
            small_load(sm("b_r2")[:, 4:36], bc(t["b_router_expert_2"][0]), "smalls")
            small_load(sm("w_r1").rearrange("p (k n) -> p k n", k=KD),
                       t["w_router"][0].rearrange("(k p) n -> p k n", p=P), "smalls")
            wr2 = sm("w_r2").rearrange("p (k n) -> p k n", k=KD)
            small_load(wr2[:, :, 0:4], t["w_router_group_2"][0].rearrange("(k p) n -> p k n", p=P), "smalls")
            small_load(wr2[:, :, 4:36], t["w_router_expert_2"][0].rearrange("(k p) n -> p k n", p=P), "smalls")
            pool.wait_ge(S("gain_free"), 1)
            small_load(gain, bc(t["norm2_gain"][0]), "gain")
            pool.wait_ge(S("m1_brow_free"), 1)
            small_load(at(MMAP, "bdown")[0:NE, 0:D], t["b_down"][0], "bdown")
            pool.wait_ge(S("gain_free"), 2)
            small_load(gain, bc(t["norm_mix_g_2"][0]), "gain")
            pool.wait_ge(S("gain_free"), 3)
            small_load(at(A2MAP, "gain"), bc(t["norm_ffn_g_2"][0]), "ffn_gain")

        NSMALLS = 12 * 16
        lb_rows = t["lower_bound_logits"].rearrange("l (h k) -> (l h) k", k=P)
        conv_rows = t["conv_w_2"][0].rearrange("j (m k) -> (j m) k", k=P)

        @block.scalar
        def _(act):
            A = nc.scalar.activation
            act.dma_start(consts[:, :], t["consts"]).then_inc(S("consts"), 16)
            act.dma_start(rows[0:8, :], t["c"][0].rearrange("(k p) -> k p", p=P)).then_inc(S("rows"), 16)
            act.dma_start(rows[8:16, :], lb_rows).then_inc(S("rows"), 16)
            act.dma_start(rows[16:28, :], conv_rows).then_inc(S("rows"), 16)
            act.dma_start(rows[28:36, :], t["norm1_gain"][0].rearrange("(k p) -> k p", p=P)).then_inc(S("rows"), 16)
            act.dma_start(x[:, :, :], t["x"][0].rearrange("(t p) d -> p t d", p=P)).then_inc(S("x"), 16)
            act.dma_start(pos[64:66, :], t["positions"][0].rearrange("(t p) -> t p", p=P)).then_inc(S("pos"), 16)
            act.wait_ge(S("modrow_zero"), 1)
            for j in range(4):
                act.dma_start(modrow[32 * j:32 * j + 1, :, :],
                              t["b_ada"].rearrange("o (b j n) -> o b j n", b=3, j=4)[:, :, j, :]).then_inc(S("b_ada"), 16)

            act.wait_ge(S("x"), 16)
            for i in range(TT):
                A(hT[:, 4 * i:4 * i + 4, :], x[:, i, :].rearrange("p (k n) -> p k n", k=4), ACT.Square,
                  accum_out=sm("ss")[:, i:i + 1]).then_inc(S("squares"), 1)
            act.wait_ge(S("cols"), 1)
            A(sm("cond"), sm("cols", 8), ACT.Sigmoid).then_inc(S("sig_c"), 1)
            act.wait_ge(S("lbd"), 1)
            A(sm("lb"), sm("lbd"), ACT.Sigmoid).then_inc(S("lb"), 1)
            act.wait_ge(S("mean_square"), 1)
            nc.scalar.sqrt(sm("rs"), sm("ss")[:, 0:2]).then_inc(S("rms"), 1)
            act.wait_ge(S("angles"), 2)
            A(sm("sin"), sm("rr"), ACT.Sin).then_inc(S("sincos"), 1)
            A(sm("cos"), sm("rn"), ACT.Sin).then_inc(S("sincos"), 1)
            act.wait_ge(S("h_transposed"), 2)
            act.wait_ge(S("modT"), 1)
            for k in range(KD):
                last = A(hT[:, k, P:SEQ], PS[:, 2 + k // 4, (k % 4) * P:(k % 4 + 1) * P], ACT.Identity,
                         scale=sm("scaleT")[:, k:k + 1], bias=sm("shiftT")[:, k:k + 1])
            last.then_inc(S("hT_A"), 1)
            act.wait_ge(S("att_ms"), 1)
            nc.scalar.sqrt(sm("rsa", 24), sm("ssa", 24)).then_inc(S("att_std"), 1)
            act.wait_ge(S("big_done"), 3)
            A(at(A1MAP, "b"), PS[:, banks(2), :], ACT.Sigmoid).then_inc(S("big_free_A"), 1)
            act.wait_ge(S("forget"), 4)
            A(at(A1MAP, "b"), at(A1MAP, "k"), ACT.Ln).then_inc(S("log_f"), 1)
            act.wait_ge(S("b_ready"), 1)
            A(at(A1MAP, "tmp"), at(A1MAP, "b"), ACT.Exp).then_inc(S("hg_expb"), 1)
            for n in range(5):
                act.wait_ge(S("hg_arg"), n + 1)
                A(HG_EXPS[n], HG_EXPS[n], ACT.Exp).then_inc(S("hg_exp"), 1)
            act.wait_ge(S("big_done"), 4)
            A(at(A1MAP, "q"), PS[:, banks(3), :], ACT.Sigmoid).then_inc(S("sig_q"), 1)
            act.wait_ge(S("att_nm"), 1)
            s = at(A1MAP, "s").rearrange("p (h n) -> p h n", h=AH)
            for hh in range(AH):
                A(s[:, hh, 0:P], s[:, hh, 0:P], ACT.Exp, bias=sm("nm")[:, hh:hh + 1],
                  accum_out=sm("den")[:, hh:hh + 1]).then_inc(S("att_exp"), 1)
                A(s[:, hh, P:3 * P], s[:, hh, P:3 * P], ACT.Exp, bias=sm("nm")[:, 8 + hh:9 + hh],
                  accum_out=sm("den")[:, 8 + hh:9 + hh]).then_inc(S("att_exp"), 1)
            A(sm("es"), sm("es"), ACT.Exp).then_inc(S("att_exp"), 1)
            act.wait_ge(S("hg_arg"), 6)
            for buf in HG_EXPS[5:]:
                A(buf, buf, ACT.Exp).then_inc(S("hg_exp"), 1)
            act.wait_ge(S("big_done"), 5)
            A(at(A1MAP, "v"), PS[:, banks(4), :], ACT.Copy).then_inc(S("big_free_A"), 1)
            act.wait_ge(S("big_done"), 6)
            act.wait_ge(S("att_pT"), 6)
            A(at(A1MAP, "gs"), PS[:, banks(5), :], ACT.Sigmoid).then_inc(S("sig_g"), 1)
            for n in range(3):
                gate_sig(act, 6 + n, n, A1MAP)
            act.wait_ge(S("hgo_ms"), 1)
            nc.scalar.sqrt(sm("rsh"), sm("ssh")).then_inc(S("hgo_std"), 1)
            gate_sig(act, 9, 3, A1MAP)
            rms_sums(act, "n2", hT)
            hT_copy_act(act, "n2")
            for i in range(TT):
                act.wait_ge(S("r1_arg"), i + 1)
                A(EX[:, i, 0:4], EX[:, i, 0:4], ACT.Exp, accum_out=ESUM[:, i:i + 1])\
                    .then_inc(S("r1_exp"), 1)
            moe1_act_gather(act, "m1", 0)
            with act.Fori(0, NE) as e:
                moe1_act(act, "m1", e, e)
            act.wait_ge(S("m1_flag"), 1)
            more = act.value_load(flag[0:1, 0:1], min_val=0, max_val=SEQ)
            with act.If(more > CAP):
                with act.Fori(0, EXTRA) as p:
                    moe1_act_gather(act, "m1", (NE + 1) * (p + 1))
                    with act.Fori(0, NE) as e:
                        moe1_act(act, "m1", NE * (p + 1) + e, (NE + 1) * (p + 1) + e)
            rms_sums(act, "n3", hT)
            split_upper(act, 1)
            act.wait_ge(S("h_transposed"), 6)
            A(hT_up[:, :, P:256], PS[:, 2:4, :].rearrange("p b (k n) -> p (b k) n", n=P), ACT.Copy).then_inc(S("hT_A"), 1)
            for n in range(2, 8):
                split_upper(act, n)
            act.wait_ge(S("big_done"), R2 + 3)
            A(at(A2MAP, "v"), PS[:, banks(R2 + 2), :], ACT.Copy).then_inc(S("big_free_A"), 1)
            split_upper(act, 8)
            act.wait_ge(S("sb_ms"), 1)
            nc.scalar.sqrt(sm("rsa"), sm("ssa")).then_inc(S("sb_std"), 1)
            for n in range(9, 15):
                split_upper(act, n)
            z = at(A2MAP, "z")
            sp_ = at(A2MAP, "sp")
            for g in range(2):
                act.wait_ge(S("sb_z"), g + 1)
                c = slice(1536 * g, 1536 * (g + 1))
                A(sp_[:, c], z[:, c], ACT.Abs).then_inc(S("sb_e"), 1)
                act.wait_ge(S("sb_e"), 2 * g + 1)
                A(sp_[:, c], sp_[:, c], ACT.Exp, scale=-1.0).then_inc(S("sb_e"), 1)
                act.wait_ge(S("sb_e"), 2 * g + 2)
                A(sp_[:, c], sp_[:, c], ACT.Ln, bias=C("ones")[:, 0:1]).then_inc(S("sb_ln"), 1)
                split_upper(act, 15 + g)
            gate_sig(act, R2 + 6, 0, A2MAP)
            split_upper(act, 17)
            gate_sig(act, R2 + 7, 1, A2MAP)
            split_upper(act, 18)
            split_upper(act, 19)
            gate_sig(act, R2 + 8, 2, A2MAP)
            split_upper(act, 20)
            for g in range(2):
                act.wait_ge(S("sb_d"), g + 1)
                c = slice(1536 * g, 1536 * (g + 1))
                A(z[:, c], z[:, c], ACT.Exp).then_inc(S("sb_a"), 1)
            split_upper(act, 21)
            gate_sig(act, R2 + 9, 3, A2MAP)
            for n in range(22, 25):
                split_upper(act, n)
            for n in range(2):
                act.wait_ge(S("merged2"), n + 1)
                A(hT_up[:, 4 * n:4 * n + 4, :], at(A2MAP, "gates", 1024 * n, 1024).rearrange("p (k t) -> p k t", k=4),
                  ACT.Copy).then_inc(S("merged_upper"), 1)
                if n == 0:
                    split_upper(act, 25)
            split_upper(act, 26)
            split_upper(act, 27)
            rms_sums(act, "n4", at(A2MAP, "gates", 0, 2048).rearrange("p (k t) -> p k t", k=KD))
            hT_copy_act(act, "n4")
            act.wait_ge(S("r2_arg"), TT)
            for i in range(TT):
                A(GEX[:, i, 0:4], GEX[:, i, 0:4], ACT.Exp, accum_out=GSUM[:, i:i + 1])\
                    .then_inc(S("r2_exp"), 1)
                A(EX[:, i, 0:2], EX[:, i, 0:2], ACT.Exp, accum_out=ESUM[:, i:i + 1])\
                    .then_inc(S("r2_exp"), 1)
            moe2_act_gather(act, "m2", 0)
            with act.Fori(0, NE // 4) as q:
                moe2_act(act, "m2", q, q)
            act.wait_ge(S("m2_flag"), 1)
            more = act.value_load(flag[0:1, 1:2], min_val=0, max_val=SEQ)
            with act.If(more > CAP2):
                with act.Fori(0, EXTRA2) as p:
                    moe2_act_gather(act, "m2", (NE // 4 + 1) * (p + 1))
                    with act.Fori(0, NE // 4) as q:
                        moe2_act(act, "m2", (NE // 4) * (p + 1) + q, (NE // 4 + 1) * (p + 1) + q)

        @block.tensor
        def _(pe):
            aux = [0]

            def aux_bank():
                r = aux[0]
                aux[0] += 1
                if r >= 2:
                    pe.wait_ge(S("aux_free"), r - 1)
                return PS[:, 4 + r % 2, :]

            def begin(r):
                wait(pe, loaded(ROUNDS[r][0]))
                if r >= 2:
                    wait(pe, round_free(r - 2))
                return PS[:, banks(r), :], slots[SLOT_OF[ROUNDS[r][0]]]

            def dense_tokens(r, n=512, src=hT):
                o, w = begin(r)
                w = w[:, 0:KD * n].rearrange("p (k n) -> p k n", k=KD)
                for i in range(TT):
                    for k in range(KD):
                        last = mm(o[:, i, 0:n], src[:, k, i * P:(i + 1) * P], w[:, k, :], k == 0, k == KD - 1)
                last.then_inc(S("big_done"), 1)

            def dense_cols(r, src, nk, n, c0=0):
                o, w = begin(r)
                o = o.rearrange("p b (c t) -> p (b c) t", c=2)
                w = w.rearrange("p (k n) -> p k n", k=nk)
                for c in range(4):
                    for k in range(nk):
                        last = mm(o[:, c, :], w[:, k, c0 + c * P:c0 + (c + 1) * P], src[:, k, :], k == 0, k == nk - 1)
                last.then_inc(S("big_done"), 1)

            def split_products(r, product, up, lo, ready):
                if r >= 2:
                    wait(pe, round_free(r - 2))
                ns = pieces_of(r)
                for j, n in enumerate(ns):
                    pe.wait_ge(S("w_lower"), n + 1)
                    if ready:
                        pe.wait_ge(S(ready), j + 1)
                    wu, wl = upper(n), PIECES[n][3]
                    last = product(j, ((up[j], wl), (lo[j], wu), (up[j], wu)), j == 0, j == len(ns) - 1)
                    last.then_inc(S("big_done") if j == len(ns) - 1 else S("half_done"), 1)

            def split_tokens(r, lo0=hT_low[:, 0:4, :], ready=None):
                o = PS[:, banks(r), :]

                def product(j, parts, first, last):
                    for i in range(TT):
                        for k in range(4):
                            for m, (a, w) in enumerate(parts):
                                ins = mm(o[:, i, :], a[:, k, i * P:(i + 1) * P], w[:, k, :],
                                         first and k == 0 and m == 0, last and k == 3 and m == 2)
                    return ins
                split_products(r, product, (hT_up[:, 0:4, :], hT_up[:, 4:8, :]), (lo0, hT_low[:, 4:8, :]), ready)

            def split_cols(r, up=hT_up, lo=hT_low):
                o = PS[:, banks(r), :].rearrange("p b (c t) -> p (b c) t", c=2)

                def product(j, parts, first, last):
                    nk, nc_ = parts[0][1].shape[1], parts[0][1].shape[2] // P
                    for c in range(nc_):
                        for k in range(nk):
                            for m, (a, w) in enumerate(parts):
                                ins = mm(o[:, nc_ * j + c, :], w[:, k, c * P:(c + 1) * P], a[:, k, :],
                                         k == 0 and m == 0, k == nk - 1 and m == 2)
                    return ins
                split_products(r, product, (up, up), (lo, lo), None)

            def ada(n):
                u = ADA[n]
                b, kp = PRE[u][1:]
                wait(pe, loaded(u))
                w = slots[SLOT_OF[u]].rearrange("p (k n) -> p k n", k=2)
                for kk in range(2):
                    k = 2 * kp + kk
                    for j in range(4):
                        last = nc.tensor.matmul(PS[32 * j:32 * j + 32, 7 if b != 1 else 6, :],
                                                sm("cond32")[:, 32 * k:32 * k + 32], w[:, kk, 512 * j:512 * (j + 1)],
                                                start=k == 0, stop=k == KD - 1, tile_position=(0, 32 * j))
                last.then_inc(S("ada_done"), 1)

            def spread_row(j):
                return ident[:, 32 * j:32 * j + 1].broadcast_to([P, P])

            pe.wait_ge(S("consts"), 16)
            pe.wait_ge(S("rows"), 64)
            nc.tensor.transpose(PS[:, 0, 0:36], rows[0:36, :], ident[0:36, 0:36])
            pe.wait_ge(S("posf"), 1)
            nc.tensor.transpose(PS[:, 1, 0:2], rows[64:66, :], ident[64:66, 64:66]).then_inc(S("rowsT"), 1)
            transpose_h(pe, "n1")
            pe.wait_ge(S("cond32"), 1)
            for n in range(4):
                ada(n)
            pe.wait_ge(S("modrow"), 1)
            for c in range(4):
                last = nc.tensor.transpose(PS[:, 4, c * P:(c + 1) * P], modrow[:, 0, c * P:(c + 1) * P], ident)
            last.then_inc(S("mod1"), 1)
            pe.wait_ge(S("hT_V"), 1)
            pe.wait_ge(S("hT_A"), 1)
            dense_tokens(0)
            ada(4)
            dense_tokens(1, 256)
            ada(5)
            dense_cols(2, hT, KD, 512)
            ada(6)
            qk = at(A1MAP, "qk").rearrange("p (t b w) -> p t b w", t=TT, w=P)
            qkT = at(A1MAP, "qkT").rearrange("p (b t) -> p b t", b=6)
            pe.wait_ge(S("att_qk"), 1)
            for r in range(3):
                o = aux_bank()
                for j in range(2):
                    for i in range(TT):
                        last = nc.tensor.transpose(o[:, (2 * j + i) * P:(2 * j + i + 1) * P], qk[:, i, 2 * r + j, :], ident)
                last.then_inc(S("aux_done"), 1)
            dense_cols(3, hT, KD, 512)
            ada(7)
            pe.wait_ge(S("att_qkT"), 3)

            def att_score(o, hh, qtile, keys):
                q = slice(64 * (hh % 2), 64 * (hh % 2) + 64)
                return mm(o, qkT[q, hh // 2, qtile * P:(qtile + 1) * P], qkT[q, 4 + hh // 4, 0:keys], True, True)

            for r in range(2):
                o = aux_bank()
                for j in range(4):
                    last = att_score(o[:, j * P:(j + 1) * P], 2 * j + r, 0, P)
                last.then_inc(S("aux_done"), 1)
            for r in range(4):
                o = aux_bank()
                for j in range(2):
                    last = att_score(o[:, j * 256:(j + 1) * 256], 4 * (r // 2) + r % 2 + 2 * j, 1, 256)
                last.then_inc(S("aux_done"), 1)
            dense_tokens(4)
            ada(8)
            dense_tokens(5)
            ada(9)
            s = at(A1MAP, "s").rearrange("p (h n) -> p h n", h=AH)
            pe.wait_ge(S("att_p"), 1)
            for b in range(3):
                for r in range(2):
                    o = aux_bank()
                    for j in range(4):
                        last = nc.tensor.transpose(o[:, j * P:(j + 1) * P], s[:, 4 * r + j, b * P:(b + 1) * P], ident)
                    last.then_inc(S("aux_done"), 1)
            dense_cols(6, hT, KD, 512)
            ada(10)
            pT0 = at(A1MAP, "pT0").rearrange("p (h q) -> p h q", h=AH)
            pT1 = at(A1MAP, "pT1").rearrange("p (h q) -> p h q", h=AH)
            vv = at(A1MAP, "vv").rearrange("p (t d) -> p t d", t=TT)
            pe.wait_ge(S("att_pT"), 6)
            for r in range(2):
                o = aux_bank().rearrange("p (m t) -> p m t", m=2)
                for j in range(4):
                    hh = 4 * r + j
                    q, kv = slice(64 * (hh % 2), 64 * (hh % 2) + 64), slice(HD * (hh // 4), HD * (hh // 4) + HD)
                    mm(o[q, j // 2, :], vv[:, 0, kv], pT0[:, hh, :], True, False)
                    last = mm(o[q, j // 2, P:256], vv[:, 1, kv], pT1[:, hh, :], False, True)
                last.then_inc(S("aux_done"), 1)
            pe.wait_ge(S("hg_scores_in"), 1)
            o = aux_bank().rearrange("p (g i) -> p g i", g=8)
            qt = at(A1MAP, "qt").rearrange("p (g i) -> p g i", g=16)
            for hc in range(16):
                q0 = 64 * (hc % 2)
                for i in range(4):
                    n = SUB * (i + 1)
                    last = mm(o[q0:q0 + n, hc // 2, SUB * i:SUB * i + SUB], kt_view(i)[:, hc, :],
                              qt[:, hc, SUB * i:SUB * i + SUB], True, True)
            last.then_inc(S("aux_done"), 1)
            dense_cols(7, hT, KD, 512)
            ada(11)
            pe.wait_ge(S("hg_kd"), 1)
            kd = at(A1MAP, "b").rearrange("p (h t) -> p h t", h=HH)
            kdT = at(A1MAP, "kdT").rearrange("p (t h k) -> p t h k", t=TT, h=HH)
            vals = at(A1MAP, "v").rearrange("p (t h v) -> p t h v", t=TT, h=HH)
            for i in range(TT):
                o = aux_bank()
                for hh in range(HH):
                    last = nc.tensor.transpose(o[:, hh * P:(hh + 1) * P], kd[:, hh, i * P:(i + 1) * P], ident)
                last.then_inc(S("aux_done"), 1)
            for c in range(3):
                i, q = c // 2, slice(64 * (c % 2), 64 * (c % 2) + 64)
                o = aux_bank()
                pe.wait_ge(S("hg_kdT"), i + 1)
                for hh in range(HH):
                    last = mm(o[:, hh * P:(hh + 1) * P], kdT[q, i, hh, :], vals[q, i, hh, :], True, True)
                last.then_inc(S("aux_done"), 1)
            dense_cols(8, hT, KD, 512)
            st = at(A1MAP, "st").rearrange("p (h t i) -> p h t i", h=HH, t=TT)
            qb = at(A1MAP, "q").rearrange("p (h t) -> p h t", h=HH)
            states = at(A1MAP, "state").rearrange("p (c h v) -> p c h v", c=3, h=HH)
            pe.wait_ge(S("hg_st"), 1)
            for i in range(TT):
                o = aux_bank()
                for par in range(2):
                    c, q = 2 * i + par, slice(64 * par, 64 * par + 64)
                    if c:
                        pe.wait_ge(S("hg_state"), c)
                    for hh in range(HH):
                        oo = o[q, hh * P:(hh + 1) * P]
                        last = mm(oo, st[q, hh, i, :], vals[q, i, hh, :], True, c == 0)
                        if c:
                            last = mm(oo, qb[:, hh, c * CH:(c + 1) * CH], states[:, c - 1, hh, :], False, True)
                last.then_inc(S("aux_done"), 1)
            dense_cols(9, hT, KD, 512)

            def spread(b, j):
                mm(aux_bank(), spread_row(j), modrow[:, b, :], True, True).then_inc(S("aux_done"), 1)

            pe.wait_ge(S("modrow"), 3)
            for j in range(4):
                spread(1, j)
            pe.wait_ge(S("hg_out"), 1)
            ho = at(A1MAP, "o").rearrange("p (t h v) -> p t h v", t=TT, h=HH)
            for r in range(2):
                o = aux_bank()
                for j in range(2):
                    for i in range(TT):
                        last = nc.tensor.transpose(o[:, (2 * j + i) * P:(2 * j + i + 1) * P], ho[:, i, 2 * r + j, :], ident)
                last.then_inc(S("aux_done"), 1)
            for j in range(2, 4):
                spread(2, j)
            pe.wait_ge(S("att_oT"), 2)
            attT = at(A1MAP, "attT").rearrange("p (m t) -> p m t", m=4)
            dense_cols(10, attT, 4, D)
            dense_cols(11, attT, 4, D, 512)
            pe.wait_ge(S("hg_oT"), 2)
            oT = at(A1MAP, "oT").rearrange("p (h t) -> p h t", h=HH)
            dense_cols(12, oT, 4, D)
            dense_cols(13, oT, 4, D, 512)
            for j in range(2):
                spread(2, j)
            pe.wait_ge(S("merged"), 1)
            merged = at(A1MAP, "gates", 0, 2048).rearrange("p (k t) -> p k t", k=KD)
            dense_tokens(14, src=merged)
            dense_tokens(15, src=merged)
            keep_warm(7, 7)
            transpose_h(pe, "n2")
            router_mm(pe, "n2", sm("w_r1").rearrange("p (k n) -> p k n", k=KD), NE)
            keep_warm(4, 7)
            positions_mm(pe, "n2")
            keep_warm(1, 7)
            pe.wait_ge(S("weights"), 1)
            for i in range(TT):
                last = nc.tensor.transpose(PS[0:NE, 6, i * P:(i + 1) * P], G[:, i, 0:NE], ident)
            last.then_inc(S("gT"), 1)
            moe1_gather(pe, "m1", 0)

            def bias_rows():
                pe.wait_ge(S("gT_copy"), 1)
                pe.wait_ge(S("bdown"), 16)
                for i in range(TT):
                    for b in range(2):
                        last = mm(PS[:, 4 + 2 * i + b, :], GT[:, i * P:(i + 1) * P],
                                  at(MMAP, "bdown")[0:NE, b * 512:(b + 1) * 512], True, True)
                last.then_inc(S("bias_rows"), 1)

            def arrival(e):
                def arrived(pe, i):
                    if i == "bias":
                        pe.wait_ge(S("m1_brow"), 16 * e + 16)
                    else:
                        sl, n = loaded(MOE1 + i)
                        pe.wait_ge(sl, 16 * e + n)
                return arrived

            moe1_pe(pe, "m1", 0, 0, arrival(0), bias_rows)
            with pe.Fori(1, NE) as e:
                moe1_pe(pe, "m1", e, e, arrival(e))
            pe.wait_ge(S("m1_flag"), 1)
            more = pe.value_load(flag[0:1, 0:1], min_val=0, max_val=SEQ)
            with pe.If(more > CAP):
                with pe.Fori(0, EXTRA) as p:
                    moe1_gather(pe, "m1", (NE + 1) * (p + 1))
                    with pe.Fori(0, NE) as e:
                        def arrived(pe, i):
                            if i == "bias":
                                pe.wait_ge(S("x1_loaded"), 112 * (NE * p + e) + 112)
                        moe1_pe(pe, "m1", NE * (p + 1) + e, (NE + 1) * (p + 1) + e, arrived)
            keep_warm(13, 2)
            transpose_h(pe, "n3")
            pe.wait_ge(S("hT_V"), 3)
            pe.wait_ge(S("hT_A"), 3)
            pe.wait_ge(S("hT_lower"), 1)
            r = R2
            for n in range(3):
                split_tokens(r + n)
            split_cols(r + 3)
            split_cols(r + 4)
            qk2 = at(A2MAP, "qk").rearrange("p (t b w) -> p t b w", t=TT, w=P)
            qkT2 = at(A2MAP, "qkT").rearrange("p (b t) -> p b t", b=8)
            pe.wait_ge(S("sb_qk"), 1)
            for n in range(4):
                o = aux_bank()
                for j in range(2):
                    for i in range(TT):
                        last = nc.tensor.transpose(o[:, (2 * j + i) * P:(2 * j + i + 1) * P], qk2[:, i, 2 * n + j, :], ident)
                last.then_inc(S("aux_done"), 1)
            split_cols(r + 5)
            pe.wait_ge(S("sb_qkT"), 4)
            for hh in range(8):
                q, m = slice(64 * (hh % 2), 64 * (hh % 2) + 64), hh // 2
                o = aux_bank()
                mm(o[:, 0:256], qkT2[q, 4 + m, 0:P], qkT2[q, m, :], True, True)
                mm(o[:, 256:384], qkT2[q, 4 + m, P:256], qkT2[q, m, P:256], True, True).then_inc(S("aux_done"), 1)
            for n in range(6, 9):
                split_cols(r + n)
            spv = at(A2MAP, "sp").rearrange("p (h n) -> p h n", h=8)
            for hh in range(8):
                if hh % 4 == 0:
                    pe.wait_ge(S("sb_sp"), hh // 4 + 1)
                o = aux_bank()
                mm(o[:, 0:256], C("from_here"), spv[:, hh, 0:256], True, False)
                mm(o[:, P:256], C("ones"), spv[:, hh, 256:384], False, True)
                mm(o[:, 256:384], C("from_here"), spv[:, hh, 256:384], True, True).then_inc(S("aux_done"), 1)
            split_cols(r + 9)
            pe.wait_ge(S("conv"), 1)
            split_cols(r + 10, cv_up, cv_low)
            za = at(A2MAP, "z").rearrange("p (h n) -> p h n", h=8)
            v2 = at(A2MAP, "v").rearrange("p (t d) -> p t d", t=TT)
            for n in range(2):
                pe.wait_ge(S("sb_w"), n + 1)
                o = aux_bank().rearrange("p (m t) -> p m t", m=2)
                for j in range(4):
                    hh = 4 * n + j
                    q = slice(64 * (hh % 2), 64 * (hh % 2) + 64)
                    mm(o[q, j // 2, :], v2[:, 0, hh * HD:(hh + 1) * HD], za[:, hh, 0:256], True, False)
                    last = mm(o[q, j // 2, P:256], v2[:, 1, hh * HD:(hh + 1) * HD], za[:, hh, 256:384], False, True)
                last.then_inc(S("aux_done"), 1)
            split_cols(r + 11, cv_up, cv_low)
            pe.wait_ge(S("sb_oT"), 2)
            for n in range(2):
                split_cols(r + 12 + n, sb_up, hT_low[:, 0:4, :])
            for n in range(2):
                split_tokens(r + 14 + n, cv_low, "merged_lower" if n == 0 else None)
            keep_warm(6, 7)
            transpose_h(pe, "n4")
            router_mm(pe, "n4", sm("w_r2").rearrange("p (k n) -> p k n", k=KD), 36)
            keep_warm(5, 7)
            positions_mm(pe, "n4")
            keep_warm(4, 7)
            moe2_gather(pe, "m2", 0)
            with pe.Fori(0, NE // 4) as q:
                def arrived(pe, i):
                    sl, n = loaded(MOE2 + i)
                    pe.wait_ge(sl, 16 * q + n)
                moe2_pe(pe, "m2", q, q, arrived)
            pe.wait_ge(S("m2_flag"), 1)
            more = pe.value_load(flag[0:1, 1:2], min_val=0, max_val=SEQ)
            with pe.If(more > CAP2):
                with pe.Fori(0, EXTRA2) as p:
                    moe2_gather(pe, "m2", (NE // 4 + 1) * (p + 1))
                    with pe.Fori(0, NE // 4) as q:
                        def arrived(pe, i):
                            if i == 0:
                                pe.wait_ge(S("x2_loaded"), 96 * ((NE // 4) * p + q) + 96)
                        moe2_pe(pe, "m2", (NE // 4) * (p + 1) + q, (NE // 4 + 1) * (p + 1) + q, arrived)

        @block.vector
        def _(v):
            count, aux = {}, [0]

            def sig(ins, name):
                count[name] = count.get(name, 0) + 1
                ins.then_inc(S(name), 1)
                v.wait_ge(S(name), count[name])

            def L(ins):
                sig(ins, "v_step")

            def aux_bank():
                r = aux[0]
                aux[0] += 1
                v.wait_ge(S("aux_done"), r + 1)
                return PS[:, 4 + r % 2, :]

            def begin(r):
                v.wait_ge(S("big_done"), r + 1)
                return PS[:, banks(r), :]

            TS, TV, STT, CP = V.tensor_scalar, V.tensor_tensor, V.scalar_tensor_tensor, V.tensor_copy

            sig(V.memset(modrow[:, :, :], 0.0), "modrow_zero")
            v.wait_ge(S("pos"), 16)
            sig(CP(rows[64:66, :], pos[64:66, :]), "posf")
            v.wait_ge(S("rowsT"), 1)
            cols = sm("cols")
            CP(sm("posf"), PS[:, 1, 0:2])
            L(CP(cols, PS[:, 0, 0:36]))
            sig(TV(sm("lbd"), cols[:, 8:12], cols[:, 12:16], ALU.subtract), "lbd")
            sig(CP(sm("one_lb"), sm("lbd")), "cols")
            v.wait_ge(S("sig_c"), 1)
            L(TV(sm("cond"), sm("cond"), cols[:, 0:8], ALU.mult))
            sig(CP(sm("cond32").rearrange("p (k m) -> p k m", k=KD), bc_last(sm("cond"), 32)), "cond32")
            v.wait_ge(S("lb"), 1)
            L(TS(sm("one_lb"), sm("lb"), -1.0, 1.0, ALU.mult, ALU.add))
            v.wait_ge(S("squares"), 2)
            sig(TS(sm("ss")[:, 0:2], sm("ss")[:, 0:2], 1.0 / D, EPS, ALU.mult, ALU.add), "mean_square")
            v.wait_ge(S("rms"), 1)
            L(V.reciprocal(sm("rs"), sm("rs")))
            for i in range(TT):
                sig(TS(h[:, i, :], x[:, i, :], sm("rs")[:, i:i + 1], None, ALU.mult), "h")
            v.wait_ge(S("consts"), 16)
            ang, rr, rn = sm("ang"), sm("rr"), sm("rn")
            for i in range(TT):
                last = TS(ang[:, 8 * i:8 * i + 8], C("inv_freq"), sm("posf")[:, i:i + 1], None, ALU.mult)
            L(last)
            ROUND = 12582912.0
            C1 = 6.28125
            C2 = float(np.float32(2 * np.pi - C1))
            C3 = float(np.float32(2 * np.pi - C1 - np.float64(C2)))
            for dst, turn, add in ((rr, 0.0, 0.0), (rn, 0.25, float(np.float32(np.pi / 2)))):
                t_ = sm("cos")
                L(TS(t_, ang, float(np.float32(1 / (2 * np.pi))), turn, ALU.mult, ALU.add))
                L(TS(t_, t_, ROUND, None, ALU.add))
                L(TS(t_, t_, ROUND, None, ALU.subtract))
                L(STT(out=dst, in0=t_, scalar=-C1, in1=ang, op0=ALU.mult, op1=ALU.add))
                L(STT(out=dst, in0=t_, scalar=-C2, in1=dst, op0=ALU.mult, op1=ALU.add))
                L(STT(out=dst, in0=t_, scalar=-C3, in1=dst, op0=ALU.mult, op1=ALU.add))
                L(TS(dst, dst, add, None, ALU.add))
                sig(TS(dst, dst, 3.1415925, -3.1415925, ALU.min, ALU.max), "angles")
            v.wait_ge(S("b_ada"), 64)
            v.wait_ge(S("ada_done"), 4)
            sig(TV(modrow[:, 0, :], modrow[:, 0, :], PS[:, 7, :], ALU.add), "modrow")
            v.wait_ge(S("mod1"), 1)
            mT = PS[:, 4, :].rearrange("p (c n) -> p n c", c=4)
            for j in range(2):
                CP(sm("shiftT")[:, 4 * j:4 * j + 4], mT[:, 32 * j, :])
                last = STT(out=sm("scaleT")[:, 4 * j:4 * j + 4], in0=mT[:, 64 + 32 * j, :], scalar=1.0,
                           in1=cols[:, 28 + 4 * j:32 + 4 * j], op0=ALU.add, op1=ALU.mult)
            sig(last, "modT")
            v.wait_ge(S("h_transposed"), 2)
            for k in range(KD):
                last = TS(hT[:, k, 0:P], PS[:, k // 4, (k % 4) * P:(k % 4 + 1) * P],
                          sm("scaleT")[:, k:k + 1], sm("shiftT")[:, k:k + 1], ALU.mult, ALU.add)
            sig(last, "hT_V")

            def hT_copy_dve(name):
                v.wait_ge(S("h_transposed"), 2 * int(name[1]) - 1)
                sig(CP(hT[:, :, 0:P], PS[:, 0:2, :].rearrange("p b (k n) -> p (b k) n", n=P)), "hT_V")

            flat = "p b n -> p (b n)"
            q, k, b, tmp = (at(A1MAP, n) for n in ("q", "k", "b", "tmp"))
            qk = at(A1MAP, "qk").rearrange("p (t g d) -> p t g d", t=TT, d=HD)
            vv = at(A1MAP, "vv").rearrange("p (t d) -> p t d", t=TT)
            o = begin(0)
            sig(CP(qk[:, :, 0:8, :], o.rearrange("p t (g d) -> p t g d", d=HD)), "big_free_V")
            o = begin(1)
            for i in range(TT):
                for c in range(2):
                    CP(qk[:, i, 8 + c:12:2, :], o[:, i, 0:128].rearrange("p (g d) -> p g d", d=HD))
            sig(CP(vv, o[:, :, 128:256]), "big_free_V")
            v.wait_ge(S("smalls"), NSMALLS)

            def head_norm(qk, nh, sq, gains, name, meanwhile=None):
                w = TT * nh
                flat3 = qk.rearrange("p t g d -> p (t g) d")
                s3 = sq.rearrange("p (g d) -> p g d", d=HD)
                L(TV(s3, flat3, flat3, ALU.mult))
                L(V.reduce_sum(sm("ssa", w), s3, axis=AX))
                sig(TS(sm("ssa", w), sm("ssa", w), 1.0 / HD, EPS, ALU.mult, ALU.add), f"{name}_ms")
                if meanwhile:
                    meanwhile()
                v.wait_ge(S(f"{name}_std"), 1)
                L(V.reciprocal(sm("rsa", w), sm("rsa", w)))
                L(TV(flat3, flat3, bc_last(sm("rsa", w), HD), ALU.mult))
                for i in range(TT):
                    for a, n, g_ in gains:
                        last = TV(qk[:, i, a:a + n, :], qk[:, i, a:a + n, :], bc_mid(sm(g_), n), ALU.mult)
                return last

            L(head_norm(qk, 12, at(A1MAP, "qkT"), [(0, 8, "q_gain"), (8, 4, "k_gain")], "att"))
            v.wait_ge(S("sincos"), 2)
            rt_ = at(A1MAP, "rt")
            for i in range(TT):
                x1, x2 = qk[:, i, :, 0:8], qk[:, i, :, 8:16]
                cs, sn = bc_mid(sm("cos")[:, 8 * i:8 * i + 8], 12), bc_mid(sm("sin")[:, 8 * i:8 * i + 8], 12)
                p4 = [rt_[:, 96 * n + 384 * i:96 * n + 96 + 384 * i].rearrange("p (g d) -> p g d", d=8) for n in range(4)]
                TV(p4[0], x1, cs, ALU.mult)
                TV(p4[1], x2, sn, ALU.mult)
                TV(p4[2], x2, cs, ALU.mult)
                L(TV(p4[3], x1, sn, ALU.mult))
                TV(x1, p4[0], p4[1], ALU.subtract)
                last = TV(x2, p4[2], p4[3], ALU.add)
            sig(last, "att_qk")
            v.wait_ge(S("big_free_A"), 1)
            for i in range(HH):
                c = slice(256 * i, 256 * (i + 1))
                sig(TS(k[:, c], b[:, c], sm("one_lb")[:, i:i + 1], sm("lb")[:, i:i + 1], ALU.mult, ALU.add), "forget")
            for r in range(3):
                sig(CP(at(A1MAP, "qkT", 512 * r, 512), aux_bank()), "att_qkT")
                sig(V.memset(sm("ang"), 0.0), "aux_free")
            reset = at(A1MAP, "reset")
            L(V.memset(reset, 1.0))
            L(V.memset(reset.rearrange("p (g j) -> p g j", g=16)[:, :, 0:1], 0.0))
            v.wait_ge(S("log_f"), 1)
            TS(k, k, -1.0, 1.0, ALU.mult, ALU.add)
            sig(V.tensor_tensor_scan(b, reset, b, 0.0, ALU.mult, ALU.add), "b_ready")
            bg = b.rearrange("p (g j) -> p g j", j=SUB)
            bc_ = b.rearrange("p (g j) -> p g j", j=CH)
            kc = k.rearrange("p (g j) -> p g j", j=CH)
            decay = sm("decay")
            CP(decay, bc_[:, :, CH - 1])
            qt = at(A1MAP, "qt")
            L(TV(qt.rearrange("p (g j) -> p g j", j=SUB), bg, bg[:, :, SUB // 2 - 1:SUB // 2].broadcast_to([P, 64, SUB]),
                 ALU.subtract))
            sig(TS(qt, qt, EXP_CAP, None, ALU.min), "hg_arg")
            for i in range(4):
                n = SUB * (i + 1)
                mid = SUB * i + SUB // 2 - 1
                L(TV(kt_view(i), bc_[:, :, mid:mid + 1].broadcast_to([P, 16, n]), bc_[:, :, 0:n], ALU.subtract))
                sig(TS(kt_view(i), kt_view(i), EXP_CAP, None, ALU.min), "hg_arg")
            s = at(A1MAP, "s").rearrange("p (h n) -> p h n", h=AH)
            wb = C("win_bias")
            for r in range(2):
                o = aux_bank().rearrange("p (h n) -> p h n", h=4)
                sig(STT(out=s[:, r:8:2, 0:P], in0=o, scalar=HD ** -0.5, in1=bc_mid(wb[:, P:256], 4),
                        op0=ALU.mult, op1=ALU.add), "aux_free")
            for r in range(4):
                o = aux_bank().rearrange("p (h n) -> p h n", h=2)
                h0 = 4 * (r // 2) + r % 2
                sig(STT(out=s[:, h0:h0 + 3:2, P:384], in0=o, scalar=HD ** -0.5, in1=bc_mid(wb, 2),
                        op0=ALU.mult, op1=ALU.add), "aux_free")
            m_ = sm("m")
            V.reduce_max(m_[:, 0:8], s[:, :, 0:P], axis=AX)
            L(V.reduce_max(m_[:, 8:16], s[:, :, P:384], axis=AX))
            m2, sink2 = m_.rearrange("p (a h) -> p a h", a=2), bc_mid(sm("sink"), 2)
            L(TV(m2, m2, sink2, ALU.max))
            L(TV(sm("es").rearrange("p (a h) -> p a h", a=2), sink2, m2, ALU.subtract))
            sig(TS(sm("nm"), m_, -1.0, None, ALU.mult), "att_nm")
            o = begin(3)
            v.wait_ge(S("sig_q"), 1)
            sig(TV(q, o.rearrange(flat), q, ALU.mult), "big_free_V")
            v.wait_ge(S("hg_expb"), 1)
            sig(TV(bc_, bc_last(decay, CH), bc_, ALU.subtract), "hg_arg")
            v.wait_ge(S("hg_exp"), 1)
            L(TV(qt, qt, q, ALU.mult))
            L(TV(q, q, tmp, ALU.mult))
            for i in range(4):
                v.wait_ge(S("hg_exp"), i + 2)
                last = TV(kt_view(i), kt_view(i), kc[:, :, 0:SUB * (i + 1)], ALU.mult)
            sig(last, "hg_scores_in")
            v.wait_ge(S("att_exp"), 17)
            L(TV(sm("den"), sm("den"), sm("es"), ALU.add))
            L(V.reciprocal(sm("den"), sm("den")))
            TV(s[:, :, 0:P], s[:, :, 0:P], bc_last(sm("den")[:, 0:8], P), ALU.mult)
            sig(TV(s[:, :, P:384], s[:, :, P:384], bc_last(sm("den")[:, 8:16], 256), ALU.mult), "att_p")
            v.wait_ge(S("hg_exp"), 6)
            sig(TV(b, b, k, ALU.mult), "hg_kd")
            pT0 = at(A1MAP, "pT0").rearrange("p (h q) -> p h q", h=AH)
            pT1 = at(A1MAP, "pT1").rearrange("p (h q) -> p h q", h=AH)
            for b_ in range(3):
                for r in range(2):
                    dst = pT1[:, 4 * r:4 * r + 4, :] if b_ == 2 else pT0[:, 4 * r:4 * r + 4, b_ * P:(b_ + 1) * P]
                    o = aux_bank().rearrange("p (h n) -> p h n", h=4)
                    sig(CP(dst, o), "att_pT")
                    sig(V.memset(sm("ang"), 0.0), "aux_free")
            v.wait_ge(S("sig_g"), 1)
            gs = at(A1MAP, "gs")
            o = begin(5)
            sig(TV(gs, o.rearrange(flat), gs, ALU.mult), "big_free_V")
            L(TV(gs.rearrange("p (g v) -> p g v", g=8), gs.rearrange("p (g v) -> p g v", g=8), bc_mid(sm("hg_gain"), 8),
                 ALU.mult))
            for r in range(2):
                sig(CP(at(A1MAP, "attT", 512 * r, 512), aux_bank()), "att_oT")
                sig(V.memset(sm("ang"), 0.0), "aux_free")
            st = at(A1MAP, "st")
            st8 = st.rearrange("p (g i) -> p g i", g=8)
            L(V.memset(st, 0.0))
            o = aux_bank().rearrange("p (g i) -> p g i", g=8)
            for par in range(2):
                for i in range(4):
                    q_, c = slice(64 * par, 64 * par + SUB * (i + 1)), slice(SUB * i, SUB * (i + 1))
                    mk = C("chunk_causal")[q_, c]
                    last = TV(st8[q_, :, c], o[q_, :, c], bc_mid(mk, 8), ALU.mult)
            last.then_inc(S("hg_st"), 1)
            v.wait_ge(S("hg_st"), 1)
            sig(V.memset(sm("ang"), 0.0), "aux_free")
            kdT = at(A1MAP, "kdT")
            for i in range(TT):
                o = aux_bank()
                last = CP(kdT[:, 512 * i:512 * (i + 1)], o)
                sig(last, "hg_kdT")
                sig(V.memset(sm("ang"), 0.0), "aux_free")
            states = at(A1MAP, "state").rearrange("p (c h v) -> p c h v", c=3, h=HH)
            for c in range(3):
                o = aux_bank().rearrange("p (h v) -> p h v", h=HH)
                if c == 0:
                    sig(CP(states[:, 0], o), "hg_state")
                else:
                    for hh in range(HH):
                        last = STT(out=states[:, c, hh, :], in0=states[:, c - 1, hh, :], scalar=decay[:, 4 * hh + c:4 * hh + c + 1],
                                   in1=o[:, hh, :], op0=ALU.mult, op1=ALU.add)
                    sig(last, "hg_state")
                sig(V.memset(sm("ang"), 0.0), "aux_free")
            v.wait_ge(S("ada_done"), 12)
            sig(TV(modrow[:, 1, :], modrow[:, 1, :], PS[:, 6, :], ALU.add), "modrow")
            sig(TV(modrow[:, 2, :], modrow[:, 2, :], PS[:, 7, :], ALU.add), "modrow")
            ho = at(A1MAP, "o")
            for i in range(TT):
                sig(CP(ho[:, 512 * i:512 * (i + 1)], aux_bank()), "aux_free")
            o8 = ho.rearrange("p (g v) -> p g v", g=8)
            sq8 = at(A1MAP, "qt").rearrange("p (g v) -> p g v", g=8)
            L(TV(sq8, o8, o8, ALU.mult))
            L(V.reduce_sum(sm("ssh"), sq8, axis=AX))
            sig(TS(sm("ssh"), sm("ssh"), 1.0 / 128, EPS, ALU.mult, ALU.add), "hgo_ms")
            v.wait_ge(S("hgo_std"), 1)
            L(V.reciprocal(sm("rsh"), sm("rsh")))
            for g in range(8):
                c = slice(128 * g, 128 * (g + 1))
                last = STT(out=ho[:, c], in0=ho[:, c], scalar=sm("rsh")[:, g:g + 1], in1=gs[:, c], op0=ALU.mult, op1=ALU.mult)
            sig(last, "hg_out")
            sig(V.memset(sm("ang"), 0.0), "m1_brow_free")
            for j in range(2):
                sig(CP(G1[:, 512 * j:512 * (j + 1)], aux_bank()), "aux_free")
            for j in range(2):
                sig(CP(SH2[:, 512 * j:512 * (j + 1)], aux_bank()), "aux_free")
            for r in range(2):
                sig(CP(at(A1MAP, "oT", 512 * r, 512), aux_bank()), "hg_oT")
                sig(V.memset(sm("ang"), 0.0), "aux_free")
            sig(V.memset(sm("ang"), 0.0), "gain_free")
            for j in range(2):
                sig(CP(G2[:, 512 * j:512 * (j + 1)], aux_bank()), "aux_free")

            def merge(r0, m):
                g = at(m, "gates")
                for n in range(4):
                    c = slice(1024 * n, 1024 * (n + 1))
                    o = begin(r0 + n)
                    if n < 2:
                        sig(TV(g[:, c], g[:, c], o.rearrange(flat), ALU.mult), "big_free_V")
                    else:
                        sig(TV(g[:, c], g[:, c], o.rearrange(flat), ALU.mult), "big_free_V")
                sig(TV(g[:, 0:2048], g[:, 0:2048], g[:, 2048:4096], ALU.add), "merged")

            v.wait_ge(S("big_free_A"), 6)
            merge(10, A1MAP)
            v.wait_ge(S("gain"), 16)
            for j in range(2):
                c = slice(512 * j, 512 * (j + 1))
                sig(STT(out=A2[:, c], in0=aux_bank(), scalar=1.0, in1=gain[:, c], op0=ALU.add, op1=ALU.mult), "aux_free")
            sig(V.memset(sm("ang"), 0.0), "gain_free")
            L(V.memset(rt, 0.0))
            L(V.memset(SL, 512.0))
            xt = at(A1MAP, "v")
            for j in range(2):
                c = slice(512 * j, 512 * (j + 1))
                o = begin(14 + j)
                sig(TV(xt.rearrange("p (t n) -> p t n", t=TT), o, bc_mid(G1[:, c], TT), ALU.mult), "big_free_V")
                sig(TV(x[:, :, c], x[:, :, c], xt.rearrange("p (t n) -> p t n", t=TT), ALU.add), "x_ready")
                L(TV(h[:, :, c], x[:, :, c], bc_mid(A2[:, c], TT), ALU.mult))

            def rms(name, squares):
                v.wait_ge(S("squares"), squares)
                ss = sm("ss")
                if name != "n3":
                    L(TV(ss[:, 0:2], ss[:, 0:2], ss[:, 2:4], ALU.add))
                sig(TS(ss[:, 0:2], ss[:, 0:2], 1.0 / D, EPS, ALU.mult, ALU.add), "mean_square")
                v.wait_ge(S("rms"), int(name[1]))
                L(V.reciprocal(sm("rs"), sm("rs")))

            rms("n2", 6)
            for i in range(TT):
                sig(STT(out=h[:, i, :], in0=h[:, i, :], scalar=sm("rs")[:, i:i + 1], in1=SH2, op0=ALU.mult, op1=ALU.add),
                    "h")
            hT_copy_dve("n2")
            v.wait_ge(S("logits"), 1)
            logits = PS[:, 4, 0:64 * TT].rearrange("p (t e) -> p t e", t=TT)
            L(TV(LG[:, :, 0:NE], logits[:, :, 0:NE], bc_mid(sm("b_r1"), TT), ALU.add))
            for i in range(TT):
                L(V.max(V8[:, i, :], LG[:, i, 0:NE]))
                sig(TS(EX[:, i, :], V8[:, i, :], V8[:, i, 0:1], None, ALU.subtract), "r1_arg")
            for i in range(TT):
                last = V.max_index(idx[:, i, :], V8[:, i, :], LG[:, i, 0:NE])
            L(last)
            L(CP(IDF[:, :, :], idx[:, :, :]))

            def ranks(n, e):
                return EQ[:, 0:TT * n * e].rearrange("p (t k e) -> p t k e", t=TT, k=n)

            def one_hots(n, e, mask, weights, done):
                eq = ranks(n, e)
                for i in range(TT):
                    last = TV(eq[:, i], bc_mid(C("iota")[:, 0:e], n), bc_last(IDF[:, i, 0:n], e), ALU.is_equal)
                L(last)
                L(V.reduce_sum(mask, eq.rearrange("p t k e -> p t e k"), axis=AX))
                done()
                for i in range(TT):
                    last = TV(eq[:, i], eq[:, i], bc_last(EX[:, i, 0:n], e), ALU.mult)
                L(last)
                sig(V.reduce_sum(weights, eq.rearrange("p t k e -> p t e k"), axis=AX), "weights")

            def r1_weights():
                sig(V.memset(sm("ang"), 0.0), "mask")
                v.wait_ge(S("r1_exp"), TT)
                L(V.reciprocal(ESUM, ESUM))
                for i in range(TT):
                    last = TS(EX[:, i, 0:4], EX[:, i, 0:4], ESUM[:, i:i + 1], None, ALU.mult)
                L(last)

            one_hots(4, NE, M[:, :, :], G[:, :, 0:NE], r1_weights)

            def slot_numbers(n):
                v.wait_ge(S("positions"), n)
                L(STT(out=SL[:, :, 0:NE], in0=PS[:, 5, 0:64 * TT].rearrange("p (t e) -> p t e", t=TT)[:, :, 0:NE],
                      scalar=-512.0, in1=M[:, :, :], op0=ALU.add, op1=ALU.mult))
                L(TS(SL[:, :, 0:NE], SL[:, :, 0:NE], 512.0, None, ALU.add))

            def largest_count(f, m):
                L(V.reduce_max(CMAX[:, 0:1], PS[:, 5, 128:160], axis=AX))
                sig(CP(flag[:, f:f + 1], CMAX[:, 0:1]), f"{m}_flag")

            slot_numbers(1)
            iota0 = C("iota")[:, 0:CAP]
            moe1_select("m1", 0, iota0)
            largest_count(0, "m1")
            v.wait_ge(S("gT"), 1)
            sig(CP(GT, PS[0:NE, 6, 0:256]), "gT_copy")

            def bias_rows():
                v.wait_ge(S("bias_rows"), 1)
                sig(CP(acc, PS[:, 4:8, :].rearrange(flat)), "m1_acc")

            moe1_dve(v, "m1", 0, 0, 0, iota0, bias_rows)
            with v.Fori(1, NE) as e:
                moe1_dve(v, "m1", e, e, e, iota0)
            v.wait_ge(S("m1_acc"), NE + 1)
            more = v.value_load(flag[0:1, 0:1], min_val=0, max_val=SEQ)
            with v.If(more > CAP):
                with v.Fori(0, EXTRA) as p:
                    iop = C("iota")[:, bass.ds(CAP * p + CAP, CAP)]
                    moe1_select("m1", 0, iop)
                    with v.Fori(0, NE) as e:
                        moe1_dve(v, "m1", NE * (p + 1) + e, e, (NE + 1) * (p + 1) + e, iop)
                v.wait_ge(S("m1_acc"), NE * (EXTRA + 1) + 1)
            for i in range(TT):
                c = slice(D * i, D * (i + 1))
                L(TV(acc[:, c], acc[:, c], G2, ALU.mult))
                sig(TV(x[:, i, :], x[:, i, :], acc[:, c], ALU.add), "x_ready")

            def gained(name, g):
                for i in range(TT):
                    sig(STT(out=h[:, i, :], in0=x[:, i, :], scalar=sm("rs")[:, i:i + 1], in1=g, op0=ALU.mult, op1=ALU.mult),
                        "h")

            rms("n3", 8)
            v.wait_ge(S("gain"), 32)
            gained("n3", gain)
            split_lower(v, 0)
            v.wait_ge(S("h_transposed"), 5)
            o = PS[:, 0:2, :].rearrange("p b (k n) -> p (b k) n", n=P)
            sig(CP(hT_up[:, :, 0:P], o), "hT_V")
            TV(hT_low[:, :, 0:P], o, hT_up[:, :, 0:P], ALU.subtract)
            v.wait_ge(S("hT_A"), 3)
            sig(TV(hT_low[:, :, P:256], PS[:, 2:4, :].rearrange("p b (k n) -> p (b k) n", n=P), hT_up[:, :, P:256],
                   ALU.subtract), "hT_lower")
            for n in range(1, 4):
                split_lower(v, n)
            qk = at(A2MAP, "qk").rearrange("p (t g d) -> p t g d", t=TT, d=HD)
            for n in range(2):
                o = begin(R2 + n)
                sig(CP(qk[:, :, 8 * n:8 * n + 8, :], o.rearrange("p t (g d) -> p t g d", d=HD)), "big_free_V")
                split_lower(v, 4 + 2 * n)
                if n == 0:
                    split_lower(v, 5)
            sig(head_norm(qk, 16, at(A2MAP, "sp", 0, 2048), [(0, 8, "q_gain2"), (8, 8, "k_gain2")], "sb",
                          lambda: split_lower(v, 7)), "sb_qk")
            split_lower(v, 8)
            split_lower(v, 9)
            cb, tmp2, cv = at(A2MAP, "cb"), at(A2MAP, "tmp"), at(A2MAP, "cv")
            o = begin(R2 + 3)
            sig(CP(tmp2, o.rearrange(flat)), "big_free_V")
            split_lower(v, 10)
            split_lower(v, 11)
            cu = at(A2MAP, "cu", 0, 4 * 258).rearrange("p (m t) -> p m t", m=4)
            L(V.memset(cu[:, :, 0:2], 0.0))
            o = begin(R2 + 4)
            sig(TV(cu[:, :, 2:258], o.rearrange("p b (c t) -> p (b c) t", c=2), tmp2.rearrange("p (m t) -> p m t", m=4),
                   ALU.mult), "big_free_V")
            for n in range(4):
                sig(CP(at(A2MAP, "qkT", 512 * n, 512), aux_bank()), "sb_qkT")
                sig(V.memset(sm("ang"), 0.0), "aux_free")
            split_lower(v, 12)
            split_lower(v, 13)
            o = begin(R2 + 5)
            sig(CP(cb, o.rearrange(flat)), "big_free_V")
            z = at(A2MAP, "z")
            z3 = z.rearrange("p (h n) -> p h n", h=8)
            sp_ = at(A2MAP, "sp")
            sp3 = sp_.rearrange("p (h n) -> p h n", h=8)
            before = C("before")
            for hh in range(8):
                o = aux_bank()
                sig(TS(z3[:, hh, :], o[:, 0:384], HD ** -0.5, None, ALU.mult), "aux_free")
                if hh % 4 == 3:
                    sig(V.memset(sm("ang"), 0.0), "sb_z")
            split_lower(v, 14)
            split_lower(v, 15)
            cv3 = cv.rearrange("p (m t) -> p m t", m=4)
            for m in range(4):
                w = [cols[:, 16 + 4 * j + m:17 + 4 * j + m] for j in range(3)]
                L(TS(cv3[:, m, :], cu[:, m, 0:256], w[0], None, ALU.mult))
                L(STT(out=cv3[:, m, :], in0=cu[:, m, 1:257], scalar=w[1], in1=cv3[:, m, :], op0=ALU.mult, op1=ALU.add))
                L(STT(out=cv3[:, m, :], in0=cu[:, m, 2:258], scalar=w[2], in1=cv3[:, m, :], op0=ALU.mult, op1=ALU.add))
            L(TV(cv, cv, cb, ALU.mult))
            L(CP(cv_up, cv3))
            sig(TV(cv_low, cv3, cv_up, ALU.subtract), "conv")
            split_lower(v, 16)
            for g in range(2):
                c, hs = slice(1536 * g, 1536 * (g + 1)), slice(4 * g, 4 * g + 4)
                v.wait_ge(S("sb_ln"), g + 1)
                L(STT(out=sp_[:, c], in0=z[:, c], scalar=0.0, in1=sp_[:, c], op0=ALU.max, op1=ALU.add))
                TV(sp3[:, hs, 0:P], sp3[:, hs, 0:P], bc_mid(before, 4), ALU.mult)
                sig(TV(sp3[:, hs, 256:384], sp3[:, hs, 256:384], bc_mid(before, 4), ALU.mult), "sb_sp")
            for n in range(17, 20):
                split_lower(v, n)
            for hh in range(8):
                o = aux_bank()
                sig(TV(z3[:, hh, :], z3[:, hh, :], o[:, 0:384], ALU.subtract), "aux_free")
                if hh % 4 == 3:
                    c = slice(1536 * (hh // 4), 1536 * (hh // 4 + 1))
                    sig(TS(z[:, c], z[:, c], 0.0, None, ALU.min), "sb_d")
            split_lower(v, 20)
            for g in range(2):
                hs = slice(4 * g, 4 * g + 4)
                v.wait_ge(S("sb_a"), g + 1)
                TV(z3[:, hs, 0:P], z3[:, hs, 0:P], bc_mid(before, 4), ALU.mult)
                sig(TV(z3[:, hs, 256:384], z3[:, hs, 256:384], bc_mid(before, 4), ALU.mult), "sb_w")
            split_lower(v, 21)
            split_lower(v, 22)
            v.wait_ge(S("big_free_A"), 11)
            g = at(A2MAP, "gates")

            def gated(n):
                c = slice(1024 * n, 1024 * (n + 1))
                sig(TV(g[:, c], g[:, c], begin(R2 + 10 + n).rearrange(flat), ALU.mult), "big_free_V")
                if n < 2:
                    split_lower(v, 23 + n)

            for n in range(2):
                o = aux_bank().rearrange("p (m t) -> p m t", m=2)
                L(CP(sb_up[:, 2 * n:2 * n + 2, :], o))
                sig(TV(hT_low[:, 2 * n:2 * n + 2, :], o, sb_up[:, 2 * n:2 * n + 2, :], ALU.subtract), "sb_oT")
                sig(V.memset(sm("ang"), 0.0), "aux_free")
            sig(V.memset(sm("ang"), 0.0), "gain_free")
            merged_low = (cv_low, hT_low[:, 4:8, :])

            def merged_half(n):
                c = slice(1024 * n, 1024 * (n + 1))
                sig(TV(g[:, c], g[:, c], g[:, 2048 + 1024 * n:3072 + 1024 * n], ALU.add), "merged2")
                v.wait_ge(S("merged_upper"), n + 1)
                sig(TV(merged_low[n], g[:, c].rearrange("p (k t) -> p k t", k=4), hT_up[:, 4 * n:4 * n + 4, :],
                       ALU.subtract), "merged_lower")

            for n in range(3):
                gated(n)
            merged_half(0)
            split_lower(v, 25)
            sig(TV(g[:, 3072:4096], g[:, 3072:4096], begin(R2 + 13).rearrange(flat), ALU.mult), "big_free_V")
            merged_half(1)
            L(V.memset(rt, 0.0))
            L(V.memset(SL, 512.0))
            L(V.memset(GL, NEG))
            split_lower(v, 26)
            split_lower(v, 27)
            for j in range(2):
                c = slice(512 * j, 512 * (j + 1))
                o = begin(R2 + 14 + j)
                sig(TV(x[:, :, c], x[:, :, c], o, ALU.add), "big_free_V")
                sig(V.memset(sm("ang"), 0.0), "x_ready")
            rms("n4", 12)
            v.wait_ge(S("ffn_gain"), 16)
            gained("n4", at(A2MAP, "gain"))
            hT_copy_dve("n4")
            v.wait_ge(S("logits"), 2)
            L(TV(LG[:, :, :], logits[:, :, 0:36], bc_mid(sm("b_r2"), TT), ALU.add))
            L(CP(GL[:, :, 0:4], LG[:, :, 0:4]))
            for i in range(TT):
                last = V.max(GV8[:, i, :], GL[:, i, :])
            L(last)
            for i in range(TT):
                TS(GEX[:, i, 0:4], GL[:, i, 0:4], GV8[:, i, 0:1], None, ALU.subtract)
                last = V.max_index(idx[:, i, :], GV8[:, i, :], GL[:, i, :])
            L(last)
            L(CP(GID[:, :, :], idx[:, :, :]))
            L(TV(OH[:, :, :], bc_mid(C("iota")[:, 0:4], TT), bc_last(GID[:, :, 0], 4), ALU.is_equal))
            for i in range(TT):
                last = TV(EQ[:, 32 * i:32 * i + 32].rearrange("p (g e) -> p g e", g=4),
                          LG[:, i, 4:36].rearrange("p (g e) -> p g e", g=4), bc_last(OH[:, i, :], 8), ALU.mult)
            L(last)
            L(V.reduce_sum(EIG[:, :, :], EQ[:, 0:64].rearrange("p (t g e) -> p t e g", t=TT, g=4), axis=AX))
            for i in range(TT):
                last = V.max(V8[:, i, :], EIG[:, i, :])
            L(last)
            for i in range(TT):
                sig(TS(EX[:, i, :], V8[:, i, :], V8[:, i, 0:1], None, ALU.subtract), "r2_arg")
            for i in range(TT):
                last = V.max_index(idx2[:, i, :], V8[:, i, :], EIG[:, i, :])
            L(last)
            L(CP(IDF[:, :, :], idx2[:, :, :]))

            def to_all(dst, src):
                for i in range(TT):
                    last = TV(dst[:, i, 0:NE].rearrange("p (g e) -> p g e", g=4), bc_mid(src[:, i, :], 4),
                              bc_last(OH[:, i, :], 8), ALU.mult)
                return last

            def r2_weights():
                sig(to_all(M, M8), "mask")
                v.wait_ge(S("r2_exp"), 2 * TT)
                L(TV(ESUM, ESUM, GSUM, ALU.mult))
                L(V.reciprocal(ESUM, ESUM))
                for i in range(TT):
                    last = TS(EX[:, i, 0:2], EX[:, i, 0:2], ESUM[:, i:i + 1], None, ALU.mult)
                L(last)

            one_hots(2, 8, M8[:, :, :], W8[:, :, :], r2_weights)
            L(to_all(G, W8))
            slot_numbers(2)
            iota2 = C("iota")[:, 0:CAP2]
            moe2_select("m2", 0, iota2)
            largest_count(1, "m2")
            sig(V.memset(acc, 0.0), "m2_acc")
            with v.Fori(0, NE // 4) as q:
                moe2_dve(v, "m2", q, q, q, iota2)
            v.wait_ge(S("m2_acc"), NE // 4 + 1)
            more = v.value_load(flag[0:1, 1:2], min_val=0, max_val=SEQ)
            with v.If(more > CAP2):
                with v.Fori(0, EXTRA2) as p:
                    iop = C("iota")[:, bass.ds(CAP2 * p + CAP2, CAP2)]
                    moe2_select("m2", 0, iop)
                    with v.Fori(0, NE // 4) as q:
                        moe2_dve(v, "m2", (NE // 4) * (p + 1) + q, q, (NE // 4 + 1) * (p + 1) + q, iop)
                v.wait_ge(S("m2_acc"), (NE // 4) * (EXTRA2 + 1) + 1)
            TV(x[:, :, :].rearrange("p t d -> p (t d)"), x[:, :, :].rearrange("p t d -> p (t d)"), acc, ALU.add)\
                .then_inc(S("result"), 1)


_INS = ["x", "c", "positions", "w_ada", "b_ada", "norm1_gain", "w_in", "lower_bound_logits", "hg_norm_gain", "w_hg_branch",
        "q_norm_gain", "k_norm_gain", "attn_sinks", "w_attn_branch", "w_out", "norm2_gain", "w_router", "b_router", "w_up",
        "b_up", "w_down", "b_down", "norm_mix_g_2", "w_in_2", "q_norm_g_2", "k_norm_g_2", "conv_w_2", "w_sb_branch_2",
        "w_conv_branch_2", "w_out_2", "norm_ffn_g_2", "w_router_group_2", "b_router_group_2", "w_router_expert_2",
        "b_router_expert_2", "w_gate_e_2", "w_up_e_2", "w_down_e_2"]


def kernel(**inputs):
    import concourse.bacc as _bacc
    from concourse.bass_utils import run_bass_kernel_spmd as _run

    nc = _bacc.Bacc("TRN2", target_bir_lowering=False, num_devices=1)
    arrays, t = {}, {}
    for name in _INS + ["consts"]:
        a = CONSTS if name == "consts" else np.ascontiguousarray(inputs[name])
        arrays[f"in_{name}"] = a
        t[name] = nc.dram_tensor(f"in_{name}", a.shape, mybir.dt.from_np(a.dtype), kind="ExternalInput").ap()
    out = nc.dram_tensor("out_0", (1, SEQ, D), F32, kind="ExternalOutput").ap()
    program(nc, t, out)
    r = _run(nc, [arrays], core_ids=[0])
    return r.results[0]["out_0"]
```
